# Optimizing a Trainium2 kernel written in Bass

```python
import jax, jax.numpy as jnp
from jax import lax
import numpy as np

D_MODEL = 1024
BATCH = 1
SEQ = 1024
DEPTH = 1
DEC_BATCH = 8
DEC_SEQ = 16
PAST_LEN = 128

CHUNK = 64
EPS = 1e-6
NEG_INF = -1e30
GDN_HEADS = 4
GDN_DK = 128
GDN_DV = 128
GDN_CONV = 4
GDN_QK = GDN_HEADS * GDN_DK
GDN_V = GDN_HEADS * GDN_DV
GDN_CONV_CH = 2 * GDN_QK + GDN_V
SWA_HEADS = 4
SWA_KV_HEADS = 2
SWA_GROUP = SWA_HEADS // SWA_KV_HEADS
SWA_HD = 64
WINDOW = 128
WIN_CHUNKS = WINDOW // CHUNK
SWA_Q = SWA_HEADS * SWA_HD
SWA_KV = SWA_KV_HEADS * SWA_HD
SC_WIDTH = 256
SC_CONV = 3
MEM_TOKENS = 256
MEM_HEADS = 4
MEM_HD = D_MODEL // MEM_HEADS
D_FF = 2816
FFN_CONV = 3
IN_SIZES = (GDN_CONV_CH, GDN_V, GDN_HEADS, GDN_HEADS, SWA_Q, SWA_KV, SWA_KV, SC_WIDTH, SC_WIDTH, SC_WIDTH)
D_IN = GDN_CONV_CH + GDN_V + 2 * GDN_HEADS + SWA_Q + 2 * SWA_KV + 3 * SC_WIDTH
MIX_WIDTH = GDN_V + SWA_Q + SC_WIDTH

kernel_name = "hymba_gdn_swa_shortconv_streaming_step"

def rmsnorm(x, g):
    xf = x.astype(jnp.float32)
    y = xf * lax.rsqrt(jnp.mean(xf * xf, axis=-1, keepdims=True) + EPS)
    return (y * g.astype(jnp.float32)).astype(x.dtype)

def l2norm(x):
    xf = x.astype(jnp.float32)
    return (xf * lax.rsqrt(jnp.sum(xf * xf, axis=-1, keepdims=True) + EPS)).astype(x.dtype)

def split_cols(a, sizes):
    out, o = [], 0
    for s in sizes:
        out.append(a[..., o:o + s])
        o += s
    return out

def causal_dwconv(x, buf, w):
    W = w.shape[0]
    T = x.shape[1]
    xp = jnp.concatenate([buf.astype(x.dtype), x], axis=1)
    y = xp[:, 0:T] * w[0]
    for i in range(1, W):
        y = y + xp[:, i:i + T] * w[i]
    return y, xp[:, T:]

def gated_delta(q, k, v, g, beta, S0):
    B, T, H, dk = q.shape
    dv = v.shape[-1]
    C = CHUNK if T % CHUNK == 0 else T
    N = T // C

    def blk(a):
        a = a.reshape((B, N, C, H) + a.shape[3:])
        return jnp.moveaxis(a, (1, 3), (0, 2))

    qf, kf, vf = (blk(a).astype(jnp.float32) for a in (q, k, v))
    gc = jnp.cumsum(blk(g).astype(jnp.float32), axis=-1)
    bt = blk(beta).astype(jnp.float32)
    idx = jnp.arange(C)
    strict = idx[:, None] > idx[None, :]
    incl = idx[:, None] >= idx[None, :]
    diff = gc[..., :, None] - gc[..., None, :]
    dec_strict = jnp.exp(jnp.where(strict, diff, NEG_INF))
    dec_incl = jnp.exp(jnp.where(incl, diff, NEG_INF))
    kk = jnp.einsum('nbhid,nbhjd->nbhij', kf, kf)
    lower = bt[..., :, None] * kk * dec_strict + jnp.eye(C, dtype=jnp.float32)
    rhs = jnp.concatenate([bt[..., None] * vf, (bt * jnp.exp(gc))[..., None] * kf], axis=-1)
    sol = lax.linalg.triangular_solve(lower, rhs, left_side=True, lower=True, unit_diagonal=True)
    u0, wk = sol[..., :dv], sol[..., dv:]
    qk = jnp.einsum('nbhid,nbhjd->nbhij', qf, kf) * dec_incl
    qg = qf * jnp.exp(gc)[..., None]
    kd = kf * jnp.exp(gc[..., -1:] - gc)[..., None]
    gl = jnp.exp(gc[..., -1])

    def step(S, xs):
        u0c, wc, qkc, qgc, kdc, glc = xs
        u = u0c - jnp.einsum('bhck,bhkv->bhcv', wc, S)
        o = jnp.einsum('bhck,bhkv->bhcv', qgc, S) + jnp.einsum('bhij,bhjv->bhiv', qkc, u)
        S = glc[..., None, None] * S + jnp.einsum('bhck,bhcv->bhkv', kdc, u)
        return S, o

    S, o = lax.scan(step, S0.astype(jnp.float32), (u0, wk, qk, qg, kd, gl))
    o = jnp.moveaxis(o, (0, 2), (1, 3)).reshape(B, T, H, dv)
    return o, S

def sink_probs(s, sinks):
    sk = sinks.astype(jnp.float32).reshape(SWA_KV_HEADS, SWA_GROUP)[:, :, None, None]
    m = jnp.maximum(jnp.max(s, axis=-1, keepdims=True), sk)
    p = jnp.exp(s - m)
    return p / (jnp.sum(p, axis=-1, keepdims=True) + jnp.exp(sk - m))

def swa_prompt(q, k, v, sinks):
    B, T = q.shape[:2]
    N = T // CHUNK
    qb = q.reshape(B, N, CHUNK, SWA_KV_HEADS, SWA_GROUP, SWA_HD)

    def band(a):
        ab = a.reshape(B, N, CHUNK, SWA_KV_HEADS, SWA_HD)
        ap = jnp.pad(ab, ((0, 0), (WIN_CHUNKS, 0), (0, 0), (0, 0), (0, 0)))
        return jnp.concatenate([ap[:, i:i + N] for i in range(WIN_CHUNKS + 1)], axis=2)

    kb, vb = band(k), band(v)
    key_chunk = jnp.arange(N)[:, None] + jnp.arange(WIN_CHUNKS + 1)[None, :] - WIN_CHUNKS
    valid = jnp.repeat(key_chunk >= 0, CHUNK, axis=1)
    s = jnp.einsum('bnqhgd,bnkhd->bnhgqk', qb, kb, preferred_element_type=jnp.float32) * (SWA_HD ** -0.5)
    s = jnp.where(valid[None, :, None, None, None, :], s, NEG_INF)
    p = sink_probs(s, sinks).astype(v.dtype)
    o = jnp.einsum('bnhgqk,bnkhd->bnqhgd', p, vb)
    return o.reshape(B, T, SWA_Q)

def swa_sample(q, k, v, k_past, v_past, sinks):
    B, T = q.shape[:2]
    qg = q.reshape(B, T, SWA_KV_HEADS, SWA_GROUP, SWA_HD)
    kk = jnp.concatenate([k_past.astype(k.dtype), k], axis=1)
    vv = jnp.concatenate([v_past.astype(v.dtype), v], axis=1)
    s = jnp.einsum('bqhgd,bkhd->bhgqk', qg, kk, preferred_element_type=jnp.float32) * (SWA_HD ** -0.5)
    p = sink_probs(s, sinks).astype(v.dtype)
    o = jnp.einsum('bhgqk,bkhd->bqhgd', p, vv)
    return o.reshape(B, T, SWA_Q)

def memory_kv(mem, lw):
    B, M, _ = mem.shape
    m = rmsnorm(mem, lw['mem_in_norm_g'])
    k = rmsnorm((m @ lw['w_mk']).reshape(B, M, MEM_HEADS, MEM_HD), lw['mem_k_norm_g'])
    v = (m @ lw['w_mv']).reshape(B, M, MEM_HEADS, MEM_HD)
    return k, v

def memory_attend(hn, mem_k, mem_v, lw):
    B, T, _ = hn.shape
    q = rmsnorm((hn @ lw['w_mq']).reshape(B, T, MEM_HEADS, MEM_HD), lw['mem_q_norm_g'])
    s = jnp.einsum('bqhd,bkhd->bhqk', q, mem_k.astype(q.dtype), preferred_element_type=jnp.float32) * (MEM_HD ** -0.5)
    p = jax.nn.softmax(s, axis=-1).astype(hn.dtype)
    o = jnp.einsum('bhqk,bkhd->bqhd', p, mem_v.astype(hn.dtype)).reshape(B, T, D_MODEL)
    return o @ lw['w_mo']

def trunk_layer(x, mem_k, mem_v, gdn_S0, gdn_buf, sc_buf, ffn_buf, swa_k_past, swa_v_past, lw):
    B, T, _ = x.shape
    xn = rmsnorm(x, lw['norm_mix_g'])
    (qkv_raw, z, a, b, sq, sk, sv, sc_b, sc_c, sc_h) = split_cols(xn @ lw['w_in'], IN_SIZES)
    qkv, gdn_buf_new = causal_dwconv(qkv_raw, gdn_buf, lw['w_gdn_conv'])
    qkv = jax.nn.silu(qkv)
    gq, gk, gv = split_cols(qkv, (GDN_QK, GDN_QK, GDN_V))
    gq = l2norm(gq.reshape(B, T, GDN_HEADS, GDN_DK)) * (GDN_DK ** -0.5)
    gk = l2norm(gk.reshape(B, T, GDN_HEADS, GDN_DK))
    gv = gv.reshape(B, T, GDN_HEADS, GDN_DV)
    log_decay = -jnp.exp(lw['gdn_a_log'].astype(jnp.float32)) * jax.nn.softplus(
        a.astype(jnp.float32) + lw['gdn_dt_bias'].astype(jnp.float32))
    beta = jax.nn.sigmoid(b.astype(jnp.float32))
    go, S = gated_delta(gq, gk, gv, log_decay, beta, gdn_S0)
    go = rmsnorm(go, lw['gdn_norm_g']) * jax.nn.silu(z.astype(jnp.float32).reshape(B, T, GDN_HEADS, GDN_DV))
    out_a = go.reshape(B, T, GDN_V).astype(x.dtype)
    sq = rmsnorm(sq.reshape(B, T, SWA_HEADS, SWA_HD), lw['swa_q_norm_g'])
    sk = rmsnorm(sk.reshape(B, T, SWA_KV_HEADS, SWA_HD), lw['swa_k_norm_g'])
    sv = sv.reshape(B, T, SWA_KV_HEADS, SWA_HD)
    if swa_k_past is None:
        out_b = swa_prompt(sq, sk, sv, lw['swa_sinks'])
    else:
        out_b = swa_sample(sq, sk, sv, swa_k_past, swa_v_past, lw['swa_sinks'])
    cu, sc_buf_new = causal_dwconv(sc_c * sc_h, sc_buf, lw['w_sc_conv'])
    out_c = sc_b * cu
    h = x + jnp.concatenate([out_a, out_b, out_c], axis=-1) @ lw['w_o']
    h = h + memory_attend(rmsnorm(h, lw['norm_mem_g']), mem_k, mem_v, lw)
    u, ffn_buf_new = causal_dwconv(rmsnorm(h, lw['norm_ffn_g']) @ lw['w_up'], ffn_buf, lw['w_ffn_conv'])
    ug, uv = split_cols(u, (D_FF, D_FF))
    h = h + (jax.nn.silu(ug) * uv) @ lw['w_down']
    return h, S.astype(x.dtype), gdn_buf_new, sc_buf_new, ffn_buf_new, sk, sv

def setup_inputs(seed: int = 0) -> dict:
    key = jax.random.key(seed)
    ks = iter(jax.random.split(key, 48))

    def nrm(shape, scale=1.0):
        return jax.random.normal(next(ks), shape, jnp.float32) * scale

    def dense(shape):
        return nrm(shape, shape[-2] ** -0.5)

    def gain(shape):
        return 1.0 + nrm(shape, 0.02)

    swa_buf = min(WINDOW, PAST_LEN)
    dt = jnp.exp(jax.random.uniform(next(ks), (DEPTH, GDN_HEADS), jnp.float32, np.log(1e-3), np.log(1e-1)))
    inputs = {
        'x_prompt': nrm((BATCH, SEQ, D_MODEL)),
        'x_sample': nrm((DEC_BATCH, DEC_SEQ, D_MODEL)),
        'mem_prompt': nrm((BATCH, MEM_TOKENS, D_MODEL)),
        'state_gdn': nrm((DEPTH, DEC_BATCH, GDN_HEADS, GDN_DK, GDN_DV), 0.1),
        'state_gdn_conv': nrm((DEPTH, DEC_BATCH, GDN_CONV - 1, GDN_CONV_CH)),
        'cache_swa_k': nrm((DEPTH, DEC_BATCH, swa_buf, SWA_KV_HEADS, SWA_HD)),
        'cache_swa_v': nrm((DEPTH, DEC_BATCH, swa_buf, SWA_KV_HEADS, SWA_HD)),
        'state_sc_conv': nrm((DEPTH, DEC_BATCH, SC_CONV - 1, SC_WIDTH)),
        'cache_mem_k': nrm((DEPTH, DEC_BATCH, MEM_TOKENS, MEM_HEADS, MEM_HD)),
        'cache_mem_v': nrm((DEPTH, DEC_BATCH, MEM_TOKENS, MEM_HEADS, MEM_HD)),
        'state_ffn_conv': nrm((DEPTH, DEC_BATCH, FFN_CONV - 1, 2 * D_FF)),
        'norm_mix_g': gain((DEPTH, D_MODEL)),
        'w_in': dense((DEPTH, D_MODEL, D_IN)),
        'w_gdn_conv': nrm((DEPTH, GDN_CONV, GDN_CONV_CH), GDN_CONV ** -0.5),
        'gdn_a_log': jnp.log(jax.random.uniform(next(ks), (DEPTH, GDN_HEADS), jnp.float32, 1.0, 16.0)),
        'gdn_dt_bias': dt + jnp.log(-jnp.expm1(-dt)),
        'gdn_norm_g': gain((DEPTH, GDN_DV)),
        'swa_q_norm_g': gain((DEPTH, SWA_HD)),
        'swa_k_norm_g': gain((DEPTH, SWA_HD)),
        'swa_sinks': nrm((DEPTH, SWA_HEADS), 0.5),
        'w_sc_conv': nrm((DEPTH, SC_CONV, SC_WIDTH), SC_CONV ** -0.5),
        'w_o': dense((DEPTH, MIX_WIDTH, D_MODEL)),
        'norm_mem_g': gain((DEPTH, D_MODEL)),
        'mem_in_norm_g': gain((DEPTH, D_MODEL)),
        'w_mq': dense((DEPTH, D_MODEL, D_MODEL)),
        'w_mk': dense((DEPTH, D_MODEL, D_MODEL)),
        'w_mv': dense((DEPTH, D_MODEL, D_MODEL)),
        'mem_q_norm_g': gain((DEPTH, MEM_HD)),
        'mem_k_norm_g': gain((DEPTH, MEM_HD)),
        'w_mo': dense((DEPTH, D_MODEL, D_MODEL)),
        'norm_ffn_g': gain((DEPTH, D_MODEL)),
        'w_up': dense((DEPTH, D_MODEL, 2 * D_FF)),
        'w_ffn_conv': nrm((DEPTH, FFN_CONV, 2 * D_FF), FFN_CONV ** -0.5),
        'w_down': dense((DEPTH, D_FF, D_MODEL)),
    }
    return inputs

def reference(x_prompt, x_sample, mem_prompt,
              state_gdn, state_gdn_conv, cache_swa_k, cache_swa_v, state_sc_conv,
              cache_mem_k, cache_mem_v, state_ffn_conv,
              norm_mix_g, w_in, w_gdn_conv, gdn_a_log, gdn_dt_bias, gdn_norm_g,
              swa_q_norm_g, swa_k_norm_g, swa_sinks, w_sc_conv, w_o,
              norm_mem_g, mem_in_norm_g, w_mq, w_mk, w_mv, mem_q_norm_g, mem_k_norm_g, w_mo,
              norm_ffn_g, w_up, w_ffn_conv, w_down):
    hp, hs = x_prompt, x_sample
    Bp, Tp, _ = x_prompt.shape
    keep = min(WINDOW, Tp)
    p_S, p_gb, p_sk, p_sv, p_sb, p_mk, p_mv, p_fb = [], [], [], [], [], [], [], []
    s_S, s_gb, s_sk, s_sv, s_sb, s_fb = [], [], [], [], [], []
    for l in range(DEPTH):
        lw = {
            'norm_mix_g': norm_mix_g[l], 'w_in': w_in[l], 'w_gdn_conv': w_gdn_conv[l],
            'gdn_a_log': gdn_a_log[l], 'gdn_dt_bias': gdn_dt_bias[l], 'gdn_norm_g': gdn_norm_g[l],
            'swa_q_norm_g': swa_q_norm_g[l], 'swa_k_norm_g': swa_k_norm_g[l], 'swa_sinks': swa_sinks[l],
            'w_sc_conv': w_sc_conv[l], 'w_o': w_o[l], 'norm_mem_g': norm_mem_g[l],
            'mem_in_norm_g': mem_in_norm_g[l], 'w_mq': w_mq[l], 'w_mk': w_mk[l], 'w_mv': w_mv[l],
            'mem_q_norm_g': mem_q_norm_g[l], 'mem_k_norm_g': mem_k_norm_g[l], 'w_mo': w_mo[l],
            'norm_ffn_g': norm_ffn_g[l], 'w_up': w_up[l], 'w_ffn_conv': w_ffn_conv[l], 'w_down': w_down[l],
        }
        mk, mv = memory_kv(mem_prompt, lw)
        dt_p = hp.dtype
        hp, S, gb, sb, fb, sk, sv = trunk_layer(
            hp, mk, mv,
            jnp.zeros((Bp, GDN_HEADS, GDN_DK, GDN_DV), dt_p),
            jnp.zeros((Bp, GDN_CONV - 1, GDN_CONV_CH), dt_p),
            jnp.zeros((Bp, SC_CONV - 1, SC_WIDTH), dt_p),
            jnp.zeros((Bp, FFN_CONV - 1, 2 * D_FF), dt_p),
            None, None, lw)
        p_S.append(S); p_gb.append(gb); p_sb.append(sb); p_fb.append(fb)
        p_sk.append(sk[:, Tp - keep:]); p_sv.append(sv[:, Tp - keep:])
        p_mk.append(mk); p_mv.append(mv)
        hs, S, gb, sb, fb, sk, sv = trunk_layer(
            hs, cache_mem_k[l], cache_mem_v[l], state_gdn[l], state_gdn_conv[l],
            state_sc_conv[l], state_ffn_conv[l], cache_swa_k[l], cache_swa_v[l], lw)
        s_S.append(S); s_gb.append(gb); s_sb.append(sb); s_fb.append(fb)
        s_sk.append(sk); s_sv.append(sv)
    y_prompt, y_sample = hp, hs
    p_state_gdn = jnp.stack(p_S)
    p_state_gdn_conv = jnp.stack(p_gb)
    p_cache_swa_k = jnp.stack(p_sk)
    p_cache_swa_v = jnp.stack(p_sv)
    p_state_sc_conv = jnp.stack(p_sb)
    p_cache_mem_k = jnp.stack(p_mk)
    p_cache_mem_v = jnp.stack(p_mv)
    p_state_ffn_conv = jnp.stack(p_fb)
    s_state_gdn = jnp.stack(s_S)
    s_state_gdn_conv = jnp.stack(s_gb)
    s_swa_k_new = jnp.stack(s_sk)
    s_swa_v_new = jnp.stack(s_sv)
    s_state_sc_conv = jnp.stack(s_sb)
    s_state_ffn_conv = jnp.stack(s_fb)
    return (y_prompt, y_sample,
            p_state_gdn, p_state_gdn_conv, p_cache_swa_k, p_cache_swa_v, p_state_sc_conv,
            p_cache_mem_k, p_cache_mem_v, p_state_ffn_conv,
            s_state_gdn, s_state_gdn_conv, s_swa_k_new, s_swa_v_new, s_state_sc_conv, s_state_ffn_conv)


_drawn_inputs = setup_inputs


def setup_inputs(seed=0):
    import zlib

    import numpy as np

    out = dict(_drawn_inputs(seed))
    spreads = {}
    factors = {'gdn_norm_g': 5.068,
     'swa_q_norm_g': 8.0,
     'swa_k_norm_g': 2.791,
     'swa_sinks': 64.0,
     'norm_mem_g': 8.0,
     'mem_in_norm_g': 2.904,
     'mem_q_norm_g': 8.0,
     'mem_k_norm_g': 2.764,
     'norm_ffn_g': 2.805}
    for name, (base, spread) in spreads.items():
        noise = np.random.default_rng([zlib.crc32(name.encode()), seed]).standard_normal(out[name].shape)
        drawn = base * np.exp(spread * noise) if base else spread * noise
        out[name] = __import__('jax').numpy.asarray(drawn.astype(out[name].dtype))
    for name, factor in factors.items():
        out[name] = (out[name] * factor).astype(out[name].dtype)
    return out
```

```python
from contextlib import ExitStack

import concourse.bass as bass
from concourse import mybir

F32 = mybir.dt.float32
F32R = mybir.dt.float32r
ALU = mybir.AluOpType
ACT = mybir.ActivationFunctionType
AX = mybir.AxisListType

P = 128
D = 1024
KD = D // P
TP = 1024
NB, TB = 8, 16
TS = NB * TB
T = TP + TS
NT = T // P
PT = TP // P
NP = 3
TC = T // NP
PP = TP - 2 * TC
HEADS = 4
HW = HEADS * P
CONV_CH = 1536
WIDTH = 3336
EPS = 1e-6
NEG = -1e30
FF = 2816
NF = FF // P
MEM = 256
SWA_HD = 64

V_MIX, V_MEM, V_MIN, V_FFN, V_MQ, V_GN, V_SQ, V_SK, V_GC, V_SC, V_FC = 0, 8, 16, 24, 32, 34, 35, 36, 37, 85, 91
V_ALL = V_FC + 3 * 2 * NF


def xp_len(w):
    return TP + w - 1 + NB * (TB + w - 1)


def xp_sample(buf, w, lo, n):
    s = TB + w - 1
    a = TP + w - 1
    return buf[:, a:a + NB * s].rearrange("p (b s) -> p b s", s=s)[:, :, lo:lo + n]


def seqs(ap):
    return ap.rearrange("p (b s) -> p b s", s=TB)


def heads(ap):
    return ap.rearrange("p (h c) -> p h c", h=HEADS)


def over(ap, n):
    return ap.unsqueeze(2).to_broadcast([ap.shape[0], ap.shape[1], n])


def each(ap, n):
    return ap.unsqueeze(1).to_broadcast([ap.shape[0], n, ap.shape[1]])


class Ctx:

    def __init__(self, nc, stack):
        self.nc, self.stack = nc, stack

    def sb(self, name, shape, dt=F32):
        return self.stack.enter_context(self.nc.sbuf_tensor(name, shape, dt))

    def psum(self, name, shape, dt=F32):
        return self.stack.enter_context(self.nc.psum_tensor(name, shape, dt))

    def sem(self, name):
        return self.stack.enter_context(self.nc.semaphore(name))

    def phase(self):
        return Phase(self.nc)


class Phase(Ctx):

    def __init__(self, nc):
        super().__init__(nc, ExitStack())
        self.open = None
        self.sems = []

    def sem(self, name):
        s = super().sem(name)
        self.sems.append(s)
        return s

    def __enter__(self):
        self.stack.__enter__()
        return self

    def end_block(self):
        if self.open is not None:
            self.open.__exit__(None, None, None)
            self.open = None

    def block(self):
        self.end_block()
        self.open = self.nc.Block()
        return self.open.__enter__()

    def __exit__(self, *a):
        if a[0] is None:
            self.end_block()
            for s in self.sems:
                self.nc.sync.sem_clear(s)
        return self.stack.__exit__(*a)



def setup(nc, C, A):
    with C.phase() as ph:
        rows_a = ph.sb("vec_rows_a", [91, P])
        rows_b = ph.sb("vec_rows_b", [88, P])
        rows_c = ph.sb("vec_rows_c", [44, P])
        blocks = ph.sb("same_block", [P, 7, P])
        tp = ph.psum("vec_cols", [P, 512])
        loaded, masks, turned, copied = (ph.sem(n) for n in ("s0_loaded", "s0_masks", "s0_turned", "s0_copied"))
        pool_step = ph.sem("s0_pool_step")
        ident, ones = C.ident, C.ones
        block = ph.block()

        @block.sync
        def _(sp):
            n = 0
            for col, name, k in ((V_MIX, "norm_mix_g", 8), (V_MEM, "norm_mem_g", 8), (V_MIN, "mem_in_norm_g", 8),
                                 (V_FFN, "norm_ffn_g", 8), (V_MQ, "mem_q_norm_g", 2), (V_GN, "gdn_norm_g", 1)):
                sp.dma_start(rows_a[col:col + k, :], A[name][0].rearrange("(k p) -> k p", p=P)).then_inc(loaded, 16)
                n += 1
            for col, name in ((V_SQ, "swa_q_norm_g"), (V_SK, "swa_k_norm_g")):
                for half in range(2):
                    sp.dma_start(rows_a[col:col + 1, half * 64:half * 64 + 64], A[name]).then_inc(loaded, 16)
                    n += 1
            for i in range(4):
                sp.dma_start(rows_a[V_GC + 12 * i:V_GC + 12 * i + 12, :],
                             A["w_gdn_conv"][0, i].rearrange("(k p) -> k p", p=P)).then_inc(loaded, 16)
                n += 1
            for i in range(3):
                sp.dma_start(rows_a[V_SC + 2 * i:V_SC + 2 * i + 2, :],
                             A["w_sc_conv"][0, i].rearrange("(k p) -> k p", p=P)).then_inc(loaded, 16)
                to = rows_b[44 * i:44 * i + 44, :] if i < 2 else rows_c[:, :]
                sp.dma_start(to, A["w_ffn_conv"][0, i].rearrange("(k p) -> k p", p=P)).then_inc(loaded, 16)
                n += 2
            sp.dma_start(C.k_gain[:], A["mem_k_norm_g"].to_broadcast([P, 256])).then_inc(loaded, 16)
            sp.dma_start(C.a_log[:], A["gdn_a_log"].to_broadcast([P, 4])).then_inc(loaded, 16)
            sp.dma_start(C.dt_bias[:], A["gdn_dt_bias"].to_broadcast([P, 4])).then_inc(loaded, 16)
            sp.dma_start(C.sinks[:], A["swa_sinks"].to_broadcast([P, 4])).then_inc(loaded, 16)
            n += 4
            sp.wait_ge(loaded, 16 * n)
            sp.sem_inc(masks, 1)

        @block.gpsimd
        def _(pool):
            steps = 0

            def step(ins):
                nonlocal steps
                ins.then_inc(pool_step, 1)
                steps += 1
                pool.wait_ge(pool_step, steps)

            step(nc.gpsimd.memset(ones[:], 1.0))
            for k in range(7):
                s = 1 << k
                v = blocks[:, k, :].rearrange("p (b c) -> p b c", c=s)
                one = ones[:].rearrange("p (b c) -> p b c", c=s)
                step(nc.gpsimd.affine_select(out=v, in_=one, compare_op=ALU.is_ge, fill=0.0, base=0,
                                             pattern=[[-s, P // s], [0, s]], channel_multiplier=1))
                step(nc.gpsimd.affine_select(out=v, in_=v, compare_op=ALU.is_ge, fill=0.0, base=s - 1,
                                             pattern=[[s, P // s], [0, s]], channel_multiplier=-1))
            step(nc.gpsimd.tensor_copy(ident[:], blocks[:, 0, :]))
            step(nc.gpsimd.tensor_copy(C.pair_ones[:], blocks[:, 6, :]))
            for kind, k in ((0, 6), (1, 4)):
                step(nc.gpsimd.affine_select(out=C.upto[:, kind, :], in_=blocks[:, k, :], compare_op=ALU.is_ge,
                                             fill=0.0, base=0, pattern=[[1, P]], channel_multiplier=-1))
                step(nc.gpsimd.affine_select(out=C.after[:, kind, :], in_=blocks[:, k, :], compare_op=ALU.is_gt,
                                             fill=0.0, base=0, pattern=[[-1, P]], channel_multiplier=1))
            for k in range(6):
                step(nc.gpsimd.tensor_tensor(C.level[:, k, :], blocks[:, k + 1, :], blocks[:, k, :], ALU.subtract))
                step(nc.gpsimd.affine_select(out=C.level[:, k, :], in_=C.level[:, k, :], compare_op=ALU.is_gt,
                                             fill=0.0, base=0, pattern=[[-1, P]], channel_multiplier=1))
            step(nc.gpsimd.memset(C.hide[:], 0.0))
            for kind in range(2):
                step(nc.gpsimd.memset(C.hide[0:64, kind, 192:256], NEG))
                step(nc.gpsimd.memset(C.hide[64:128, kind, 0:64], NEG))
            step(nc.gpsimd.memset(C.hide[:, 1, 0:128], NEG))
            step(nc.gpsimd.tensor_scalar(C.hide[:, 2, 128:256], blocks[:, 4, :], 1.0, -NEG, ALU.subtract, ALU.mult))
            step(nc.gpsimd.tensor_copy(C.seq_mask[:], blocks[:, 4, :].rearrange("p (b s) -> p b s", s=TB)[:, :, 0]))
            step(nc.gpsimd.memset(C.eps[:], EPS))
            pool.sem_inc(masks, 1)

        @block.tensor
        def _(pe):
            pe.wait_ge(masks, 2)
            nc.tensor.transpose(tp[:, 0:91], rows_a[:], ident[0:91, 0:91])
            nc.tensor.transpose(tp[:, 91:179], rows_b[:], ident[0:88, 0:88])
            nc.tensor.transpose(tp[:, 179:223], rows_c[:], ident[0:44, 0:44]).then_inc(turned, 1)

        @block.vector
        def _(dve):
            dve.wait_ge(turned, 1)
            nc.vector.tensor_copy(C.vec[:], tp[:, 0:V_ALL]).then_inc(copied, 1)
            dve.wait_ge(copied, 1)



def norm_turn(nc, C, tag, src, loads, n_tiles, gain_col, out, out_lo=None):
    with C.phase() as ph:
        group = 3 if n_tiles % 3 == 0 else n_tiles
        ng = n_tiles // group
        W = group * P
        squares = ph.sb(f"{tag}_squares", [P, D])
        sums = ph.sb(f"{tag}_sums", [P, n_tiles])
        root = ph.sb(f"{tag}_root", [P, n_tiles])
        inv = ph.sb(f"{tag}_inv", [P, n_tiles])
        xn = ph.sb(f"{tag}_xn", [P, 2, group, D])
        banks = ph.psum(f"{tag}_banks", [P, 4, 512])
        landed = [ph.sem(f"{tag}_landed{t}") for t in range(len(loads))]
        summed, rooted, inverted, scaled, turned, high, low = (
            ph.sem(f"{tag}_{n}") for n in ("summed", "rooted", "inverted", "scaled", "turned", "high", "low"))
        block = ph.block()

        @block.sync
        def _(sp):
            for t, dram in enumerate(loads):
                sp.dma_start(src[:, t, :], dram).then_inc(landed[t], 16)

        @block.scalar
        def _(act):
            for t in range(n_tiles):
                if loads:
                    act.wait_ge(landed[t], 16)
                if t:
                    act.wait_ge(summed, t)
                nc.scalar.activation(squares[:], src[:, t, :], ACT.Square, accum_out=sums[:, t:t + 1]).then_inc(summed, 1)
            act.wait_ge(summed, n_tiles)
            nc.scalar.activation(root[:], sums[:], ACT.Sqrt, scale=1.0 / D, bias=C.eps[:, 0:1]).then_inc(rooted, 1)
            for i in range(ng * KD):
                g, k = divmod(i, KD)
                act.wait_ge(turned, i + 1)
                nc.scalar.activation(out[:, k, g * W:g * W + W], banks[:, i % 4, 0:W], ACT.Copy,
                                     scale=C.vec[:, gain_col + k:gain_col + k + 1]).then_inc(high, 1)

        @block.vector
        def _(dve):
            dve.wait_ge(rooted, 1)
            nc.vector.reciprocal(inv[:], root[:]).then_inc(inverted, 1)
            dve.wait_ge(inverted, 1)

            def scale(g):
                if g >= 2:
                    dve.wait_ge(turned, KD * (g - 1))
                for j in range(group):
                    t = g * group + j
                    nc.vector.tensor_scalar(xn[:, g % 2, j, :], src[:, t, :], inv[:, t:t + 1], None,
                                            ALU.mult).then_inc(scaled, 1)
            scale(0)
            for g in range(ng):
                if g + 1 < ng:
                    scale(g + 1)
                if out_lo is not None:
                    for k in range(KD):
                        i = g * KD + k
                        dve.wait_ge(high, i + 1)
                        nc.vector.scalar_tensor_tensor(
                            out_lo[:, k, g * W:g * W + W], banks[:, i % 4, 0:W], C.vec[:, gain_col + k:gain_col + k + 1],
                            out[:, k, g * W:g * W + W].bitcast(F32), ALU.mult, ALU.subtract).then_inc(low, 1)

        @block.tensor
        def _(pe):
            for i in range(ng * KD):
                g, k = divmod(i, KD)
                pe.wait_ge(scaled, group * (g + 1))
                if i >= 4:
                    pe.wait_ge(high if out_lo is None else low, i - 3)
                for j in range(group):
                    ins = nc.tensor.transpose(banks[:, i % 4, j * P:j * P + P], xn[:, g % 2, j, k * P:k * P + P],
                                              C.ident[:])
                ins.then_inc(turned, 1)



def column_tiles():
    z0 = CONV_CH
    ab0 = z0 + 512
    sq0 = ab0 + 8
    sk0, sv0 = sq0 + 256, sq0 + 384
    b0 = sv0 + 128
    c0, h0 = b0 + 256, b0 + 512
    tiles = []
    for i in range(2):
        tiles += [("sc_c", i, [(c0 + P * i, P)]), ("sc_h", i, [(h0 + P * i, P)]), ("sc_b", i, [(b0 + P * i, P)])]
    tiles += [("swa_q", i, [(sq0 + 64 * i, 64), (sq0 + 128 + 64 * i, 64)]) for i in range(2)]
    tiles += [("swa_k", 0, [(sk0, P)]), ("swa_v", 0, [(sv0, P)]), ("gate", 0, [(ab0, 8)])]
    for h in range(HEADS):
        tiles += [("conv", HEADS * j + h, [(512 * j + P * h, P)]) for j in range(3)] + [("z", h, [(z0 + P * h, P)])]
    return tiles


def in_projection(nc, C, A, O, M):
    tiles = column_tiles()
    n_tiles = len(tiles)
    RING = 3
    at = {(kind, i): n for n, (kind, i, _) in enumerate(tiles)}
    by_act = [kind not in ("sc_h", "sc_b") for kind, _, _ in tiles]
    act_count = [sum(by_act[:n + 1]) for n in range(n_tiles)]
    dve_count = [n + 1 - act_count[n] for n in range(n_tiles)]
    convs = [(n, i) for n, (kind, i, _) in enumerate(tiles) if kind == "conv"]
    L4, L3 = xp_len(4), xp_len(3)
    with C.phase() as ph:
        w = ph.sb("w_in_ring", [P, RING, KD, P])
        xp = ph.sb("conv_in", [P, 2, L4])
        y = ph.sb("conv_out", [P, L4])
        sc_c = ph.sb("sc_c", [P, T])
        old_rows = ph.sb("gdn_old_rows", [24, CONV_CH])
        old_sc_rows = ph.sb("sc_old_rows", [16, 256])
        old = ph.sb("gdn_old", [P, 12 * 24 + 2 * 16])
        tail = ph.sb("tail", [P, 2, 27])
        new_s = ph.sb("new_sample_rows", [24, 2, P])
        new_p = ph.sb("new_prompt_rows", [3, 2, P])
        banks = ph.psum("proj_banks", [P, 2 * NP, 512])
        state_in = ph.psum("state_in", [P, 512])
        state_out = ph.psum("state_out", [P, 512])
        w_landed = [ph.sem(f"c_w_landed{r}") for r in range(RING)]
        stored = C.conv_stored
        (rows_landed, projected, act_freed, dve_freed, old_turned, old_copied, padded, conv_step, conv_done,
         silu_done, state_turned, state_saved, sc_done, gathered) = (
            ph.sem(f"c_{n}") for n in (
                "rows_landed", "projected", "act_freed", "dve_freed", "old_turned", "old_copied", "padded",
                "conv_step", "conv_done", "silu_done", "state_turned", "state_saved", "sc_done", "gathered"))
        xT = M["xT"]
        q, mixT = M["qkv"], C.mixT
        dest = {"swa_q": M["swa_q"], "swa_k": M["swa_k"], "swa_v": M["swa_v"]}
        padded_of = {("sc", 0): 0, ("sc", 1): 1, **{("conv", i): 2 + m for m, (_, i) in enumerate(convs)}}
        block = ph.block()

        @block.sync
        def _(sp):
            sp.dma_start(old_rows[:], A["state_gdn_conv"][0].rearrange("b i c -> (b i) c")).then_inc(rows_landed, 16)
            sp.dma_start(old_sc_rows[:], A["state_sc_conv"][0].rearrange("b i c -> (b i) c")).then_inc(rows_landed, 16)
            for n, (kind, i, cols) in enumerate(tiles):
                if n >= RING:
                    sp.wait_ge(projected, NP * (n - RING + 1))
                o = 0
                for c0, width in cols:
                    sp.dma_start(w[:, n % RING, :, o:o + width],
                                 A["w_in"][0].rearrange("(k p) c -> p k c", p=P)[:, :, c0:c0 + width]
                                 ).then_inc(w_landed[n % RING], 16)
                    o += width

        w_count = [16 * sum(len(tiles[m][2]) for m in range(n % RING, n + 1, RING)) for n in range(n_tiles)]

        @block.tensor
        def _(pe):
            pe.wait_ge(rows_landed, 32)
            for i in range(12):
                nc.tensor.transpose(state_in[:, 24 * i:24 * i + 24], old_rows[:, P * i:P * i + P], C.ident[0:24, 0:24])
            for i in range(2):
                ins = nc.tensor.transpose(state_in[:, 288 + 16 * i:304 + 16 * i], old_sc_rows[:, P * i:P * i + P],
                                          C.ident[0:16, 0:16])
            ins.then_inc(old_turned, 1)

            def turn_state(m):
                W = 3 if m < 2 else 4
                pe.wait_ge(gathered, m + 1)
                if m:
                    pe.wait_ge(state_saved, m)
                nc.tensor.transpose(state_out[0:W - 1, 0:P], tail[:, m % 2, 24:24 + W - 1], C.ident[:])
                nc.tensor.transpose(state_out[0:NB * (W - 1), P:2 * P], tail[:, m % 2, 0:NB * (W - 1)],
                                    C.ident[:]).then_inc(state_turned, 1)

            for n, (kind, i, cols) in enumerate(tiles):
                rows = sum(c for _, c in cols)
                pe.wait_ge(w_landed[n % RING], w_count[n])
                if n >= 2:
                    if by_act[n - 2]:
                        pe.wait_ge(act_freed, act_count[n - 2])
                    else:
                        pe.wait_ge(dve_freed, dve_count[n - 2])
                for piece in range(NP):
                    for k in range(KD):
                        ins = nc.tensor.matmul(banks[0:rows, (n % 2) * NP + piece, 0:TC], w[:, n % RING, k, 0:rows],
                                               xT[:, k, piece * TC:piece * TC + TC], start=(k == 0), stop=(k == KD - 1))
                    ins.then_inc(projected, 1)
                if n >= 1 and tiles[n - 1][0] == "sc_h":
                    turn_state(tiles[n - 1][1])
                if n >= 1 and tiles[n - 1][0] == "conv":
                    turn_state(padded_of["conv", tiles[n - 1][1]])

        def pieces(n):
            return [((n % 2) * NP + p, p * TC, TC if p < 2 else PP) for p in range(NP)]

        @block.scalar
        def _(act):
            def silu(m):
                n, i = convs[m]
                act.wait_ge(conv_done, m + 1)
                nc.scalar.activation(q[:, i, 0:TP], y[:, 0:TP], ACT.Silu)
                nc.scalar.activation(seqs(q[:, i, TP:T]), xp_sample(y, 4, 0, TB), ACT.Silu).then_inc(silu_done, 1)

            m = 0
            for n, (kind, i, cols) in enumerate(tiles):
                rows = sum(c for _, c in cols)
                if by_act[n]:
                    for p, (bank, c0, cn) in enumerate(pieces(n)):
                        act.wait_ge(projected, NP * n + p + 1)
                        if kind == "conv":
                            pad = padded_of[kind, i]
                            if p == 0:
                                act.wait_ge(padded, pad + 1)
                            ins = nc.scalar.activation(xp[:, pad % 2, 3 + c0:3 + c0 + cn], banks[:, bank, 0:cn], ACT.Copy)
                            if p == 2:
                                ins = nc.scalar.activation(xp_sample(xp[:, pad % 2, :], 4, 3, TB),
                                                           seqs(banks[:, bank, PP:TC]), ACT.Copy)
                        elif kind == "z":
                            ins = nc.scalar.activation(mixT[:, i, p * TC:p * TC + TC], banks[:, bank, 0:TC], ACT.Silu)
                        else:
                            to = {"sc_c": sc_c[:], "gate": M["gate"][:]}.get(kind)
                            to = dest[kind][:, i, :] if to is None else to
                            if kind == "sc_c" and i:
                                act.wait_ge(dve_freed, dve_count[at["sc_h", 0]])
                            ins = nc.scalar.activation(to[0:rows, p * TC:p * TC + TC], banks[0:rows, bank, 0:TC], ACT.Copy)
                    ins.then_inc(act_freed, 1)
                if n >= 1 and tiles[n - 1][0] == "conv":
                    silu(m)
                    m += 1

        @block.gpsimd
        def _(pool):
            def store_state(m):
                W = 3 if m < 2 else 4
                i = m if m < 2 else convs[m - 2][1]
                to_p, to_s = (O["p_sc_conv"], O["s_sc_conv"]) if m < 2 else (O["p_gdn_conv"], O["s_gdn_conv"])
                pool.wait_ge(state_saved, m + 1)
                pool.dma_start(to_p[0, 0][:, P * i:P * i + P], new_p[0:W - 1, m % 2, :]).then_inc(stored[m % 2], 16)
                pool.dma_start(to_s[0].rearrange("b i c -> (b i) c")[:, P * i:P * i + P],
                               new_s[0:NB * (W - 1), m % 2, :]).then_inc(stored[m % 2], 16)

            for pad in range(14):
                W = 3 if pad < 2 else 4
                buf = xp[:, pad % 2, :]
                if pad == 0:
                    pool.wait_ge(old_copied, 1)
                if pad >= 2:
                    if pad < 4:
                        pool.wait_ge(sc_done, pad - 1)
                    else:
                        pool.wait_ge(conv_done, pad - 3)
                if pad < 2:
                    was = old[:, 288 + 16 * pad:304 + 16 * pad]
                else:
                    i = convs[pad - 2][1]
                    was = old[:, 24 * i:24 * i + 24]
                nc.gpsimd.memset(buf[:, 0:W - 1], 0.0)
                nc.gpsimd.tensor_copy(xp_sample(buf, W, 0, W - 1), was.rearrange("p (b i) -> p b i", b=NB)
                                      ).then_inc(padded, 1)
                if pad >= 2:
                    store_state(pad - 2)
            store_state(12)
            store_state(13)
            for r in range(2):
                pool.wait_ge(stored[r], 32 * 7)

        @block.vector
        def _(dve):
            steps = 0

            def taps(W, pad, vec0, stride):
                nonlocal steps
                L = xp_len(W) - (W - 1)
                buf = xp[:, pad % 2, :]
                for j in range(W):
                    wt = C.vec[:, vec0 + stride * j:vec0 + stride * j + 1]
                    if j == 0:
                        ins = nc.vector.tensor_scalar(y[:, 0:L], buf[:, 0:L], wt, None, ALU.mult)
                    else:
                        dve.wait_ge(conv_step, steps)
                        ins = nc.vector.scalar_tensor_tensor(y[:, 0:L], buf[:, j:j + L], wt, y[:, 0:L],
                                                             ALU.mult, ALU.add)
                    if j < W - 1:
                        ins.then_inc(conv_step, 1)
                        steps += 1
                return ins

            def gather_tail(m):
                W = 3 if m < 2 else 4
                if m >= 2:
                    dve.wait_ge(state_turned, m - 1)
                nc.vector.tensor_copy(tail[:, m % 2, 0:NB * (W - 1)].rearrange("p (b i) -> p b i", b=NB),
                                      xp_sample(xp[:, m % 2, :], W, TB, W - 1))
                nc.vector.tensor_copy(tail[:, m % 2, 24:24 + W - 1], xp[:, m % 2, TP:TP + W - 1]).then_inc(gathered, 1)

            def save_state(m):
                W = 3 if m < 2 else 4
                dve.wait_ge(state_turned, m + 1)
                if m >= 2:
                    dve.wait_ge(stored[m % 2], 32 * (m // 2))
                nc.vector.tensor_copy(new_p[0:W - 1, m % 2, :], state_out[0:W - 1, 0:P])
                nc.vector.tensor_copy(new_s[0:NB * (W - 1), m % 2, :], state_out[0:NB * (W - 1), P:2 * P]
                                      ).then_inc(state_saved, 1)

            dve.wait_ge(old_turned, 1)
            nc.vector.tensor_copy(old[:], state_in[:, 0:320]).then_inc(old_copied, 1)
            for n, (kind, i, cols) in enumerate(tiles):
                if kind == "sc_h":
                    dve.wait_ge(act_freed, act_count[at["sc_c", i]])
                    dve.wait_ge(padded, i + 1)
                    for p, (bank, c0, cn) in enumerate(pieces(n)):
                        dve.wait_ge(projected, NP * n + p + 1)
                        nc.vector.tensor_tensor(xp[:, i, 2 + c0:2 + c0 + cn], banks[:, bank, 0:cn], sc_c[:, c0:c0 + cn],
                                                ALU.mult)
                    nc.vector.tensor_tensor(xp_sample(xp[:, i, :], 3, 2, TB), seqs(banks[:, bank, PP:TC]),
                                            seqs(sc_c[:, TP:T]), ALU.mult).then_inc(dve_freed, 1)
                    dve.wait_ge(dve_freed, dve_count[n])
                    gather_tail(i)
                    taps(3, i, V_SC + i, 2).then_inc(sc_done, 1)
                    dve.wait_ge(sc_done, i + 1)
                elif kind == "sc_b":
                    save_state(i)
                    for p, (bank, c0, cn) in enumerate(pieces(n)):
                        dve.wait_ge(projected, NP * n + p + 1)
                        nc.vector.tensor_tensor(mixT[:, 6 + i, c0:c0 + cn], banks[:, bank, 0:cn], y[:, c0:c0 + cn], ALU.mult)
                    nc.vector.tensor_tensor(seqs(mixT[:, 6 + i, TP:T]), seqs(banks[:, bank, PP:TC]),
                                            xp_sample(y, 3, 0, TB), ALU.mult).then_inc(dve_freed, 1)
                    dve.wait_ge(dve_freed, dve_count[n])
                elif kind == "conv":
                    pad = padded_of[kind, i]
                    dve.wait_ge(act_freed, act_count[n])
                    if pad >= 3:
                        dve.wait_ge(silu_done, pad - 2)
                    gather_tail(pad)
                    taps(4, pad, V_GC + i, 12).then_inc(conv_done, 1)
                    save_state(pad)



def column_norms(nc, C, tag, items):
    n_items = len(items)
    with C.phase() as ph:
        squares = ph.sb(f"{tag}_squares", [P, 2, T])
        logs = ph.sb(f"{tag}_logs", [P, 2, T])
        banks = ph.psum(f"{tag}_sums", [P, 2 * NP, 512])
        squared, summed, logged, rooted, normed = (ph.sem(f"{tag}_{n}") for n in (
            "squared", "summed", "logged", "rooted", "normed"))
        squares_of = [(m, j) for m, it in enumerate(items) for j in range(len(it[0]))]
        through = [sum(len(it[0]) for it in items[:m + 1]) for m in range(n_items)]
        block = ph.block()

        @block.gpsimd
        def _(pool):
            for n, (m, j) in enumerate(squares_of):
                if n >= 2:
                    pool.wait_ge(summed, n - 1)
                x = items[m][0][j]
                nc.gpsimd.tensor_tensor(squares[:, n % 2, :], x, x, ALU.mult).then_inc(squared, 1)

        @block.tensor
        def _(pe):
            for n, (m, j) in enumerate(squares_of):
                pe.wait_ge(squared, n + 1)
                if j == 0 and m >= 2:
                    pe.wait_ge(logged, m - 1)
                for p in range(NP):
                    ins = nc.tensor.matmul(banks[:, (m % 2) * NP + p, 0:TC], items[m][2],
                                           squares[:, n % 2, p * TC:p * TC + TC], start=(j == 0),
                                           stop=(j == len(items[m][0]) - 1), skip_group_check=True)
                ins.then_inc(summed, 1)

        @block.scalar
        def _(act):
            for m in range(n_items):
                act.wait_ge(summed, through[m])
                if m >= 2:
                    act.wait_ge(normed, through[m - 2])
                for p in range(NP):
                    ins = nc.scalar.activation(logs[:, m % 2, p * TC:p * TC + TC], banks[:, (m % 2) * NP + p, 0:TC],
                                               ACT.Ln, scale=items[m][3], bias=C.eps[:, 0:1])
                ins.then_inc(logged, 1)
                act.wait_ge(logged, m + 1)
                nc.scalar.activation(logs[:, m % 2, :], logs[:, m % 2, :], ACT.Exp, scale=-0.5).then_inc(rooted, 1)

        @block.vector
        def _(dve):
            for m in range(n_items):
                dve.wait_ge(rooted, m + 1)
                for j, (x, out) in enumerate(zip(items[m][0], items[m][1])):
                    ins = nc.vector.scalar_tensor_tensor(out, x, items[m][4][j], logs[:, m % 2, :], ALU.mult, ALU.mult)
                    ins.then_inc(normed, 1)


def group_norms(nc, C, M):
    qkv, sq, sk = M["qkv"], M["swa_q"], M["swa_k"]
    items = [([qkv[:, h, :]], [qkv[:, h, :]], C.ones[:], 1.0, [float(P) ** -0.5]) for h in range(HEADS)]
    items += [([qkv[:, 4 + h, :]], [qkv[:, 4 + h, :]], C.ones[:], 1.0, [1.0]) for h in range(HEADS)]
    items += [([x], [x], C.pair_ones[:], 1.0 / SWA_HD, [C.vec[:, v:v + 1]])
              for x, v in ((sq[:, 0, :], V_SQ), (sq[:, 1, :], V_SQ), (sk[:, 0, :], V_SK))]
    column_norms(nc, C, "gn", items)



def gates(nc, C, M):
    with C.phase() as ph:
        raw, pos, neg, e, l = (ph.sb(f"gate_{n}", [P, NT, HEADS]) for n in ("raw", "pos", "neg", "e", "l"))
        eb = ph.sb("gate_eb", [P, NT, HEADS])
        rate = ph.sb("gate_rate", [P, HEADS])
        ps = ph.psum("gate_rows", [P, NT, 8])
        sums = ph.psum("gate_sums", [P, 2, NT, HEADS])
        turned, act_step, dve_step, summed = (ph.sem(f"g_{n}") for n in ("turned", "act_step", "dve_step", "summed"))
        g, beta, up, tail, bu = (M[n] for n in ("g", "beta", "up", "tail", "beta_up"))
        block = ph.block()

        @block.tensor
        def _(pe):
            for t in range(NT):
                ins = nc.tensor.transpose(ps[:, t, :], M["gate"][:, P * t:P * t + P], C.ident[0:8, 0:8])
            ins.then_inc(turned, 1)
            pe.wait_ge(dve_step, 6)
            for kind, a, b in ((0, 0, PT), (1, PT, NT)):
                nc.tensor.matmul(sums[:, 0, a:b, :], C.upto[:, kind, :], g[:, a:b, :], start=True, stop=True)
                ins = nc.tensor.matmul(sums[:, 1, a:b, :], C.after[:, kind, :], g[:, a:b, :], start=True, stop=True)
            ins.then_inc(summed, 1)

        @block.scalar
        def _(act):
            act.wait_ge(dve_step, 1)
            nc.scalar.activation(neg[:], raw[:], ACT.Abs).then_inc(act_step, 1)
            act.wait_ge(act_step, 1)
            nc.scalar.activation(e[:], neg[:], ACT.Exp, scale=-1.0).then_inc(act_step, 1)
            nc.scalar.activation(eb[:], ps[:, :, 4:8], ACT.Exp, scale=-1.0).then_inc(act_step, 1)
            nc.scalar.activation(rate[:], C.a_log[:], ACT.Exp).then_inc(act_step, 1)
            act.wait_ge(act_step, 2)
            nc.scalar.activation(l[:], e[:], ACT.Ln, bias=C.ones[:, 0:1]).then_inc(act_step, 1)
            act.wait_ge(summed, 1)
            nc.scalar.activation(up[:], sums[:, 0], ACT.Exp).then_inc(act_step, 1)
            nc.scalar.activation(tail[:], sums[:, 1], ACT.Exp).then_inc(act_step, 1)
            act.wait_ge(act_step, 7)

        @block.vector
        def _(dve):
            dve.wait_ge(turned, 1)
            nc.vector.tensor_tensor(raw[:], ps[:, :, 0:4], each(C.dt_bias[:], NT), ALU.add).then_inc(dve_step, 1)
            dve.wait_ge(dve_step, 1)
            nc.vector.tensor_scalar(pos[:], raw[:], 0.0, None, ALU.max).then_inc(dve_step, 1)
            dve.wait_ge(act_step, 3)
            nc.vector.tensor_scalar(eb[:], eb[:], 1.0, None, ALU.add).then_inc(dve_step, 1)
            dve.wait_ge(dve_step, 3)
            nc.vector.reciprocal(beta[:], eb[:]).then_inc(dve_step, 1)
            dve.wait_ge(act_step, 5)
            nc.vector.tensor_tensor(pos[:], pos[:], l[:], ALU.add).then_inc(dve_step, 1)
            dve.wait_ge(dve_step, 5)
            nc.vector.scalar_tensor_tensor(g[:], pos[:], -1.0, each(rate[:], NT), ALU.mult, ALU.mult
                                           ).then_inc(dve_step, 1)
            dve.wait_ge(act_step, 6)
            nc.vector.tensor_tensor(bu[:], beta[:], up[:], ALU.mult).then_inc(dve_step, 1)
            dve.wait_ge(dve_step, 7)



def delta_net(nc, C, A, O, M):
    qkv, g, beta, tail, bu = M["qkv"], M["g"], M["beta"], M["tail"], M["beta_up"]
    LEVELS = 6
    UPD = 2 * LEVELS - 1
    STEPS = (("p", 0), ("w", 0), ("p", 1), ("r", 0), ("p", 2), ("w", 1), ("p", 3), ("r", 1),
             ("p", 4), ("p", 5), ("p", 6), ("p", 7), ("p", 8))
    N = 2 * PT

    with C.phase() as ph:
        G = ph.sb("decay_steps", [P, HEADS, P])
        dec, decT = ph.sb("decay", [P, HEADS, P]), ph.sb("decay_t", [P, HEADS, P])
        E = ph.sb("decay_up", [P, 2, HEADS, P])
        low = ph.sb("low", [P, HEADS, P])
        pair = ph.sb("low_pairs", [P, 2, HEADS, P])
        X, XT, ZT = (ph.sb(n, [P, HEADS, P]) for n in ("inv", "inv_t", "inv_low_t"))
        rk, rv = ph.sb("rhs_k", [P, HEADS, P]), ph.sb("rhs_v", [P, HEADS, P])
        kd, qk, qg, u0, wT = (ph.sb(n, [P, 2, HEADS, P]) for n in ("k_tail", "qk_t", "q_up", "u0", "w_t"))
        S, Sg, u = (ph.sb(n, [P, HEADS, P]) for n in ("state", "state_decayed", "u"))
        S0 = ph.sb("sample_state", [P, NB, HEADS, P])
        kdm = ph.sb("k_tail_one", [P, 2, HEADS, P])
        wsT = ph.sb("w_state_t", [P, HEADS, P])
        bank = {n: ph.psum(f"gdn_bank_{n}", [P, HEADS, P]) for n in ("a", "b", "c", "d", "e", "u", "o", "s")}
        (g_ready, sums_done, exp_done, products, low_done, low_scaled, qk_raw, qk_done, qg_done, rhs_done, masked, upd,
         z_done, z_copied, xx_done, xt_done, solved, solved_copied, zeroed, sg_done, ws_done, u_done, os_done,
         s_product, o_copied, s_done, wst_copied, wst_turned, kdm_done, sample_product, sample_decayed,
         sample_done, s0_landed) = (ph.sem(f"d_{n}") for n in (
             "g_ready", "sums_done", "exp_done", "products", "low_done", "low_scaled", "qk_raw", "qk_done", "qg_done",
             "rhs_done", "masked", "upd", "z_done", "z_copied", "xx_done", "xt_done", "solved", "solved_copied",
             "zeroed", "sg_done", "ws_done", "u_done", "os_done", "s_product", "o_copied", "s_done", "wst_copied",
             "wst_turned", "kdm_done", "sample_product", "sample_decayed", "sample_done", "s0_landed"))
        stored = C.state_stored

        def cols(t):
            return slice(P * t, P * t + P)

        def run(prep, scan, sample):
            for t in range(NT):
                for what, s in STEPS:
                    if what == "p":
                        prep(t, s)
                    elif t >= 1:
                        scan(t - 1, s, what)
            sample(NT - 1)

        block = ph.block()

        @block.sync
        def _(sp):
            for b in range(NB):
                sp.dma_start(S0[:, b], A["state_gdn"][0, b].rearrange("h k v -> k h v")).then_inc(s0_landed, 16)
            sp.wait_ge(s_done, N)
            sp.dma_start(O["p_gdn"][0, 0].rearrange("h k v -> k h v"), S[:]).then_inc(stored, 16)
            for b in range(NB):
                sp.wait_ge(sample_done, b + 1)
                sp.dma_start(O["s_gdn"][0, b].rearrange("h k v -> k h v"), S0[:, b]).then_inc(stored, 16)
            sp.wait_ge(stored, 16 * (NB + 1))

        @block.tensor
        def _(pe):
            def prep(t, s):
                kind = t // PT
                if s == 0:
                    pe.wait_ge(g_ready, t + 1)
                    if t:
                        pe.wait_ge(upd, UPD * t)
                    for h in range(HEADS):
                        nc.tensor.matmul(bank["a"][:, h, :], G[:, h, :], C.after[:, kind, :], start=True, stop=True)
                    nc.tensor.matmul(bank["b"][:], C.after[:, kind, :], G[:], start=True, stop=True)
                    nc.tensor.matmul(bank["c"][:], C.ones[:], G[:], start=True, stop=True).then_inc(sums_done, 1)
                elif s == 1:
                    if t:
                        pe.wait_ge(solved_copied, 2 * t)
                    for h in range(HEADS):
                        k = qkv[:, 4 + h, cols(t)]
                        nc.tensor.matmul(bank["d"][:, h, :], k, k, start=True, stop=True)
                    for h in range(HEADS):
                        ins = nc.tensor.matmul(bank["e"][:, h, :], qkv[:, 4 + h, cols(t)], qkv[:, h, cols(t)],
                                               start=True, stop=True)
                    ins.then_inc(products, 1)
                    pe.wait_ge(exp_done, 3 * t + 3)
                    for h in range(HEADS):
                        nc.tensor.transpose(bank["a"][:, h, :], qkv[:, 4 + h, cols(t)], C.ident[:])
                    for h in range(HEADS):
                        ins = nc.tensor.transpose(bank["b"][:, h, :], qkv[:, 8 + h, cols(t)], C.ident[:])
                    ins.then_inc(products, 1)
                elif s == 2:
                    pe.wait_ge(masked, LEVELS * t + 1)
                    for h in range(HEADS):
                        ins = nc.tensor.transpose(bank["c"][:, h, :], pair[:, 0, h, :], C.ident[:])
                    ins.then_inc(z_done, 1)
                elif s < 2 + LEVELS:
                    k = s - 2
                    pe.wait_ge(masked, LEVELS * t + k + 1)
                    pe.wait_ge(upd, UPD * t + 2 * k)
                    if k == 1:
                        pe.wait_ge(rhs_done, t + 1)
                    for h in range(HEADS):
                        ins = nc.tensor.matmul(bank["a"][:, h, :], pair[:, k % 2, h, :], XT[:, h, :],
                                               start=True, stop=True)
                    ins.then_inc(z_done, 1)
                    pe.wait_ge(z_copied, (LEVELS - 1) * t + k)
                    for h in range(HEADS):
                        ins = nc.tensor.matmul(bank["b"][:, h, :], X[:, h, :], ZT[:, h, :], start=True, stop=True)
                    ins.then_inc(xt_done, 1)
                    if k < LEVELS - 1:
                        for h in range(HEADS):
                            ins = nc.tensor.matmul(bank["c"][:, h, :], ZT[:, h, :], X[:, h, :], start=True, stop=True)
                        ins.then_inc(xx_done, 1)
                else:
                    pe.wait_ge(upd, UPD * (t + 1))
                    pe.wait_ge(qk_raw, t + 1)
                    for h in range(HEADS):
                        ins = nc.tensor.matmul(bank["d"][:, h, :], XT[:, h, :], rv[:, h, :], start=True, stop=True)
                    ins.then_inc(solved, 1)
                    for h in range(HEADS):
                        ins = nc.tensor.matmul(bank["e"][:, h, :], rk[:, h, :], XT[:, h, :], start=True, stop=True)
                    ins.then_inc(solved, 1)

            def scan(t, c, what):
                n = 2 * t + c
                r, i = slice(64 * c, 64 * c + 64), t % 2
                if what == "w":
                    pe.wait_ge(solved_copied, 2 * t + 2)
                    if n:
                        pe.wait_ge(s_done, n)
                    else:
                        pe.wait_ge(zeroed, 2)
                    for h in range(HEADS):
                        ins = nc.tensor.matmul(bank["u"][r, h, :], wT[:, i, h, r], S[:, h, :], start=True, stop=True)
                    ins.then_inc(ws_done, 1)
                else:
                    pe.wait_ge(u_done, n + 1)
                    pe.wait_ge(qk_done, t + 1)
                    pe.wait_ge(qg_done, t + 1)
                    if n:
                        pe.wait_ge(o_copied, n)
                    for h in range(HEADS):
                        nc.tensor.matmul(bank["o"][:, h, 0:64], S[:, h, :], qg[:, i, h, r], start=True, stop=False)
                        ins = nc.tensor.matmul(bank["o"][:, h, 0:64], u[:, h, :], qk[:, i, h, r], start=False, stop=True)
                    ins.then_inc(os_done, 1)
                    for h in range(HEADS):
                        ins = nc.tensor.matmul(bank["s"][:, h, :], kd[r, i, h, :], u[r, h, :], start=True, stop=True)
                    ins.then_inc(s_product, 1)

            def sample(t):
                i = t % 2
                pe.wait_ge(solved_copied, 2 * t + 2)
                pe.wait_ge(s0_landed, 16 * NB)
                pe.wait_ge(s_done, N)
                for h in range(HEADS):
                    for b in range(NB):
                        ins = nc.tensor.matmul(bank["u"][:, h, TB * b:TB * b + TB], S0[:, b, h, :],
                                               wT[:, i, h, TB * b:TB * b + TB], start=True, stop=True)
                ins.then_inc(ws_done, 1)
                pe.wait_ge(qg_done, t + 1)
                pe.wait_ge(o_copied, N)
                for h in range(HEADS):
                    for b in range(NB):
                        nc.tensor.matmul(bank["o"][:, h, TB * b:TB * b + TB], S0[:, b, h, :],
                                         qg[:, i, h, TB * b:TB * b + TB], start=(h + b == 0), stop=False,
                                         skip_group_check=True)
                pe.wait_ge(wst_copied, 1)
                for h in range(HEADS):
                    ins = nc.tensor.transpose(bank["s"][:, h, :], wsT[:, h, :], C.ident[:])
                ins.then_inc(wst_turned, 1)
                pe.wait_ge(u_done, N + 1)
                pe.wait_ge(qk_done, t + 1)
                for h in range(HEADS):
                    ins = nc.tensor.matmul(bank["o"][:, h, :], u[:, h, :], qk[:, i, h, :], start=False, stop=True,
                                           skip_group_check=True)
                ins.then_inc(os_done, 1)
                for b in range(NB):
                    pe.wait_ge(kdm_done, b + 1)
                    if b >= 2:
                        pe.wait_ge(sample_done, b - 1)
                    for h in range(HEADS):
                        ins = nc.tensor.matmul(bank["de"[b % 2]][:, h, :], kdm[:, b % 2, h, :], u[:, h, :],
                                               start=True, stop=True)
                    ins.then_inc(sample_product, 1)

            run(prep, scan, sample)

        @block.scalar
        def _(act):
            def prep(t, s):
                if s == 0:
                    act.wait_ge(sums_done, t + 1)
                    if t:
                        act.wait_ge(low_done, t)
                        act.wait_ge(qk_raw, t)
                    if t >= 2:
                        act.wait_ge(s_done, 2 * t - 2)
                    nc.scalar.activation(dec[:], bank["a"][:], ACT.Exp).then_inc(exp_done, 1)
                    nc.scalar.activation(decT[:], bank["b"][:], ACT.Exp).then_inc(exp_done, 1)
                    nc.scalar.activation(E[:, t % 2], bank["c"][:], ACT.Exp).then_inc(exp_done, 1)
                elif 3 <= s < 2 + LEVELS:
                    act.wait_ge(z_done, LEVELS * t + s - 1)
                    nc.scalar.activation(ZT[:], bank["a"][:], ACT.Copy).then_inc(z_copied, 1)
                elif s == 8:
                    for j, (to, b) in enumerate(((u0, "d"), (wT, "e"))):
                        act.wait_ge(solved, 2 * t + j + 1)
                        nc.scalar.activation(to[:, t % 2], bank[b][:], ACT.Copy).then_inc(solved_copied, 1)

            def scan(t, c, what):
                if what == "r":
                    act.wait_ge(os_done, 2 * t + c + 1)
                    nc.scalar.activation(qkv[:, 8:12, P * t + 64 * c:P * t + 64 * c + 64], bank["o"][:, :, 0:64],
                                         ACT.Copy).then_inc(o_copied, 1)

            def sample(t):
                act.wait_ge(ws_done, N + 1)
                nc.scalar.activation(wsT[:], bank["u"][:], ACT.Copy).then_inc(wst_copied, 1)
                act.wait_ge(os_done, N + 1)
                nc.scalar.activation(qkv[:, 8:12, cols(t)], bank["o"][:], ACT.Copy).then_inc(o_copied, 1)
                for b in range(NB):
                    if b >= 2:
                        act.wait_ge(sample_product, b - 1)
                    nc.scalar.activation(kdm[:, b % 2], kd[:, t % 2], ACT.Copy, scale=C.seq_mask[:, b:b + 1]
                                         ).then_inc(kdm_done, 1)

            run(prep, scan, sample)

        @block.gpsimd
        def _(pool):
            def mask(t, k):
                if k >= 2:
                    pool.wait_ge(z_done, LEVELS * t + k - 1)
                if k == 2:
                    pool.wait_ge(upd, UPD * t + 1)
                if t == PT and k >= 4:
                    ins = nc.gpsimd.memset(pair[:, k % 2], 0.0)
                else:
                    ins = nc.gpsimd.tensor_tensor(pair[:, k % 2], low[:], each(C.level[:, k, :], HEADS), ALU.mult)
                ins.then_inc(masked, 1)

            def prep(t, s):
                if s == 1:
                    pool.wait_ge(low_done, t + 1)
                    nc.gpsimd.tensor_tensor(low[:], low[:], over(beta[:, t, :], P), ALU.mult).then_inc(low_scaled, 1)
                    pool.wait_ge(low_scaled, t + 1)
                    if t:
                        pool.wait_ge(z_done, LEVELS * t)
                    mask(t, 0)
                    mask(t, 1)
                    pool.wait_ge(qk_raw, t + 1)
                    nc.gpsimd.tensor_tensor(qk[:, t % 2], qk[:, t % 2], each(C.upto[:, t // PT, :], HEADS), ALU.mult
                                            ).then_inc(qk_done, 1)
                    pool.wait_ge(exp_done, 3 * t + 3)
                    nc.gpsimd.tensor_tensor(qg[:, t % 2], qkv[:, 0:4, cols(t)], E[:, t % 2], ALU.mult
                                            ).then_inc(qg_done, 1)
                elif 3 <= s < 1 + LEVELS:
                    mask(t, s - 1)

            def scan(t, c, what):
                n = 2 * t + c
                if what == "w":
                    if n:
                        pool.wait_ge(s_done, n)
                    else:
                        pool.wait_ge(zeroed, 2)
                    last = 64 * c + 63
                    nc.gpsimd.tensor_tensor(Sg[:], S[:], E[:, t % 2, :, last:last + 1].to_broadcast([P, HEADS, P]),
                                            ALU.mult).then_inc(sg_done, 1)

            def sample(t):
                pool.wait_ge(os_done, N + 1)
                pool.wait_ge(s0_landed, 16 * NB)
                for b in range(NB):
                    last = TB * b + TB - 1
                    nc.gpsimd.tensor_tensor(S0[:, b], S0[:, b],
                                            E[:, t % 2, :, last:last + 1].to_broadcast([P, HEADS, P]), ALU.mult
                                            ).then_inc(sample_decayed, 1)

            run(prep, scan, sample)

        @block.vector
        def _(dve):
            def decay_steps(t):
                nc.vector.tensor_tensor(G[:], each(C.upto[:, t // PT, :], HEADS), over(g[:, t, :], P), ALU.mult
                                        ).then_inc(g_ready, 1)

            def prep(t, s):
                i = t % 2
                if s == 0 and t == 0:
                    nc.vector.memset(S[:], 0.0).then_inc(zeroed, 1)
                    nc.vector.memset(u[:], 0.0).then_inc(zeroed, 1)
                    decay_steps(0)
                elif s == 1:
                    dve.wait_ge(exp_done, 3 * t + 3)
                    dve.wait_ge(products, 2 * t + 1)
                    if t:
                        dve.wait_ge(masked, LEVELS * t)
                    nc.vector.tensor_tensor(low[:], bank["d"][:], dec[:], ALU.mult).then_inc(low_done, 1)
                    if t >= 2:
                        dve.wait_ge(s_done, 2 * t - 2)
                    nc.vector.tensor_tensor(qk[:, i], bank["e"][:], decT[:], ALU.mult).then_inc(qk_raw, 1)
                    dve.wait_ge(products, 2 * t + 2)
                    if t:
                        dve.wait_ge(solved, 2 * t)
                    nc.vector.tensor_tensor(rk[:], bank["a"][:], over(bu[:, t, :], P), ALU.mult)
                    nc.vector.tensor_tensor(rv[:], bank["b"][:], over(beta[:, t, :], P), ALU.mult)
                    nc.vector.tensor_tensor(kd[:, i], bank["a"][:], over(tail[:, t, :], P), ALU.mult
                                            ).then_inc(rhs_done, 1)
                elif s == 2:
                    if t:
                        dve.wait_ge(solved, 2 * t)
                    dve.wait_ge(masked, LEVELS * t + 1)
                    nc.vector.tensor_tensor(X[:], each(C.ident[:], HEADS), pair[:, 0], ALU.subtract).then_inc(upd, 1)
                    dve.wait_ge(z_done, LEVELS * t + 1)
                    nc.vector.tensor_tensor(XT[:], each(C.ident[:], HEADS), bank["c"][:], ALU.subtract).then_inc(upd, 1)
                elif 3 <= s < 2 + LEVELS:
                    k = s - 2
                    dve.wait_ge(xt_done, (LEVELS - 1) * t + k)
                    dve.wait_ge(upd, UPD * t + 2 * k)
                    nc.vector.tensor_tensor(XT[:], XT[:], bank["b"][:], ALU.subtract).then_inc(upd, 1)
                    if k < LEVELS - 1:
                        dve.wait_ge(xx_done, (LEVELS - 2) * t + k)
                        nc.vector.tensor_tensor(X[:], X[:], bank["c"][:], ALU.subtract).then_inc(upd, 1)
                elif s == 8:
                    if t + 1 < NT:
                        dve.wait_ge(sums_done, t + 1)
                        decay_steps(t + 1)

            def scan(t, c, what):
                n = 2 * t + c
                r = slice(64 * c, 64 * c + 64)
                if what == "w":
                    dve.wait_ge(ws_done, n + 1)
                    dve.wait_ge(solved_copied, 2 * t + 2)
                    if n:
                        dve.wait_ge(s_done, n)
                    else:
                        dve.wait_ge(zeroed, 2)
                    nc.vector.tensor_tensor(u[r], u0[r, t % 2], bank["u"][r], ALU.subtract).then_inc(u_done, 1)
                else:
                    dve.wait_ge(s_product, n + 1)
                    dve.wait_ge(sg_done, n + 1)
                    nc.vector.tensor_tensor(S[:], Sg[:], bank["s"][:], ALU.add).then_inc(s_done, 1)

            def sample(t):
                dve.wait_ge(wst_turned, 1)
                dve.wait_ge(solved_copied, 2 * t + 2)
                nc.vector.tensor_tensor(u[:], u0[:, t % 2], bank["s"][:], ALU.subtract).then_inc(u_done, 1)
                for b in range(NB):
                    dve.wait_ge(sample_product, b + 1)
                    dve.wait_ge(sample_decayed, b + 1)
                    nc.vector.tensor_tensor(S0[:, b], S0[:, b], bank["de"[b % 2]][:], ALU.add).then_inc(sample_done, 1)

            run(prep, scan, sample)


def gdn_output(nc, C, M):
    o = M["qkv"]
    items = [([o[:, 8 + h, :]], [o[:, 8 + h, :]], C.ones[:], 1.0 / P, [C.vec[:, V_GN:V_GN + 1]]) for h in range(HEADS)]
    column_norms(nc, C, "go", items)
    with C.phase() as ph:
        gated = ph.sem("go_gated")
        block = ph.block()

        @block.vector
        def _(dve):
            for h in range(2):
                nc.vector.tensor_tensor(C.mixT[:, h, :], C.mixT[:, h, :], o[:, 8 + h, :], ALU.mult).then_inc(gated, 1)
            dve.wait_ge(gated, 4)

        @block.gpsimd
        def _(pool):
            for h in range(2, HEADS):
                nc.gpsimd.tensor_tensor(C.mixT[:, h, :], C.mixT[:, h, :], o[:, 8 + h, :], ALU.mult).then_inc(gated, 1)



def attention(nc, C, tag, scale, hide, sinks, scores, sample_scores, values, dest, loads=None, buffers=None,
              early=None, sample_copies=None):
    slots, turned_parts, new_scores, finish_scores = sample_scores
    with C.phase() as ph:
        p = ph.sb(f"{tag}_p", [P, 2, HEADS, 256])
        pT = ph.sb(f"{tag}_pt", [P, 2, 8, P])
        mx, nm, den, rec, es = (ph.sb(f"{tag}_{n}", [P, 2, HEADS]) for n in ("mx", "nm", "den", "rec", "es"))
        B = buffers(ph) if buffers else {}
        s_bank = ph.psum(f"{tag}_scores", [P, 2, HEADS, 256])
        t_bank = ph.psum(f"{tag}_turned", [P, 8, P])
        o_bank = ph.psum(f"{tag}_out", [P, 8, P])
        names = ("scored", "hidden", "maxed", "max_step", "exp_done", "summed", "normed", "turned", "turned_copied",
                 "valued", "out_copied", "early", "sample_scored", "sample_copied")
        s = {n: ph.sem(f"{tag}_{n}") for n in names}
        block = ph.block()
        act_exps = HEADS + (1 if sinks is not None else 0)
        max_steps = 4 if sinks is not None else 2
        last = NT - 1

        @block.sync
        def _(sp):
            if loads:
                loads(sp, B, s)

        @block.tensor
        def _(pe):
            if early:
                early["pe"](pe, B, s, t_bank, o_bank)

            def score(t):
                if t >= 2:
                    pe.wait_ge(s["hidden"] if hide else s["exp_done"], t - 1 if hide else act_exps * (t - 1))
                if t < last:
                    scores(pe, t, s_bank[:, t % 2]).then_inc(s["scored"], 1)
                    return
                pe.wait_ge(s["out_copied"], last)
                pe.wait_ge(s["turned_copied"], last)
                turned_parts(pe, B, s, t_bank, o_bank)
                pe.wait_ge(s["sample_copied"], 1)
                for slot, h, half in slots:
                    ins = nc.tensor.transpose(s_bank[:, t % 2, h, P * half:P * half + P], pT[:, 1 - (last - 1) % 2, slot, :],
                                              C.ident[:])
                if new_scores:
                    ins = new_scores(pe, s_bank[:, t % 2])
                ins.then_inc(s["scored"], 1)

            def output(t):
                pe.wait_ge(s["normed"], t + 1)
                if t:
                    pe.wait_ge(s["turned_copied"], t)
                for half in range(2):
                    for h in range(HEADS):
                        ins = nc.tensor.transpose(t_bank[:, 4 * half + h, :], p[:, t % 2, h, P * half:P * half + P],
                                                  C.ident[:])
                ins.then_inc(s["turned"], 1)
                pe.wait_ge(s["turned_copied"], t + 1)
                if t:
                    pe.wait_ge(s["out_copied"], t)
                values(pe, t, pT[:, t % 2], o_bank, B, s).then_inc(s["valued"], 1)

            for t in range(NT + 1):
                if t < last:
                    score(t)
                if t >= 1:
                    output(t - 1)
                if t == last:
                    score(t)

        def output_copy(dve, t):
            dve.wait_ge(s["valued"], t + 1)
            to, frm = dest(t, o_bank)
            nc.vector.tensor_copy(to, frm).then_inc(s["out_copied"], 1)

        @block.vector
        def _(dve):
            if early and "dve" in early:
                early["dve"](dve, B, s, t_bank, o_bank)
            for t in range(NT):
                i = t % 2
                if t == last:
                    output_copy(dve, t - 1)
                    if sample_copies:
                        sample_copies(dve, B, s, o_bank)
                dve.wait_ge(s["scored"], t + 1)
                if t >= 2:
                    dve.wait_ge(s["exp_done"], act_exps * (t - 1))
                src = s_bank[:, i]
                if hide:
                    kind = 1 if t == 0 else 2 if t == last else 0
                    if t >= 2:
                        dve.wait_ge(s["turned"], t - 1)
                    nc.vector.scalar_tensor_tensor(p[:, i], s_bank[:, i], scale, each(C.hide[:, kind, :], HEADS),
                                                   ALU.mult, ALU.add).then_inc(s["hidden"], 1)
                    dve.wait_ge(s["hidden"], t + 1)
                    src = p[:, i]
                nc.vector.tensor_reduce(mx[:, i], src, AX.X, ALU.max).then_inc(s["max_step"], 1)
                dve.wait_ge(s["max_step"], max_steps * t + 1)
                if sinks is not None:
                    nc.vector.tensor_tensor(mx[:, i], mx[:, i], sinks, ALU.max).then_inc(s["max_step"], 1)
                    dve.wait_ge(s["max_step"], max_steps * t + 2)
                    if t >= 2:
                        dve.wait_ge(s["summed"], t - 1)
                    nc.vector.tensor_tensor(es[:, i], sinks, mx[:, i], ALU.subtract).then_inc(s["max_step"], 1)
                nc.vector.tensor_scalar(nm[:, i], mx[:, i], -1.0 if hide else -scale, None, ALU.mult
                                        ).then_inc(s["max_step"], 1)
                dve.wait_ge(s["exp_done"], act_exps * (t + 1))
                if sinks is not None:
                    nc.vector.tensor_tensor(den[:, i], den[:, i], es[:, i], ALU.add).then_inc(s["maxed"], 1)
                    dve.wait_ge(s["maxed"], t + 1)
                if t >= 2:
                    dve.wait_ge(s["normed"], t - 1)
                nc.vector.reciprocal(rec[:, i], den[:, i]).then_inc(s["summed"], 1)
                if 1 <= t < last:
                    output_copy(dve, t - 1)
            output_copy(dve, last)

        @block.scalar
        def _(act):
            if early and "act" in early:
                early["act"](act, B, s, t_bank, o_bank)

            def copy_turned(t):
                act.wait_ge(s["turned"], t + 1)
                if t >= 2:
                    act.wait_ge(s["valued"], t - 1)
                nc.scalar.activation(pT[:, t % 2], t_bank[:], ACT.Copy).then_inc(s["turned_copied"], 1)

            for t in range(NT):
                i = t % 2
                if t == last:
                    copy_turned(t - 1)
                    act.wait_ge(s["sample_scored"], 1)
                    act.wait_ge(s["valued"], last - 1)
                    nc.scalar.activation(pT[:, 1 - (last - 1) % 2], t_bank[:], ACT.Copy).then_inc(s["sample_copied"], 1)
                act.wait_ge(s["max_step"], max_steps * (t + 1))
                if t >= 2:
                    act.wait_ge(s["turned"], t - 1)
                    act.wait_ge(s["summed"], t - 1)
                src = p if hide else s_bank
                for h in range(HEADS):
                    nc.scalar.activation(p[:, i, h, :], src[:, i, h, :], ACT.Exp, bias=nm[:, i, h:h + 1],
                                         scale=1.0 if hide else scale, accum_out=den[:, i, h:h + 1]
                                         ).then_inc(s["exp_done"], 1)
                if sinks is not None:
                    nc.scalar.activation(es[:, i], es[:, i], ACT.Exp).then_inc(s["exp_done"], 1)
                if t >= 1 and t < last:
                    copy_turned(t - 1)
            copy_turned(last)

        @block.gpsimd
        def _(pool):
            for t in range(NT):
                pool.wait_ge(s["summed"], t + 1)
                nc.gpsimd.tensor_tensor(p[:, t % 2], p[:, t % 2], over(rec[:, t % 2], 256), ALU.mult
                                        ).then_inc(s["normed"], 1)


def window_attention(nc, C, A, O, M):
    sq, sk, sv = M["swa_q"], M["swa_k"], M["swa_v"]

    def buffers(ph):
        return {"v": ph.sb("swa_v_rows", [P, NT, P]), "kp": ph.sb("swa_k_past", [P, NB, P]),
                "vp": ph.sb("swa_v_past", [P, NB, P]), "kpT": ph.sb("swa_k_past_t", [P, NB, P]),
                "k_rows": ph.sb("swa_k_rows", [P, 2, P]),
                "landed": ph.sem("swa_past_landed"), "stored": C.window_stored, "copied": ph.sem("swa_rows_copied")}

    def loads(sp, B, s):
        sp.dma_start(B["kp"][:], A["cache_swa_k"][0].rearrange("b k h d -> k b (h d)")).then_inc(B["landed"], 16)
        sp.dma_start(B["vp"][:], A["cache_swa_v"][0].rearrange("b k h d -> k b (h d)")).then_inc(B["landed"], 16)
        sp.wait_ge(B["copied"], 5)
        for j, (k, v) in enumerate((("p_swa_k", "p_swa_v"), ("s_swa_k", "s_swa_v"))):
            for name, rows in ((k, B["k_rows"][:, j, :]), (v, B["v"][:, PT - 1 + j, :])):
                sp.dma_start(O[name][0].rearrange("b t h d -> (b t) (h d)"), rows).then_inc(B["stored"], 16)
        sp.wait_ge(B["stored"], 64)

    groups = [[("kp", b) for b in range(8)], [("v", t) for t in range(8)], [("v", 8), ("k", 7), ("k", 8)]]

    def early_pe(pe, B, s, t_bank, o_bank):
        pe.wait_ge(B["landed"], 32)
        for n, group in enumerate(groups):
            if n == 2:
                pe.wait_ge(B["copied"], 2)
            bank = t_bank if n % 2 == 0 else o_bank
            for j, (what, t) in enumerate(group):
                src = B["kp"][:, t, :] if what == "kp" else (sk if what == "k" else sv)[:, 0, P * t:P * t + P]
                ins = nc.tensor.transpose(bank[:, j, :], src, C.ident[:])
            ins.then_inc(s["early"], 1)
        pe.wait_ge(B["copied"], 5)

    def early_dve(dve, B, s, t_bank, o_bank):
        for n, (to, frm) in enumerate(((B["kpT"][:, 0:4], t_bank[:, 0:4]), (B["kpT"][:, 4:8], t_bank[:, 4:8]),
                                       (B["v"][:, 0:8], o_bank[:]), (B["v"][:, 8], t_bank[:, 0]),
                                       (B["k_rows"][:], t_bank[:, 1:3]))):
            dve.wait_ge(s["early"], (1, 1, 2, 3, 3)[n])
            nc.vector.tensor_copy(to, frm).then_inc(B["copied"], 1)

    def half(h):
        return slice(64 * (h // 2), 64 * (h // 2) + 64)

    def scores(pe, t, out):
        for h in range(HEADS):
            q = sq[half(h), h % 2, P * t:P * t + P]
            if t:
                ins = nc.tensor.matmul(out[:, h, :], q, sk[half(h), 0, P * t - P:P * t + P], start=True, stop=True)
            else:
                for j in range(2):
                    ins = nc.tensor.matmul(out[:, h, P * j:P * j + P], q, sk[half(h), 0, 0:P], start=True, stop=True)
        return ins

    def turned_parts(pe, B, s, t_bank, o_bank):
        for h in range(HEADS):
            slot = 4 * (h // 2) + h % 2
            for b in range(NB):
                ins = nc.tensor.matmul(t_bank[:, slot, TB * b:TB * b + TB], B["kpT"][half(h), b, :],
                                       sq[half(h), h % 2, TP + TB * b:TP + TB * b + TB], start=True, stop=True)
        ins.then_inc(s["sample_scored"], 1)

    def new_scores(pe, out):
        for h in range(HEADS):
            ins = nc.tensor.matmul(out[:, h, P:2 * P], sq[half(h), h % 2, TP:T], sk[half(h), 0, TP:T],
                                   start=True, stop=True)
        return ins

    def values(pe, t, pT, out, B, s):
        for h in range(HEADS):
            kv = slice(64 * (h // 2), 64 * (h // 2) + 64)
            o = out[64 * (h % 2):64 * (h % 2) + 64, h // 2, :]
            if t < NT - 1:
                nc.tensor.matmul(o, B["v"][:, max(t - 1, 0), kv], pT[:, h, :], start=True, stop=False)
                ins = nc.tensor.matmul(o, B["v"][:, t, kv], pT[:, 4 + h, :], start=False, stop=True)
            else:
                nc.tensor.matmul(o, B["v"][:, t, kv], pT[:, 4 + h, :], start=True, stop=False, skip_group_check=True)
                for b in range(NB):
                    ins = nc.tensor.matmul(o[:, TB * b:TB * b + TB], B["vp"][:, b, kv], pT[:, h, TB * b:TB * b + TB],
                                           start=False, stop=(b == NB - 1), skip_group_check=True)
        return ins

    def dest(t, o_bank):
        return C.mixT[:, 4:6, P * t:P * t + P], o_bank[:, 0:2, :]

    slots = [(4 * (h // 2) + h % 2, h, 0) for h in range(HEADS)]
    attention(nc, C, "sw", float(SWA_HD) ** -0.5, True, C.sinks[:], scores, (slots, turned_parts, new_scores, None),
              values, dest, loads, buffers, {"pe": early_pe, "dve": early_dve})



def row_projection(nc, C, tag, actT, n_tiles, w_dram, out, residual=None, add=True, more=None):
    with C.phase() as ph:
        w = ph.sb(f"{tag}_w", [P, KD, D])
        banks = ph.psum(f"{tag}_banks", [P, 4, 512])
        w_landed = [ph.sem(f"{tag}_w_landed{k}") for k in range(KD)]
        r_landed = [ph.sem(f"{tag}_r_landed{t}") for t in range(n_tiles if residual else 0)]
        projected, freed = ph.sem(f"{tag}_projected"), ph.sem(f"{tag}_freed")
        block = ph.block()

        @block.sync
        def _(sp):
            for k in range(KD):
                sp.dma_start(w[:, k, :], w_dram[P * k:P * k + P, :]).then_inc(w_landed[k], 16)
            for t, rows in enumerate(residual or ()):
                sp.dma_start(out[:, t, :], rows).then_inc(r_landed[t], 16)

        @block.tensor
        def _(pe):
            for n in range(2 * n_tiles):
                t, half = divmod(n, 2)
                if n >= 4:
                    pe.wait_ge(freed, n - 3)
                for k in range(KD):
                    if n == 0:
                        pe.wait_ge(w_landed[k], 16)
                    ins = nc.tensor.matmul(banks[:, n % 4, :], actT[:, k, P * t:P * t + P],
                                           w[:, k, 512 * half:512 * half + 512], start=(k == 0), stop=(k == KD - 1))
                ins.then_inc(projected, 1)

        @block.vector
        def _(dve):
            for n in range(2 * n_tiles):
                t, half = divmod(n, 2)
                to = out[:, t, 512 * half:512 * half + 512]
                if residual and half == 0:
                    dve.wait_ge(r_landed[t], 16)
                dve.wait_ge(projected, n + 1)
                if add:
                    nc.vector.tensor_tensor(to, to, banks[:, n % 4, :], ALU.add).then_inc(freed, 1)
                else:
                    nc.vector.tensor_copy(to, banks[:, n % 4, :]).then_inc(freed, 1)


def feature_projection(nc, C, tag, xT, w_dram, n_tiles, out):
    RING = 4
    with C.phase() as ph:
        w = ph.sb(f"{tag}_w", [P, RING, KD, P])
        banks = ph.psum(f"{tag}_banks", [P, 2 * NP, 512])
        w_landed = [ph.sem(f"{tag}_w_landed{r}") for r in range(RING)]
        projected, freed = ph.sem(f"{tag}_projected"), ph.sem(f"{tag}_freed")
        block = ph.block()

        @block.sync
        def _(sp):
            for n in range(n_tiles):
                if n >= RING:
                    sp.wait_ge(projected, NP * (n - RING + 1))
                sp.dma_start(w[:, n % RING], w_dram.rearrange("(k p) c -> p k c", p=P)[:, :, P * n:P * n + P]
                             ).then_inc(w_landed[n % RING], 16)

        @block.tensor
        def _(pe):
            for n in range(n_tiles):
                pe.wait_ge(w_landed[n % RING], 16 * (n // RING + 1))
                if n >= 2:
                    pe.wait_ge(freed, n - 1)
                for p in range(NP):
                    for k in range(KD):
                        ins = nc.tensor.matmul(banks[:, (n % 2) * NP + p, 0:TC], w[:, n % RING, k, :],
                                               xT[:, k, TC * p:TC * p + TC], start=(k == 0), stop=(k == KD - 1))
                    ins.then_inc(projected, 1)

        @block.scalar
        def _(act):
            for n in range(n_tiles):
                for p in range(NP):
                    act.wait_ge(projected, NP * n + p + 1)
                    ins = nc.scalar.activation(out[:, n, TC * p:TC * p + TC], banks[:, (n % 2) * NP + p, 0:TC], ACT.Copy)
                ins.then_inc(freed, 1)



def memory_kv(nc, C, A, O, kT, v):
    with ExitStack() as st:
        rows = st.enter_context(nc.sbuf_tensor("mem_rows", [P, 2, D], F32))
        mT = st.enter_context(nc.sbuf_tensor("mem_t", [P, KD, MEM], F32))
        norm_turn(nc, C, "nm", rows, [A["mem_prompt"][0, P * t:P * t + P, :] for t in range(2)], 2, V_MIN, mT)
        k = rows
        row_projection(nc, C, "mk", mT, 2, A["w_mk"][0], k, add=False)
        row_projection(nc, C, "mv", mT, 2, A["w_mv"][0], v, add=False)
        with C.phase() as ph:
            squares = ph.sb("mk_squares", [P, 256])
            sums, root, inv = (ph.sb(f"mk_{n}", [P, 2 * HEADS]) for n in ("sums", "root", "inv"))
            banks = ph.psum("mk_turned", [P, 4, 512])
            summed, rooted, inverted, normed, turned, copied = (ph.sem(f"mk_{n}") for n in (
                "summed", "rooted", "inverted", "normed", "turned", "copied"))
            stored = C.memory_stored
            block = ph.block()

            @block.sync
            def _(sp):
                sp.dma_start(O["p_mem_v"][0, 0].rearrange("(t p) h d -> p t (h d)", p=P), v[:]).then_inc(stored, 16)
                sp.wait_ge(normed, 2 * HEADS)
                sp.dma_start(O["p_mem_k"][0, 0].rearrange("(t p) h d -> p t (h d)", p=P), k[:]).then_inc(stored, 16)
                sp.wait_ge(stored, 32)

            @block.scalar
            def _(act):
                for n in range(2 * HEADS):
                    t, h = divmod(n, HEADS)
                    if n:
                        act.wait_ge(summed, n)
                    nc.scalar.activation(squares[:], k[:, t, 256 * h:256 * h + 256], ACT.Square,
                                         accum_out=sums[:, n:n + 1]).then_inc(summed, 1)
                act.wait_ge(summed, 2 * HEADS)
                nc.scalar.activation(root[:], sums[:], ACT.Sqrt, scale=1.0 / 256, bias=C.eps[:, 0:1]).then_inc(rooted, 1)

            @block.vector
            def _(dve):
                dve.wait_ge(rooted, 1)
                nc.vector.reciprocal(inv[:], root[:]).then_inc(inverted, 1)
                dve.wait_ge(inverted, 1)
                for n in range(2 * HEADS):
                    t, h = divmod(n, HEADS)
                    x = k[:, t, 256 * h:256 * h + 256]
                    nc.vector.scalar_tensor_tensor(x, x, inv[:, n:n + 1], C.k_gain[:], ALU.mult, ALU.mult
                                                   ).then_inc(normed, 1)
                for n in range(4):
                    dve.wait_ge(turned, n + 1)
                    nc.vector.tensor_copy(kT[:, 2 * n:2 * n + 2, :], banks[:, n, :].rearrange("p (a b) -> p a b", a=2)
                                          ).then_inc(copied, 1)

            @block.tensor
            def _(pe):
                pe.wait_ge(normed, 2 * HEADS)
                for n in range(4):
                    for j in range(2):
                        for t in range(2):
                            f = 2 * n + j
                            ins = nc.tensor.transpose(banks[:, n, 256 * j + P * t:256 * j + P * t + P],
                                                      k[:, t, P * f:P * f + P], C.ident[:])
                    ins.then_inc(turned, 1)


def memory_attention(nc, C, A, qT, kT, v, attnT):

    def buffers(ph):
        return {"kb": ph.sb("mem_k_one", [P, 2, 2, D]), "vb": ph.sb("mem_v_one", [P, 2, 2, D]),
                "kbT": ph.sb("mem_k_one_t", [P, KD, MEM]),
                "k_landed": [ph.sem(f"mem_k_landed{i}") for i in range(2)],
                "v_landed": [ph.sem(f"mem_v_landed{i}") for i in range(2)],
                "k_turned": ph.sem("mem_k_turned"), "k_copied": ph.sem("mem_k_copied"),
                "k_used": ph.sem("mem_k_used"), "v_used": ph.sem("mem_v_used")}

    def loads(sp, B, s):
        for b in range(NB):
            if b >= 2:
                sp.wait_ge(B["k_turned"], 4 * (b - 1))
            sp.dma_start(B["kb"][:, b % 2], A["cache_mem_k"][0, b].rearrange("(t p) h d -> p t (h d)", p=P)
                         ).then_inc(B["k_landed"][b % 2], 16)
        for b in range(NB):
            if b >= 2:
                sp.wait_ge(B["v_used"], b - 1)
            sp.dma_start(B["vb"][:, b % 2], A["cache_mem_v"][0, b].rearrange("(t p) h d -> p t (h d)", p=P)
                         ).then_inc(B["v_landed"][b % 2], 16)

    def scores(pe, t, out):
        for h in range(HEADS):
            for j in range(2):
                ins = nc.tensor.matmul(out[:, h, :], qT[:, 2 * h + j, P * t:P * t + P], kT[:, 2 * h + j, :],
                                       start=(j == 0), stop=(j == 1))
        return ins

    def turned_parts(pe, B, s, t_bank, o_bank):
        for b in range(NB):
            pe.wait_ge(B["k_landed"][b % 2], 16 * (b // 2 + 1))
            for n in range(4):
                m = 4 * b + n
                if m >= 2:
                    pe.wait_ge(B["k_copied"], m - 1)
                for j in range(2):
                    for kt in range(2):
                        ins = nc.tensor.transpose(o_bank[:, 4 * (n % 2) + 2 * j + kt, :],
                                                  B["kb"][:, b % 2, kt, P * (2 * n + j):P * (2 * n + j) + P], C.ident[:])
                ins.then_inc(B["k_turned"], 1)
            pe.wait_ge(B["k_copied"], 4 * b + 4)
            for kt in range(2):
                for h in range(HEADS):
                    for j in range(2):
                        ins = nc.tensor.matmul(t_bank[:, 4 * kt + h, TB * b:TB * b + TB],
                                               B["kbT"][:, 2 * h + j, P * kt:P * kt + P],
                                               qT[:, 2 * h + j, TP + TB * b:TP + TB * b + TB],
                                               start=(j == 0), stop=(j == 1))
            ins.then_inc(B["k_used"], 1)
        pe.wait_ge(B["k_used"], NB)
        pe.sem_inc(s["sample_scored"], 1)

    def sample_copies(dve, B, s, o_bank):
        for m in range(4 * NB):
            b, n = divmod(m, 4)
            dve.wait_ge(B["k_turned"], m + 1)
            if b:
                dve.wait_ge(B["k_used"], b)
            nc.vector.tensor_copy(B["kbT"][:, 2 * n:2 * n + 2, :], o_bank[:, 4 * (n % 2):4 * (n % 2) + 4, :].rearrange(
                "p (j k) c -> p j (k c)", j=2)).then_inc(B["k_copied"], 1)

    def values(pe, t, pT, out, B, s):
        if t < NT - 1:
            for h in range(HEADS):
                for j in range(2):
                    f = 2 * h + j
                    for kt in range(2):
                        ins = nc.tensor.matmul(out[:, f, :], v[:, kt, P * f:P * f + P], pT[:, 4 * kt + h, :],
                                               start=(kt == 0), stop=(kt == 1))
            return ins
        for b in range(NB):
            pe.wait_ge(B["v_landed"][b % 2], 16 * (b // 2 + 1))
            for h in range(HEADS):
                for j in range(2):
                    f = 2 * h + j
                    for kt in range(2):
                        ins = nc.tensor.matmul(out[:, f, TB * b:TB * b + TB], B["vb"][:, b % 2, kt, P * f:P * f + P],
                                               pT[:, 4 * kt + h, TB * b:TB * b + TB], start=(kt == 0), stop=(kt == 1))
            if b < NB - 1:
                ins.then_inc(B["v_used"], 1)
        return ins

    def dest(t, o_bank):
        return attnT[:, :, P * t:P * t + P], o_bank[:]

    slots = [(4 * kt + h, h, kt) for kt in range(2) for h in range(HEADS)]
    attention(nc, C, "ma", 1.0 / 16, False, None, scores, (slots, turned_parts, None, None), values, dest,
              loads, buffers, None, sample_copies)



def ffn_states_in(nc, C, A, old):
    n_tiles = 2 * NF
    with C.phase() as ph:
        rows = ph.sb("ffn_old_rows", [16, 2 * FF])
        banks = ph.psum("ffn_old_t", [P, 2, 22, 16])
        landed, turned, copied = (ph.sem(f"fs_{n}") for n in ("landed", "turned", "copied"))
        block = ph.block()

        @block.sync
        def _(sp):
            sp.dma_start(rows[:], A["state_ffn_conv"][0].rearrange("b i c -> (b i) c")).then_inc(landed, 16)

        @block.tensor
        def _(pe):
            pe.wait_ge(landed, 16)
            for n in range(n_tiles):
                ins = nc.tensor.transpose(banks[:, n // 22, n % 22, :], rows[:, P * n:P * n + P], C.ident[0:16, 0:16])
            ins.then_inc(turned, 1)

        @block.vector
        def _(dve):
            dve.wait_ge(turned, 1)
            for i in range(2):
                nc.vector.tensor_copy(old[:, 22 * i:22 * i + 22, :], banks[:, i]).then_inc(copied, 1)
            dve.wait_ge(copied, 2)


def ffn(nc, C, A, O, h, hi, lo, old):
    W = 3
    L = xp_len(W)
    LY = L - (W - 1)
    NG = 2 * NT
    with C.phase() as ph:
        raw = ph.sb("up_raw", [P, 2, KD, P])
        w_hi, w_lo = ph.sb("up_hi", [P, 2, KD, P], F32R), ph.sb("up_lo", [P, 2, KD, P], F32R)
        d_raw = ph.sb("down_raw", [P, D])
        d_hi, d_lo = ph.sb("down_hi", [P, D], F32R), ph.sb("down_lo", [P, D], F32R)
        xp = ph.sb("ffn_conv_in", [P, 2, L])
        y = ph.sb("ffn_conv_out", [P, 2, LY + 2])
        a = ph.sb("ffn_gated", [P, T])
        a_hi, a_lo = ph.sb("gated_hi", [P, T], F32R), ph.sb("gated_lo", [P, T], F32R)
        tails = ph.sb("ffn_tails", [P, 2, NF, 18])
        new_rows = ph.sb("ffn_new_rows", [18, 4, P])
        banks = ph.psum("up_banks", [P, 2 * NP, 512])
        d_banks = ph.psum("down_banks", [P, 2, 512])
        w_landed, split, w_high, up, evacuated, padded, tailed, tap0, conv = (
            [ph.sem(f"f_{n}_{s}") for s in "gv"] for n in (
                "w_landed", "split", "w_high", "up", "evacuated", "padded", "tailed", "tap0", "conv"))
        d_landed, d_split, d_high, silued, gated, a_high, a_ready, down, added, conv_step, zeroed = (
            ph.sem(f"f_{n}") for n in ("d_landed", "d_split", "d_high", "silued", "gated", "a_high", "a_ready", "down",
                                       "added", "conv_step", "zeroed"))
        G, V = 0, 1
        block = ph.block()

        def cycles(body):
            for f in range(NF + 1):
                body(f, f < NF, f >= 1)

        @block.sync
        def _(sp):
            w_up = A["w_up"][0].rearrange("(k p) c -> p k c", p=P)
            w_down = A["w_down"][0].rearrange("(f p) c -> f p c", p=P)

            def body(f, now, before):
                if now:
                    for s in (G, V):
                        if before:
                            sp.wait_ge(split[s], f)
                        sp.dma_start(raw[:, s], w_up[:, :, FF * s + P * f:FF * s + P * f + P]).then_inc(w_landed[s], 16)
                    if before:
                        sp.wait_ge(d_split, f)
                    sp.dma_start(d_raw[:], w_down[f]).then_inc(d_landed, 16)
            cycles(body)

        @block.tensor
        def _(pe):
            def project(s, f, before):
                pe.wait_ge(split[s], f + 1)
                if before:
                    pe.wait_ge(evacuated[s], f)
                for p in range(NP):
                    n = 0
                    for k in range(KD):
                        for wt, x in ((w_hi, hi), (w_hi, lo), (w_lo, hi)):
                            ins = nc.tensor.matmul(banks[:, NP * s + p, 0:TC], wt[:, s, k, :], x[:, k, TC * p:TC * p + TC],
                                                   start=(n == 0), stop=(n == 3 * KD - 1))
                            n += 1
                    ins.then_inc(up[s], 1)

            def body(f, now, before):
                if now:
                    project(G, f, before)
                    project(V, f, before)
                if before:
                    pe.wait_ge(a_ready, f)
                    pe.wait_ge(d_split, f)
                    for n in range(NG):
                        t, half = divmod(n, 2)
                        if n >= 2:
                            pe.wait_ge(added, NG * (f - 1) + n - 1)
                        tok, col = slice(P * t, P * t + P), slice(512 * half, 512 * half + 512)
                        nc.tensor.matmul(d_banks[:, n % 2, :], a_hi[:, tok], d_hi[:, col], start=True, stop=False)
                        nc.tensor.matmul(d_banks[:, n % 2, :], a_hi[:, tok], d_lo[:, col], start=False, stop=False)
                        nc.tensor.matmul(d_banks[:, n % 2, :], a_lo[:, tok], d_hi[:, col], start=False, stop=True
                                         ).then_inc(down, 1)
            cycles(body)

        @block.scalar
        def _(act):
            def weights_high(s, f, before):
                act.wait_ge(w_landed[s], 16 * (f + 1))
                if before:
                    act.wait_ge(up[s], NP * f)
                nc.scalar.activation(w_hi[:, s], raw[:, s], ACT.Copy).then_inc(w_high[s], 1)

            def evacuate(s, f, before):
                if before:
                    act.wait_ge(conv[s], f)
                    act.wait_ge(tailed[s], f)
                for p in range(NP):
                    act.wait_ge(up[s], NP * f + p + 1)
                    cn = TC if p < 2 else PP
                    nc.scalar.activation(xp[:, s, W - 1 + TC * p:W - 1 + TC * p + cn], banks[:, NP * s + p, 0:cn], ACT.Copy)
                nc.scalar.activation(xp_sample(xp[:, s, :], W, W - 1, TB), seqs(banks[:, NP * s + 2, PP:TC]), ACT.Copy
                                     ).then_inc(evacuated[s], 1)

            def first_tap(s, f, before):
                act.wait_ge(evacuated[s], f + 1)
                act.wait_ge(padded[s], f + 1)
                if before:
                    act.wait_ge(gated, f)
                col = V_FC + NF * s + f
                nc.scalar.activation(y[:, s, 0:LY], xp[:, s, 0:LY], ACT.Copy, scale=C.vec[:, col:col + 1]
                                     ).then_inc(tap0[s], 1)

            def body(f, now, before):
                if before:
                    first_tap(V, f - 1, f >= 2)
                if now:
                    if not before:
                        weights_high(G, 0, False)
                    weights_high(V, f, before)
                if before:
                    act.wait_ge(conv[G], f)
                    nc.scalar.activation(y[:, G, 0:LY], y[:, G, 0:LY], ACT.Silu).then_inc(silued, 1)
                    act.wait_ge(d_landed, 16 * f)
                    if f >= 2:
                        act.wait_ge(down, NG * (f - 1))
                    nc.scalar.activation(d_hi[:], d_raw[:], ACT.Copy).then_inc(d_high, 1)
                    act.wait_ge(gated, f)
                    nc.scalar.activation(a_hi[:], a[:], ACT.Copy).then_inc(a_high, 1)
                if now:
                    evacuate(G, f, before)
                    first_tap(G, f, before)
                    if f + 1 < NF:
                        weights_high(G, f + 1, True)
                    evacuate(V, f, before)
            cycles(body)

        @block.gpsimd
        def _(pool):
            nc.gpsimd.memset(xp[:, :, 0:W - 1], 0.0).then_inc(zeroed, 1)
            pool.wait_ge(zeroed, 1)

            def weights_low(s, f, before):
                pool.wait_ge(w_high[s], f + 1)
                nc.gpsimd.tensor_tensor(w_lo[:, s], raw[:, s], w_hi[:, s].bitcast(F32), ALU.subtract).then_inc(split[s], 1)

            def pads(s, f, before):
                if before:
                    pool.wait_ge(conv[s], f)
                nc.gpsimd.tensor_copy(xp_sample(xp[:, s, :], W, 0, W - 1),
                                      old[:, NF * s + f, :].rearrange("p (b i) -> p b i", b=NB)).then_inc(padded[s], 1)

            def tail(s, f):
                pool.wait_ge(evacuated[s], f + 1)
                nc.gpsimd.tensor_copy(tails[:, s, f, 0:2], xp[:, s, TP:TP + 2])
                nc.gpsimd.tensor_copy(tails[:, s, f, 2:18].rearrange("p (b i) -> p b i", b=NB),
                                      xp_sample(xp[:, s, :], W, TB, 2)).then_inc(tailed[s], 1)

            def body(f, now, before):
                if now:
                    if not before:
                        weights_low(G, 0, False)
                    weights_low(V, f, before)
                if before:
                    pool.wait_ge(d_high, f)
                    nc.gpsimd.tensor_tensor(d_lo[:], d_raw[:], d_hi[:].bitcast(F32), ALU.subtract).then_inc(d_split, 1)
                if now:
                    pads(G, f, before)
                    tail(G, f)
                    if f + 1 < NF:
                        weights_low(G, f + 1, True)
                    pads(V, f, before)
                    tail(V, f)
            cycles(body)

        @block.vector
        def _(dve):
            def taps(s, f):
                dve.wait_ge(tap0[s], f + 1)
                for j in (1, 2):
                    col = V_FC + 2 * NF * j + NF * s + f
                    ins = nc.vector.scalar_tensor_tensor(y[:, s, 0:LY], xp[:, s, j:j + LY], C.vec[:, col:col + 1],
                                                         y[:, s, 0:LY], ALU.mult, ALU.add)
                    if j == 1:
                        ins.then_inc(conv_step, 1)
                        dve.wait_ge(conv_step, 2 * f + s + 1)
                ins.then_inc(conv[s], 1)

            def body(f, now, before):
                if before:
                    taps(V, f - 1)
                    dve.wait_ge(conv[V], f)
                    dve.wait_ge(silued, f)
                    if f >= 2:
                        dve.wait_ge(a_ready, f - 1)
                        dve.wait_ge(a_high, f - 1)
                    nc.vector.tensor_tensor(a[:, 0:TP], y[:, G, 0:TP], y[:, V, 0:TP], ALU.mult)
                    nc.vector.tensor_tensor(seqs(a[:, TP:T]), xp_sample(y[:, G, :], W, 0, TB), xp_sample(y[:, V, :], W, 0, TB),
                                            ALU.mult).then_inc(gated, 1)
                    dve.wait_ge(a_high, f)
                    nc.vector.tensor_tensor(a_lo[:], a[:], a_hi[:].bitcast(F32), ALU.subtract).then_inc(a_ready, 1)
                if now:
                    taps(G, f)
                if before:
                    for n in range(NG):
                        t, half = divmod(n, 2)
                        to = h[:, t, 512 * half:512 * half + 512]
                        dve.wait_ge(down, NG * (f - 1) + n + 1)
                        if f >= 2:
                            dve.wait_ge(added, NG * (f - 2) + n + 1)
                        nc.vector.tensor_tensor(to, to, d_banks[:, n % 2, :], ALU.add).then_inc(added, 1)
            cycles(body)

        turned, copied = ph.sem("f_turned"), ph.sem("f_copied")
        stored, rows_stored = C.y_stored, C.ffn_rows_stored
        end = ph.block()

        @end.sync
        def _(sp):
            for t in range(NT):
                to = O["y_prompt"][0, P * t:P * t + P, :] if t < PT else O["y_sample"].rearrange("b t d -> (b t) d")
                sp.dma_start(to, h[:, t, :]).then_inc(stored, 16)
            sp.wait_ge(stored, 16 * NT)

        @end.tensor
        def _(pe):
            for n in range(2 * NF):
                if n >= 8 and n % 4 == 0:
                    pe.wait_ge(copied, n // 4 - 1)
                ins = nc.tensor.transpose(banks[0:18, (n // 4) % 2, P * (n % 4):P * (n % 4) + P], tails[:, n // NF, n % NF, :],
                                          C.ident[:])
                if n % 4 == 3:
                    ins.then_inc(turned, 1)

        @end.scalar
        def _(act):
            rows = a[0:18, 0:1024].rearrange("p (i c) -> p i c", i=2)
            for m in range(2 * NF // 4):
                act.wait_ge(turned, m + 1)
                if m >= 2:
                    act.wait_ge(rows_stored[m % 2], 32 * (m // 2))
                nc.scalar.activation(rows[:, m % 2, :], banks[0:18, m % 2, :], ACT.Copy).then_inc(copied, 1)
                act.wait_ge(copied, m + 1)
                act.dma_start(O["p_ffn_conv"][0, 0][:, 512 * m:512 * m + 512], rows[0:2, m % 2, :]
                              ).then_inc(rows_stored[m % 2], 16)
                act.dma_start(O["s_ffn_conv"][0].rearrange("b i c -> (b i) c")[:, 512 * m:512 * m + 512],
                              rows[2:18, m % 2, :]).then_inc(rows_stored[m % 2], 16)
            act.wait_ge(rows_stored[0], 32 * 6)
            act.wait_ge(rows_stored[1], 32 * 5)



def program(nc, A, O):
    with ExitStack() as stack:
        C = Ctx(nc, stack)
        C.ident, C.ones, C.pair_ones = (C.sb(n, [P, P]) for n in ("ident", "ones", "pair_ones"))
        C.upto, C.after = C.sb("upto", [P, 2, P]), C.sb("after", [P, 2, P])
        C.level, C.hide = C.sb("level", [P, 6, P]), C.sb("hide", [P, 3, 256])
        C.vec, C.k_gain = C.sb("vec", [P, V_ALL]), C.sb("k_gain", [P, 256])
        C.seq_mask = C.sb("seq_mask", [P, NB])
        C.a_log, C.dt_bias, C.sinks, C.eps = (C.sb(n, [P, 4]) for n in ("a_log", "dt_bias", "sinks", "eps"))
        C.state_stored, C.window_stored, C.memory_stored, C.y_stored = (
            C.sem(f"{n}_stored") for n in ("state", "window", "memory", "y"))
        C.conv_stored, C.ffn_rows_stored = ([C.sem(f"{n}_stored{i}") for i in range(2)] for n in ("conv", "ffn_rows"))
        setup(nc, C, A)
        x_tiles = [A["x_prompt"][0, P * t:P * t + P, :] for t in range(PT)] + [
            A["x_sample"].rearrange("b t d -> (b t) d")]
        ffn_old = C.sb("ffn_old", [P, 2 * NF, 16])
        ffn_states_in(nc, C, A, ffn_old)
        mix = ExitStack()
        C.mixT = mix.enter_context(nc.sbuf_tensor("mixT", [P, KD, T], F32))
        with ExitStack() as first:
            M = {}
            for name, shape in (("qkv", [P, 12, T]), ("swa_q", [P, 2, T]), ("swa_k", [P, 1, T]),
                                ("swa_v", [P, 1, T]), ("gate", [8, T])):
                M[name] = first.enter_context(nc.sbuf_tensor(name, shape, F32))
            with nc.sbuf_tensor("xT", [P, KD, T], F32) as xT:
                M["xT"] = xT
                x_rows = M["qkv"][:].rearrange("p a b -> p (a b)")[:, 0:NT * D].rearrange("p (t d) -> p t d", d=D)
                norm_turn(nc, C, "nx", x_rows, x_tiles, NT, V_MIX, xT)
                in_projection(nc, C, A, O, M)
            for name in ("g", "beta", "up", "tail", "beta_up"):
                M[name] = first.enter_context(nc.sbuf_tensor(f"gate_{name}", [P, NT, HEADS], F32))
            group_norms(nc, C, M)
            gates(nc, C, M)
            delta_net(nc, C, A, O, M)
            gdn_output(nc, C, M)
            window_attention(nc, C, A, O, M)
        h = stack.enter_context(nc.sbuf_tensor("h", [P, NT, D], F32, side="right"))
        row_projection(nc, C, "wo", C.mixT, NT, A["w_o"][0], h, residual=x_tiles)
        with ExitStack() as second:
            qT = second.enter_context(nc.sbuf_tensor("mem_q_t", [P, KD, T], F32))
            hT = C.mixT
            norm_turn(nc, C, "nh", h, [], NT, V_MEM, hT)
            feature_projection(nc, C, "mq", hT, A["w_mq"][0], KD, qT)
            column_norms(nc, C, "qn", [([qT[:, 2 * i, :], qT[:, 2 * i + 1, :]], [qT[:, 2 * i, :], qT[:, 2 * i + 1, :]],
                                        C.ones[:], 1.0 / 256, [C.vec[:, V_MQ + j:V_MQ + j + 1] for j in range(2)])
                                       for i in range(HEADS)])
            kT = second.enter_context(nc.sbuf_tensor("mem_k_t", [P, KD, MEM], F32))
            v = second.enter_context(nc.sbuf_tensor("mem_v", [P, 2, D], F32))
            memory_kv(nc, C, A, O, kT, v)
            memory_attention(nc, C, A, qT, kT, v, hT)
            row_projection(nc, C, "mo", hT, NT, A["w_mo"][0], h)
        mix.close()
        hi, lo = (C.sb(f"h_{n}", [P, KD, T], F32R) for n in ("hi", "lo"))
        norm_turn(nc, C, "nf", h, [], NT, V_FFN, hi, lo)
        ffn(nc, C, A, O, h, hi, lo, ffn_old)


_INS = ["x_prompt", "x_sample", "mem_prompt", "state_gdn", "state_gdn_conv", "cache_swa_k", "cache_swa_v",
        "state_sc_conv", "cache_mem_k", "cache_mem_v", "state_ffn_conv", "norm_mix_g", "w_in", "w_gdn_conv",
        "gdn_a_log", "gdn_dt_bias", "gdn_norm_g", "swa_q_norm_g", "swa_k_norm_g", "swa_sinks", "w_sc_conv", "w_o",
        "norm_mem_g", "mem_in_norm_g", "w_mq", "w_mk", "w_mv", "mem_q_norm_g", "mem_k_norm_g", "w_mo",
        "norm_ffn_g", "w_up", "w_ffn_conv", "w_down"]
_OUTS = [("y_prompt", (1, 1024, 1024)), ("y_sample", (8, 16, 1024)), ("p_gdn", (1, 1, 4, 128, 128)),
         ("p_gdn_conv", (1, 1, 3, 1536)), ("p_swa_k", (1, 1, 128, 2, 64)), ("p_swa_v", (1, 1, 128, 2, 64)),
         ("p_sc_conv", (1, 1, 2, 256)), ("p_mem_k", (1, 1, 256, 4, 256)), ("p_mem_v", (1, 1, 256, 4, 256)),
         ("p_ffn_conv", (1, 1, 2, 5632)), ("s_gdn", (1, 8, 4, 128, 128)), ("s_gdn_conv", (1, 8, 3, 1536)),
         ("s_swa_k", (1, 8, 16, 2, 64)), ("s_swa_v", (1, 8, 16, 2, 64)), ("s_sc_conv", (1, 8, 2, 256)),
         ("s_ffn_conv", (1, 8, 2, 5632))]


def kernel(**inputs):
    import numpy as _np
    import concourse.bacc as _bacc
    from concourse import mybir as _mybir
    from concourse.bass_utils import run_bass_kernel_spmd as _run

    nc = _bacc.Bacc("TRN2", target_bir_lowering=False, num_devices=1)
    arrays, A, O = {}, {}, {}
    for name in _INS:
        a = _np.ascontiguousarray(inputs[name])
        arrays[f"in_{name}"] = a
        A[name] = nc.dram_tensor(f"in_{name}", a.shape, _mybir.dt.from_np(a.dtype), kind="ExternalInput").ap()
    for name, shape in _OUTS:
        O[name] = nc.dram_tensor(f"out_{name}", shape, _mybir.dt.float32, kind="ExternalOutput").ap()
    program(nc, A, O)
    r = _run(nc, [arrays], core_ids=[0])
    return tuple(r.results[0][f"out_{name}"] for name, _ in _OUTS)
```

```python
from contextlib import ExitStack

import concourse.bass as bass
from concourse import mybir

F32 = mybir.dt.float32
F32R = mybir.dt.float32r
ALU = mybir.AluOpType
ACT = mybir.ActivationFunctionType
AX = mybir.AxisListType

P = 128
D = 1024
KD = D // P
TP = 1024
NB, TB = 8, 16
TS = NB * TB
T = TP + TS
NT = T // P
PT = TP // P
NP = 3
TC = T // NP
PP = TP - 2 * TC
HEADS = 4
HW = HEADS * P
CONV_CH = 1536
WIDTH = 3336
EPS = 1e-6
NEG = -1e30
FF = 2816
NF = FF // P
MEM = 256
SWA_HD = 64

V_MIX, V_MEM, V_MIN, V_FFN, V_MQ, V_GN, V_SQ, V_SK, V_GC, V_SC, V_FC = 0, 8, 16, 24, 32, 34, 35, 36, 37, 85, 91
V_ALL = V_FC + 3 * 2 * NF


def xp_len(w):
    return TP + w - 1 + NB * (TB + w - 1)


def xp_sample(buf, w, lo, n):
    s = TB + w - 1
    a = TP + w - 1
    return buf[:, a:a + NB * s].rearrange("p (b s) -> p b s", s=s)[:, :, lo:lo + n]


def seqs(ap):
    return ap.rearrange("p (b s) -> p b s", s=TB)


def heads(ap):
    return ap.rearrange("p (h c) -> p h c", h=HEADS)


def over(ap, n):
    return ap.unsqueeze(2).to_broadcast([ap.shape[0], ap.shape[1], n])


def each(ap, n):
    return ap.unsqueeze(1).to_broadcast([ap.shape[0], n, ap.shape[1]])


class Ctx:

    def __init__(self, nc, stack):
        self.nc, self.stack = nc, stack

    def sb(self, name, shape, dt=F32, side="left"):
        return self.stack.enter_context(self.nc.sbuf_tensor(name, shape, dt, side=side))

    def psum(self, name, shape, dt=F32):
        return self.stack.enter_context(self.nc.psum_tensor(name, shape, dt))

    def sem(self, name):
        return self.stack.enter_context(self.nc.semaphore(name))

    def phase(self):
        return Phase(self.nc)


class Phase(Ctx):

    def __init__(self, nc):
        super().__init__(nc, ExitStack())
        self.open = None
        self.sems = []

    def sem(self, name):
        s = super().sem(name)
        self.sems.append(s)
        return s

    def __enter__(self):
        self.stack.__enter__()
        return self

    def end_block(self):
        if self.open is not None:
            self.open.__exit__(None, None, None)
            self.open = None

    def block(self):
        self.end_block()
        self.open = self.nc.Block()
        return self.open.__enter__()

    def __exit__(self, *a):
        if a[0] is None:
            self.end_block()
            for s in self.sems:
                self.nc.sync.sem_clear(s)
        return self.stack.__exit__(*a)



def setup(nc, C, A):
    with C.phase() as ph:
        rows_a = ph.sb("vec_rows_a", [91, P])
        rows_b = ph.sb("vec_rows_b", [88, P])
        rows_c = ph.sb("vec_rows_c", [44, P])
        blocks = ph.sb("same_block", [P, 7, P])
        tp = ph.psum("vec_cols", [P, 512])
        loaded, masks, turned, copied = (ph.sem(n) for n in ("s0_loaded", "s0_masks", "s0_turned", "s0_copied"))
        pool_step = ph.sem("s0_pool_step")
        ident, ones = C.ident, C.ones
        block = ph.block()

        @block.sync
        def _(sp):
            n = 0
            for col, name, k in ((V_MIX, "norm_mix_g", 8), (V_MEM, "norm_mem_g", 8), (V_MIN, "mem_in_norm_g", 8),
                                 (V_FFN, "norm_ffn_g", 8), (V_MQ, "mem_q_norm_g", 2), (V_GN, "gdn_norm_g", 1)):
                sp.dma_start(rows_a[col:col + k, :], A[name][0].rearrange("(k p) -> k p", p=P)).then_inc(loaded, 16)
                n += 1
            for col, name in ((V_SQ, "swa_q_norm_g"), (V_SK, "swa_k_norm_g")):
                for half in range(2):
                    sp.dma_start(rows_a[col:col + 1, half * 64:half * 64 + 64], A[name]).then_inc(loaded, 16)
                    n += 1
            for i in range(4):
                sp.dma_start(rows_a[V_GC + 12 * i:V_GC + 12 * i + 12, :],
                             A["w_gdn_conv"][0, i].rearrange("(k p) -> k p", p=P)).then_inc(loaded, 16)
                n += 1
            for i in range(3):
                sp.dma_start(rows_a[V_SC + 2 * i:V_SC + 2 * i + 2, :],
                             A["w_sc_conv"][0, i].rearrange("(k p) -> k p", p=P)).then_inc(loaded, 16)
                to = rows_b[44 * i:44 * i + 44, :] if i < 2 else rows_c[:, :]
                sp.dma_start(to, A["w_ffn_conv"][0, i].rearrange("(k p) -> k p", p=P)).then_inc(loaded, 16)
                n += 2
            sp.dma_start(C.k_gain[:], A["mem_k_norm_g"].to_broadcast([P, 256])).then_inc(loaded, 16)
            sp.dma_start(C.a_log[:], A["gdn_a_log"].to_broadcast([P, 4])).then_inc(loaded, 16)
            sp.dma_start(C.dt_bias[:], A["gdn_dt_bias"].to_broadcast([P, 4])).then_inc(loaded, 16)
            sp.dma_start(C.sinks[:], A["swa_sinks"].to_broadcast([P, 4])).then_inc(loaded, 16)
            n += 4
            sp.wait_ge(loaded, 16 * n)
            sp.sem_inc(masks, 1)

        @block.gpsimd
        def _(pool):
            steps = 0

            def step(ins):
                nonlocal steps
                ins.then_inc(pool_step, 1)
                steps += 1
                pool.wait_ge(pool_step, steps)

            step(nc.gpsimd.memset(ones[:], 1.0))
            for k in range(7):
                s = 1 << k
                v = blocks[:, k, :].rearrange("p (b c) -> p b c", c=s)
                one = ones[:].rearrange("p (b c) -> p b c", c=s)
                step(nc.gpsimd.affine_select(out=v, in_=one, compare_op=ALU.is_ge, fill=0.0, base=0,
                                             pattern=[[-s, P // s], [0, s]], channel_multiplier=1))
                step(nc.gpsimd.affine_select(out=v, in_=v, compare_op=ALU.is_ge, fill=0.0, base=s - 1,
                                             pattern=[[s, P // s], [0, s]], channel_multiplier=-1))
            step(nc.gpsimd.tensor_copy(ident[:], blocks[:, 0, :]))
            step(nc.gpsimd.tensor_copy(C.pair_ones[:], blocks[:, 6, :]))
            for kind, k in ((0, 6), (1, 4)):
                step(nc.gpsimd.affine_select(out=C.upto[:, kind, :], in_=blocks[:, k, :], compare_op=ALU.is_ge,
                                             fill=0.0, base=0, pattern=[[1, P]], channel_multiplier=-1))
                step(nc.gpsimd.affine_select(out=C.after[:, kind, :], in_=blocks[:, k, :], compare_op=ALU.is_gt,
                                             fill=0.0, base=0, pattern=[[-1, P]], channel_multiplier=1))
            for k in range(6):
                step(nc.gpsimd.tensor_tensor(C.level[:, k, :], blocks[:, k + 1, :], blocks[:, k, :], ALU.subtract))
                step(nc.gpsimd.affine_select(out=C.level[:, k, :], in_=C.level[:, k, :], compare_op=ALU.is_gt,
                                             fill=0.0, base=0, pattern=[[-1, P]], channel_multiplier=1))
            step(nc.gpsimd.memset(C.hide[:], 0.0))
            for kind in range(2):
                step(nc.gpsimd.memset(C.hide[0:64, kind, 192:256], NEG))
                step(nc.gpsimd.memset(C.hide[64:128, kind, 0:64], NEG))
            step(nc.gpsimd.memset(C.hide[:, 1, 0:128], NEG))
            step(nc.gpsimd.tensor_scalar(C.hide[:, 2, 128:256], blocks[:, 4, :], 1.0, -NEG, ALU.subtract, ALU.mult))
            step(nc.gpsimd.tensor_copy(C.seq_mask[:], blocks[:, 4, :].rearrange("p (b s) -> p b s", s=TB)[:, :, 0]))
            step(nc.gpsimd.memset(C.eps[:], EPS))
            pool.sem_inc(masks, 1)

        @block.tensor
        def _(pe):
            pe.wait_ge(masks, 2)
            nc.tensor.transpose(tp[:, 0:91], rows_a[:], ident[0:91, 0:91])
            nc.tensor.transpose(tp[:, 91:179], rows_b[:], ident[0:88, 0:88])
            nc.tensor.transpose(tp[:, 179:223], rows_c[:], ident[0:44, 0:44]).then_inc(turned, 1)

        @block.vector
        def _(dve):
            dve.wait_ge(turned, 1)
            nc.vector.tensor_copy(C.vec[:], tp[:, 0:V_ALL]).then_inc(copied, 1)
            dve.wait_ge(copied, 1)



def norm_turn(nc, C, tag, src, loads, n_tiles, gain_col, out, out_lo=None, ahead=None):
    with C.phase() as ph:
        group = 3 if n_tiles % 3 == 0 else n_tiles
        ng = n_tiles // group
        W = group * P
        squares = ph.sb(f"{tag}_squares", [P, D])
        sums = ph.sb(f"{tag}_sums", [P, n_tiles])
        root = ph.sb(f"{tag}_root", [P, n_tiles])
        inv = ph.sb(f"{tag}_inv", [P, n_tiles])
        xn = ph.sb(f"{tag}_xn", [P, 2, group, D])
        banks = ph.psum(f"{tag}_banks", [P, 4, 512])
        landed = [ph.sem(f"{tag}_landed{t}") for t in range(len(loads))]
        summed, rooted, inverted, scaled, turned, high, low = (
            ph.sem(f"{tag}_{n}") for n in ("summed", "rooted", "inverted", "scaled", "turned", "high", "low"))
        block = ph.block()

        @block.sync
        def _(sp):
            for t, dram in enumerate(loads):
                sp.dma_start(src[:, t, :], dram).then_inc(landed[t], 16)
            if ahead:
                ahead(sp)

        @block.scalar
        def _(act):
            for t in range(n_tiles):
                if loads:
                    act.wait_ge(landed[t], 16)
                if t:
                    act.wait_ge(summed, t)
                nc.scalar.activation(squares[:], src[:, t, :], ACT.Square, accum_out=sums[:, t:t + 1]).then_inc(summed, 1)
            act.wait_ge(summed, n_tiles)
            nc.scalar.activation(root[:], sums[:], ACT.Sqrt, scale=1.0 / D, bias=C.eps[:, 0:1]).then_inc(rooted, 1)
            for i in range(ng * KD):
                g, k = divmod(i, KD)
                act.wait_ge(turned, i + 1)
                nc.scalar.activation(out[:, k, g * W:g * W + W], banks[:, i % 4, 0:W], ACT.Copy,
                                     scale=C.vec[:, gain_col + k:gain_col + k + 1]).then_inc(high, 1)

        @block.vector
        def _(dve):
            dve.wait_ge(rooted, 1)
            nc.vector.reciprocal(inv[:], root[:]).then_inc(inverted, 1)
            dve.wait_ge(inverted, 1)

            def scale(g):
                if g >= 2:
                    dve.wait_ge(turned, KD * (g - 1))
                for j in range(group):
                    t = g * group + j
                    nc.vector.tensor_scalar(xn[:, g % 2, j, :], src[:, t, :], inv[:, t:t + 1], None,
                                            ALU.mult).then_inc(scaled, 1)
            scale(0)
            for g in range(ng):
                if g + 1 < ng:
                    scale(g + 1)
                if out_lo is not None:
                    for k in range(KD):
                        i = g * KD + k
                        dve.wait_ge(high, i + 1)
                        nc.vector.scalar_tensor_tensor(
                            out_lo[:, k, g * W:g * W + W], banks[:, i % 4, 0:W], C.vec[:, gain_col + k:gain_col + k + 1],
                            out[:, k, g * W:g * W + W].bitcast(F32), ALU.mult, ALU.subtract).then_inc(low, 1)

        @block.tensor
        def _(pe):
            for i in range(ng * KD):
                g, k = divmod(i, KD)
                pe.wait_ge(scaled, group * (g + 1))
                if i >= 4:
                    pe.wait_ge(high if out_lo is None else low, i - 3)
                for j in range(group):
                    ins = nc.tensor.transpose(banks[:, i % 4, j * P:j * P + P], xn[:, g % 2, j, k * P:k * P + P],
                                              C.ident[:])
                ins.then_inc(turned, 1)



def column_tiles():
    z0 = CONV_CH
    ab0 = z0 + 512
    sq0 = ab0 + 8
    sk0, sv0 = sq0 + 256, sq0 + 384
    b0 = sv0 + 128
    c0, h0 = b0 + 256, b0 + 512
    tiles = []
    for i in range(2):
        tiles += [("sc_c", i, [(c0 + P * i, P)]), ("sc_h", i, [(h0 + P * i, P)]), ("sc_b", i, [(b0 + P * i, P)])]
    tiles += [("swa_q", i, [(sq0 + 64 * i, 64), (sq0 + 128 + 64 * i, 64)]) for i in range(2)]
    tiles += [("swa_k", 0, [(sk0, P)]), ("swa_v", 0, [(sv0, P)]), ("gate", 0, [(ab0, 8)])]
    for h in range(HEADS):
        tiles += [("conv", HEADS * j + h, [(512 * j + P * h, P)]) for j in range(3)] + [("z", h, [(z0 + P * h, P)])]
    return tiles


def in_projection(nc, C, A, O, M):
    tiles = column_tiles()
    n_tiles = len(tiles)
    RING = 3
    at = {(kind, i): n for n, (kind, i, _) in enumerate(tiles)}
    by_act = [kind not in ("sc_h", "sc_b") for kind, _, _ in tiles]
    act_count = [sum(by_act[:n + 1]) for n in range(n_tiles)]
    dve_count = [n + 1 - act_count[n] for n in range(n_tiles)]
    convs = [(n, i) for n, (kind, i, _) in enumerate(tiles) if kind == "conv"]
    L4, L3 = xp_len(4), xp_len(3)
    with C.phase() as ph:
        w = ph.sb("w_in_ring", [P, RING, KD, P])
        xp = ph.sb("conv_in", [P, 2, L4])
        y = ph.sb("conv_out", [P, L4])
        sc_c = ph.sb("sc_c", [P, T])
        old_rows = ph.sb("gdn_old_rows", [24, CONV_CH])
        old_sc_rows = ph.sb("sc_old_rows", [16, 256])
        old = ph.sb("gdn_old", [P, 12 * 24 + 2 * 16])
        tail = ph.sb("tail", [P, 2, 27])
        new_s = ph.sb("new_sample_rows", [24, 2, P])
        new_p = ph.sb("new_prompt_rows", [3, 2, P])
        banks = ph.psum("proj_banks", [P, 2 * NP, 512])
        state_in = ph.psum("state_in", [P, 512])
        state_out = ph.psum("state_out", [P, 512])
        w_landed = [ph.sem(f"c_w_landed{r}") for r in range(RING)]
        stored = C.conv_stored
        (rows_landed, projected, act_freed, dve_freed, old_turned, old_copied, padded, conv_step, conv_done,
         silu_done, state_turned, state_saved, sc_done, gathered) = (
            ph.sem(f"c_{n}") for n in (
                "rows_landed", "projected", "act_freed", "dve_freed", "old_turned", "old_copied", "padded",
                "conv_step", "conv_done", "silu_done", "state_turned", "state_saved", "sc_done", "gathered"))
        xT = M["xT"]
        q, mixT = M["qkv"], C.mixT
        dest = {"swa_q": M["swa_q"], "swa_k": M["swa_k"], "swa_v": M["swa_v"]}
        padded_of = {("sc", 0): 0, ("sc", 1): 1, **{("conv", i): 2 + m for m, (_, i) in enumerate(convs)}}
        block = ph.block()

        @block.sync
        def _(sp):
            sp.dma_start(old_rows[:], A["state_gdn_conv"][0].rearrange("b i c -> (b i) c")).then_inc(rows_landed, 16)
            sp.dma_start(old_sc_rows[:], A["state_sc_conv"][0].rearrange("b i c -> (b i) c")).then_inc(rows_landed, 16)
            for n, (kind, i, cols) in enumerate(tiles):
                if n >= RING:
                    sp.wait_ge(projected, NP * (n - RING + 1))
                o = 0
                for c0, width in cols:
                    sp.dma_start(w[:, n % RING, :, o:o + width],
                                 A["w_in"][0].rearrange("(k p) c -> p k c", p=P)[:, :, c0:c0 + width]
                                 ).then_inc(w_landed[n % RING], 16)
                    o += width

        w_count = [16 * sum(len(tiles[m][2]) for m in range(n % RING, n + 1, RING)) for n in range(n_tiles)]

        @block.tensor
        def _(pe):
            pe.wait_ge(rows_landed, 32)
            for i in range(12):
                nc.tensor.transpose(state_in[:, 24 * i:24 * i + 24], old_rows[:, P * i:P * i + P], C.ident[0:24, 0:24])
            for i in range(2):
                ins = nc.tensor.transpose(state_in[:, 288 + 16 * i:304 + 16 * i], old_sc_rows[:, P * i:P * i + P],
                                          C.ident[0:16, 0:16])
            ins.then_inc(old_turned, 1)

            def turn_state(m):
                W = 3 if m < 2 else 4
                pe.wait_ge(gathered, m + 1)
                if m:
                    pe.wait_ge(state_saved, m)
                nc.tensor.transpose(state_out[0:W - 1, 0:P], tail[:, m % 2, 24:24 + W - 1], C.ident[:])
                nc.tensor.transpose(state_out[0:NB * (W - 1), P:2 * P], tail[:, m % 2, 0:NB * (W - 1)],
                                    C.ident[:]).then_inc(state_turned, 1)

            for n, (kind, i, cols) in enumerate(tiles):
                rows = sum(c for _, c in cols)
                pe.wait_ge(w_landed[n % RING], w_count[n])
                if n >= 2:
                    if by_act[n - 2]:
                        pe.wait_ge(act_freed, act_count[n - 2])
                    else:
                        pe.wait_ge(dve_freed, dve_count[n - 2])
                for piece in range(NP):
                    for k in range(KD):
                        ins = nc.tensor.matmul(banks[0:rows, (n % 2) * NP + piece, 0:TC], w[:, n % RING, k, 0:rows],
                                               xT[:, k, piece * TC:piece * TC + TC], start=(k == 0), stop=(k == KD - 1))
                    ins.then_inc(projected, 1)
                if n >= 1 and tiles[n - 1][0] == "sc_h":
                    turn_state(tiles[n - 1][1])
                if n >= 1 and tiles[n - 1][0] == "conv":
                    turn_state(padded_of["conv", tiles[n - 1][1]])

        def pieces(n):
            return [((n % 2) * NP + p, p * TC, TC if p < 2 else PP) for p in range(NP)]

        @block.scalar
        def _(act):
            def silu(m):
                n, i = convs[m]
                act.wait_ge(conv_done, m + 1)
                nc.scalar.activation(q[:, i, 0:TP], y[:, 0:TP], ACT.Silu)
                nc.scalar.activation(seqs(q[:, i, TP:T]), xp_sample(y, 4, 0, TB), ACT.Silu).then_inc(silu_done, 1)

            m = 0
            for n, (kind, i, cols) in enumerate(tiles):
                rows = sum(c for _, c in cols)
                if by_act[n]:
                    for p, (bank, c0, cn) in enumerate(pieces(n)):
                        act.wait_ge(projected, NP * n + p + 1)
                        if kind == "conv":
                            pad = padded_of[kind, i]
                            if p == 0:
                                act.wait_ge(padded, pad + 1)
                            ins = nc.scalar.activation(xp[:, pad % 2, 3 + c0:3 + c0 + cn], banks[:, bank, 0:cn], ACT.Copy)
                            if p == 2:
                                ins = nc.scalar.activation(xp_sample(xp[:, pad % 2, :], 4, 3, TB),
                                                           seqs(banks[:, bank, PP:TC]), ACT.Copy)
                        elif kind == "z":
                            ins = nc.scalar.activation(mixT[:, i, p * TC:p * TC + TC], banks[:, bank, 0:TC], ACT.Silu)
                        else:
                            to = {"sc_c": sc_c[:], "gate": M["gate"][:]}.get(kind)
                            to = dest[kind][:, i, :] if to is None else to
                            if kind == "sc_c" and i:
                                act.wait_ge(dve_freed, dve_count[at["sc_h", 0]])
                            ins = nc.scalar.activation(to[0:rows, p * TC:p * TC + TC], banks[0:rows, bank, 0:TC], ACT.Copy)
                    ins.then_inc(act_freed, 1)
                if n >= 1 and tiles[n - 1][0] == "conv":
                    silu(m)
                    m += 1

        @block.gpsimd
        def _(pool):
            def store_state(m):
                W = 3 if m < 2 else 4
                i = m if m < 2 else convs[m - 2][1]
                to_p, to_s = (O["p_sc_conv"], O["s_sc_conv"]) if m < 2 else (O["p_gdn_conv"], O["s_gdn_conv"])
                pool.wait_ge(state_saved, m + 1)
                pool.dma_start(to_p[0, 0][:, P * i:P * i + P], new_p[0:W - 1, m % 2, :]).then_inc(stored[m % 2], 16)
                pool.dma_start(to_s[0].rearrange("b i c -> (b i) c")[:, P * i:P * i + P],
                               new_s[0:NB * (W - 1), m % 2, :]).then_inc(stored[m % 2], 16)

            for pad in range(14):
                W = 3 if pad < 2 else 4
                buf = xp[:, pad % 2, :]
                if pad == 0:
                    pool.wait_ge(old_copied, 1)
                if pad >= 2:
                    if pad < 4:
                        pool.wait_ge(sc_done, pad - 1)
                    else:
                        pool.wait_ge(conv_done, pad - 3)
                if pad < 2:
                    was = old[:, 288 + 16 * pad:304 + 16 * pad]
                else:
                    i = convs[pad - 2][1]
                    was = old[:, 24 * i:24 * i + 24]
                nc.gpsimd.memset(buf[:, 0:W - 1], 0.0)
                nc.gpsimd.tensor_copy(xp_sample(buf, W, 0, W - 1), was.rearrange("p (b i) -> p b i", b=NB)
                                      ).then_inc(padded, 1)
                if pad >= 2:
                    store_state(pad - 2)
            store_state(12)
            store_state(13)
            for r in range(2):
                pool.wait_ge(stored[r], 32 * 7)

        @block.vector
        def _(dve):
            steps = 0

            def taps(W, pad, vec0, stride):
                nonlocal steps
                L = xp_len(W) - (W - 1)
                buf = xp[:, pad % 2, :]
                for j in range(W):
                    wt = C.vec[:, vec0 + stride * j:vec0 + stride * j + 1]
                    if j == 0:
                        ins = nc.vector.tensor_scalar(y[:, 0:L], buf[:, 0:L], wt, None, ALU.mult)
                    else:
                        dve.wait_ge(conv_step, steps)
                        ins = nc.vector.scalar_tensor_tensor(y[:, 0:L], buf[:, j:j + L], wt, y[:, 0:L],
                                                             ALU.mult, ALU.add)
                    if j < W - 1:
                        ins.then_inc(conv_step, 1)
                        steps += 1
                return ins

            def gather_tail(m):
                W = 3 if m < 2 else 4
                if m >= 2:
                    dve.wait_ge(state_turned, m - 1)
                nc.vector.tensor_copy(tail[:, m % 2, 0:NB * (W - 1)].rearrange("p (b i) -> p b i", b=NB),
                                      xp_sample(xp[:, m % 2, :], W, TB, W - 1))
                nc.vector.tensor_copy(tail[:, m % 2, 24:24 + W - 1], xp[:, m % 2, TP:TP + W - 1]).then_inc(gathered, 1)

            def save_state(m):
                W = 3 if m < 2 else 4
                dve.wait_ge(state_turned, m + 1)
                if m >= 2:
                    dve.wait_ge(stored[m % 2], 32 * (m // 2))
                nc.vector.tensor_copy(new_p[0:W - 1, m % 2, :], state_out[0:W - 1, 0:P])
                nc.vector.tensor_copy(new_s[0:NB * (W - 1), m % 2, :], state_out[0:NB * (W - 1), P:2 * P]
                                      ).then_inc(state_saved, 1)

            dve.wait_ge(old_turned, 1)
            nc.vector.tensor_copy(old[:], state_in[:, 0:320]).then_inc(old_copied, 1)
            for n, (kind, i, cols) in enumerate(tiles):
                if kind == "sc_h":
                    dve.wait_ge(act_freed, act_count[at["sc_c", i]])
                    dve.wait_ge(padded, i + 1)
                    for p, (bank, c0, cn) in enumerate(pieces(n)):
                        dve.wait_ge(projected, NP * n + p + 1)
                        nc.vector.tensor_tensor(xp[:, i, 2 + c0:2 + c0 + cn], banks[:, bank, 0:cn], sc_c[:, c0:c0 + cn],
                                                ALU.mult)
                    nc.vector.tensor_tensor(xp_sample(xp[:, i, :], 3, 2, TB), seqs(banks[:, bank, PP:TC]),
                                            seqs(sc_c[:, TP:T]), ALU.mult).then_inc(dve_freed, 1)
                    dve.wait_ge(dve_freed, dve_count[n])
                    gather_tail(i)
                    taps(3, i, V_SC + i, 2).then_inc(sc_done, 1)
                    dve.wait_ge(sc_done, i + 1)
                elif kind == "sc_b":
                    save_state(i)
                    for p, (bank, c0, cn) in enumerate(pieces(n)):
                        dve.wait_ge(projected, NP * n + p + 1)
                        nc.vector.tensor_tensor(mixT[:, 6 + i, c0:c0 + cn], banks[:, bank, 0:cn], y[:, c0:c0 + cn], ALU.mult)
                    nc.vector.tensor_tensor(seqs(mixT[:, 6 + i, TP:T]), seqs(banks[:, bank, PP:TC]),
                                            xp_sample(y, 3, 0, TB), ALU.mult).then_inc(dve_freed, 1)
                    dve.wait_ge(dve_freed, dve_count[n])
                elif kind == "conv":
                    pad = padded_of[kind, i]
                    dve.wait_ge(act_freed, act_count[n])
                    if pad >= 3:
                        dve.wait_ge(silu_done, pad - 2)
                    gather_tail(pad)
                    taps(4, pad, V_GC + i, 12).then_inc(conv_done, 1)
                    save_state(pad)



def column_norms(nc, C, tag, items):
    RING, BATCH = 4, 6
    n_items = len(items)
    with C.phase() as ph:
        squares = ph.sb(f"{tag}_squares", [P, RING, T])
        logs = ph.sb(f"{tag}_logs", [P, 2 * BATCH, T])
        banks = ph.psum(f"{tag}_sums", [P, 2 * NP, 512])
        squared_pool, squared_dve, summed, logged, rooted, normed = (ph.sem(f"{tag}_{n}") for n in (
            "squared_pool", "squared_dve", "summed", "logged", "rooted", "normed"))
        squares_of = [(m, j) for m, it in enumerate(items) for j in range(len(it[0]))]
        through = [sum(len(it[0]) for it in items[:m + 1]) for m in range(n_items)]
        by_pool = [n % 3 == 0 for n in range(len(squares_of))]

        def square(engine, wait, n, done):
            m, j = squares_of[n]
            if n >= RING:
                wait.wait_ge(summed, n - RING + 1)
            x = items[m][0][j]
            engine.tensor_tensor(squares[:, n % RING, :], x, x, ALU.mult).then_inc(done, 1)

        block = ph.block()

        @block.gpsimd
        def _(pool):
            for n, mine in enumerate(by_pool):
                if mine:
                    square(nc.gpsimd, pool, n, squared_pool)

        @block.tensor
        def _(pe):
            for n, (m, j) in enumerate(squares_of):
                if by_pool[n]:
                    pe.wait_ge(squared_pool, sum(by_pool[:n + 1]))
                else:
                    pe.wait_ge(squared_dve, n + 1 - sum(by_pool[:n + 1]))
                if j == 0 and m >= 2:
                    pe.wait_ge(logged, m - 1)
                for p in range(NP):
                    ins = nc.tensor.matmul(banks[:, (m % 2) * NP + p, 0:TC], items[m][2],
                                           squares[:, n % RING, p * TC:p * TC + TC], start=(j == 0),
                                           stop=(j == len(items[m][0]) - 1), skip_group_check=True)
                ins.then_inc(summed, 1)

        @block.scalar
        def _(act):
            for m0 in range(0, n_items, BATCH):
                batch = range(m0, min(m0 + BATCH, n_items))
                for m in batch:
                    act.wait_ge(summed, through[m])
                    if m >= 2 * BATCH:
                        act.wait_ge(normed, through[m - 2 * BATCH])
                    for p in range(NP):
                        ins = nc.scalar.activation(logs[:, m % (2 * BATCH), p * TC:p * TC + TC],
                                                   banks[:, (m % 2) * NP + p, 0:TC], ACT.Ln, scale=items[m][3],
                                                   bias=C.eps[:, 0:1])
                    ins.then_inc(logged, 1)
                for m in batch:
                    act.wait_ge(logged, m + 1)
                    at = logs[:, m % (2 * BATCH), :]
                    nc.scalar.activation(at, at, ACT.Exp, scale=-0.5).then_inc(rooted, 1)

        @block.vector
        def _(dve):
            def squares_through(m):
                nonlocal done
                for n in range(done, through[min(m, n_items - 1)]):
                    if not by_pool[n]:
                        square(nc.vector, dve, n, squared_dve)
                done = max(done, through[min(m, n_items - 1)])

            done = 0
            for m0 in range(0, n_items, BATCH):
                squares_through(m0 + BATCH - 1)
                for m in range(m0, min(m0 + BATCH, n_items)):
                    squares_through(m + 4)
                    dve.wait_ge(rooted, m + 1)
                    for j, (x, out) in enumerate(zip(items[m][0], items[m][1])):
                        ins = nc.vector.scalar_tensor_tensor(out, x, items[m][4][j], logs[:, m % (2 * BATCH), :],
                                                             ALU.mult, ALU.mult)
                        ins.then_inc(normed, 1)


def group_norms(nc, C, M):
    qkv, sq, sk = M["qkv"], M["swa_q"], M["swa_k"]
    items = [([qkv[:, h, :]], [qkv[:, h, :]], C.ones[:], 1.0, [float(P) ** -0.5]) for h in range(HEADS)]
    items += [([qkv[:, 4 + h, :]], [qkv[:, 4 + h, :]], C.ones[:], 1.0, [1.0]) for h in range(HEADS)]
    items += [([x], [x], C.pair_ones[:], 1.0 / SWA_HD, [C.vec[:, v:v + 1]])
              for x, v in ((sq[:, 0, :], V_SQ), (sq[:, 1, :], V_SQ), (sk[:, 0, :], V_SK))]
    column_norms(nc, C, "gn", items)



def gates(nc, C, M):
    with C.phase() as ph:
        raw, pos, neg, e, l = (ph.sb(f"gate_{n}", [P, NT, HEADS]) for n in ("raw", "pos", "neg", "e", "l"))
        eb = ph.sb("gate_eb", [P, NT, HEADS])
        rate = ph.sb("gate_rate", [P, HEADS])
        ps = ph.psum("gate_rows", [P, NT, 8])
        sums = ph.psum("gate_sums", [P, 2, NT, HEADS])
        turned, act_step, dve_step, summed = (ph.sem(f"g_{n}") for n in ("turned", "act_step", "dve_step", "summed"))
        g, beta, up, tail, bu = (M[n] for n in ("g", "beta", "up", "tail", "beta_up"))
        block = ph.block()

        @block.tensor
        def _(pe):
            for t in range(NT):
                ins = nc.tensor.transpose(ps[:, t, :], M["gate"][:, P * t:P * t + P], C.ident[0:8, 0:8])
            ins.then_inc(turned, 1)
            pe.wait_ge(dve_step, 6)
            for kind, a, b in ((0, 0, PT), (1, PT, NT)):
                nc.tensor.matmul(sums[:, 0, a:b, :], C.upto[:, kind, :], g[:, a:b, :], start=True, stop=True)
                ins = nc.tensor.matmul(sums[:, 1, a:b, :], C.after[:, kind, :], g[:, a:b, :], start=True, stop=True)
            ins.then_inc(summed, 1)

        @block.scalar
        def _(act):
            act.wait_ge(dve_step, 1)
            nc.scalar.activation(neg[:], raw[:], ACT.Abs).then_inc(act_step, 1)
            act.wait_ge(act_step, 1)
            nc.scalar.activation(e[:], neg[:], ACT.Exp, scale=-1.0).then_inc(act_step, 1)
            nc.scalar.activation(eb[:], ps[:, :, 4:8], ACT.Exp, scale=-1.0).then_inc(act_step, 1)
            nc.scalar.activation(rate[:], C.a_log[:], ACT.Exp).then_inc(act_step, 1)
            act.wait_ge(act_step, 2)
            nc.scalar.activation(l[:], e[:], ACT.Ln, bias=C.ones[:, 0:1]).then_inc(act_step, 1)
            act.wait_ge(summed, 1)
            nc.scalar.activation(up[:], sums[:, 0], ACT.Exp).then_inc(act_step, 1)
            nc.scalar.activation(tail[:], sums[:, 1], ACT.Exp).then_inc(act_step, 1)
            act.wait_ge(act_step, 7)

        @block.vector
        def _(dve):
            dve.wait_ge(turned, 1)
            nc.vector.tensor_tensor(raw[:], ps[:, :, 0:4], each(C.dt_bias[:], NT), ALU.add).then_inc(dve_step, 1)
            dve.wait_ge(dve_step, 1)
            nc.vector.tensor_scalar(pos[:], raw[:], 0.0, None, ALU.max).then_inc(dve_step, 1)
            dve.wait_ge(act_step, 3)
            nc.vector.tensor_scalar(eb[:], eb[:], 1.0, None, ALU.add).then_inc(dve_step, 1)
            dve.wait_ge(dve_step, 3)
            nc.vector.reciprocal(beta[:], eb[:]).then_inc(dve_step, 1)
            dve.wait_ge(act_step, 5)
            nc.vector.tensor_tensor(pos[:], pos[:], l[:], ALU.add).then_inc(dve_step, 1)
            dve.wait_ge(dve_step, 5)
            nc.vector.scalar_tensor_tensor(g[:], pos[:], -1.0, each(rate[:], NT), ALU.mult, ALU.mult
                                           ).then_inc(dve_step, 1)
            dve.wait_ge(act_step, 6)
            nc.vector.tensor_tensor(bu[:], beta[:], up[:], ALU.mult).then_inc(dve_step, 1)
            dve.wait_ge(dve_step, 7)



def delta_net(nc, C, A, O, M):
    qkv, g, beta, tail, bu = M["qkv"], M["g"], M["beta"], M["tail"], M["beta_up"]
    LEVELS = 6
    UPD = 2 * LEVELS - 1
    STEPS = (("p", 0), ("w", 0), ("p", 1), ("r", 0), ("p", 2), ("w", 1), ("p", 3), ("r", 1),
             ("p", 4), ("p", 5), ("p", 6), ("p", 7), ("p", 8))
    N = 2 * PT

    with C.phase() as ph:
        G = ph.sb("decay_steps", [P, HEADS, P])
        dec, decT = ph.sb("decay", [P, HEADS, P]), ph.sb("decay_t", [P, HEADS, P])
        E = ph.sb("decay_up", [P, 2, HEADS, P])
        low = ph.sb("low", [P, HEADS, P])
        pair = ph.sb("low_pairs", [P, 2, HEADS, P])
        X, XT, ZT = (ph.sb(n, [P, HEADS, P]) for n in ("inv", "inv_t", "inv_low_t"))
        rk, rv = ph.sb("rhs_k", [P, HEADS, P]), ph.sb("rhs_v", [P, HEADS, P])
        kd, qk, qg, u0, wT = (ph.sb(n, [P, 2, HEADS, P]) for n in ("k_tail", "qk_t", "q_up", "u0", "w_t"))
        S, Sg, u = (ph.sb(n, [P, HEADS, P]) for n in ("state", "state_decayed", "u"))
        S0 = ph.sb("sample_state", [P, NB, HEADS, P])
        kdm = ph.sb("k_tail_one", [P, 2, HEADS, P])
        wsT = ph.sb("w_state_t", [P, HEADS, P])
        bank = {n: ph.psum(f"gdn_bank_{n}", [P, HEADS, P]) for n in ("a", "b", "c", "d", "e", "u", "o", "s")}
        (g_ready, sums_done, exp_done, products, low_done, low_scaled, qk_raw, qk_done, qg_done, rhs_done, masked, upd,
         z_done, z_copied, xx_done, xt_done, solved, solved_copied, zeroed, sg_done, ws_done, u_done, os_done,
         s_product, o_copied, s_done, wst_copied, wst_turned, kdm_done, sample_product, sample_decayed,
         sample_done, s0_landed) = (ph.sem(f"d_{n}") for n in (
             "g_ready", "sums_done", "exp_done", "products", "low_done", "low_scaled", "qk_raw", "qk_done", "qg_done",
             "rhs_done", "masked", "upd", "z_done", "z_copied", "xx_done", "xt_done", "solved", "solved_copied",
             "zeroed", "sg_done", "ws_done", "u_done", "os_done", "s_product", "o_copied", "s_done", "wst_copied",
             "wst_turned", "kdm_done", "sample_product", "sample_decayed", "sample_done", "s0_landed"))
        stored = C.state_stored

        def cols(t):
            return slice(P * t, P * t + P)

        def run(prep, scan, sample):
            for t in range(NT):
                for what, s in STEPS:
                    if what == "p":
                        prep(t, s)
                    elif t >= 1:
                        scan(t - 1, s, what)
            sample(NT - 1)

        block = ph.block()

        @block.sync
        def _(sp):
            for b in range(NB):
                sp.dma_start(S0[:, b], A["state_gdn"][0, b].rearrange("h k v -> k h v")).then_inc(s0_landed, 16)
            sp.wait_ge(s_done, N)
            sp.dma_start(O["p_gdn"][0, 0].rearrange("h k v -> k h v"), S[:]).then_inc(stored, 16)
            for b in range(NB):
                sp.wait_ge(sample_done, b + 1)
                sp.dma_start(O["s_gdn"][0, b].rearrange("h k v -> k h v"), S0[:, b]).then_inc(stored, 16)
            sp.wait_ge(stored, 16 * (NB + 1))

        @block.tensor
        def _(pe):
            def prep(t, s):
                kind = t // PT
                if s == 0:
                    pe.wait_ge(g_ready, t + 1)
                    if t:
                        pe.wait_ge(upd, UPD * t)
                    for h in range(HEADS):
                        nc.tensor.matmul(bank["a"][:, h, :], G[:, h, :], C.after[:, kind, :], start=True, stop=True)
                    nc.tensor.matmul(bank["b"][:], C.after[:, kind, :], G[:], start=True, stop=True)
                    nc.tensor.matmul(bank["c"][:], C.ones[:], G[:], start=True, stop=True).then_inc(sums_done, 1)
                elif s == 1:
                    if t:
                        pe.wait_ge(solved_copied, 2 * t)
                    for h in range(HEADS):
                        k = qkv[:, 4 + h, cols(t)]
                        nc.tensor.matmul(bank["d"][:, h, :], k, k, start=True, stop=True)
                    for h in range(HEADS):
                        ins = nc.tensor.matmul(bank["e"][:, h, :], qkv[:, 4 + h, cols(t)], qkv[:, h, cols(t)],
                                               start=True, stop=True)
                    ins.then_inc(products, 1)
                    pe.wait_ge(exp_done, 3 * t + 3)
                    for h in range(HEADS):
                        nc.tensor.transpose(bank["a"][:, h, :], qkv[:, 4 + h, cols(t)], C.ident[:])
                    for h in range(HEADS):
                        ins = nc.tensor.transpose(bank["b"][:, h, :], qkv[:, 8 + h, cols(t)], C.ident[:])
                    ins.then_inc(products, 1)
                elif s == 2:
                    pe.wait_ge(masked, LEVELS * t + 1)
                    for h in range(HEADS):
                        ins = nc.tensor.transpose(bank["c"][:, h, :], pair[:, 0, h, :], C.ident[:])
                    ins.then_inc(z_done, 1)
                elif s < 2 + LEVELS:
                    k = s - 2
                    pe.wait_ge(masked, LEVELS * t + k + 1)
                    pe.wait_ge(upd, UPD * t + 2 * k)
                    if k == 1:
                        pe.wait_ge(rhs_done, t + 1)
                    for h in range(HEADS):
                        ins = nc.tensor.matmul(bank["a"][:, h, :], pair[:, k % 2, h, :], XT[:, h, :],
                                               start=True, stop=True)
                    ins.then_inc(z_done, 1)
                    pe.wait_ge(z_copied, (LEVELS - 1) * t + k)
                    for h in range(HEADS):
                        ins = nc.tensor.matmul(bank["b"][:, h, :], X[:, h, :], ZT[:, h, :], start=True, stop=True)
                    ins.then_inc(xt_done, 1)
                    if k < LEVELS - 1:
                        for h in range(HEADS):
                            ins = nc.tensor.matmul(bank["c"][:, h, :], ZT[:, h, :], X[:, h, :], start=True, stop=True)
                        ins.then_inc(xx_done, 1)
                else:
                    pe.wait_ge(upd, UPD * (t + 1))
                    pe.wait_ge(qk_raw, t + 1)
                    for h in range(HEADS):
                        ins = nc.tensor.matmul(bank["d"][:, h, :], XT[:, h, :], rv[:, h, :], start=True, stop=True)
                    ins.then_inc(solved, 1)
                    for h in range(HEADS):
                        ins = nc.tensor.matmul(bank["e"][:, h, :], rk[:, h, :], XT[:, h, :], start=True, stop=True)
                    ins.then_inc(solved, 1)

            def scan(t, c, what):
                n = 2 * t + c
                r, i = slice(64 * c, 64 * c + 64), t % 2
                if what == "w":
                    pe.wait_ge(solved_copied, 2 * t + 2)
                    if n:
                        pe.wait_ge(s_done, n)
                    else:
                        pe.wait_ge(zeroed, 2)
                    for h in range(HEADS):
                        ins = nc.tensor.matmul(bank["u"][r, h, :], wT[:, i, h, r], S[:, h, :], start=True, stop=True)
                    ins.then_inc(ws_done, 1)
                else:
                    pe.wait_ge(u_done, n + 1)
                    pe.wait_ge(qk_done, t + 1)
                    pe.wait_ge(qg_done, t + 1)
                    if n:
                        pe.wait_ge(o_copied, n)
                    for h in range(HEADS):
                        nc.tensor.matmul(bank["o"][:, h, 0:64], S[:, h, :], qg[:, i, h, r], start=True, stop=False)
                        ins = nc.tensor.matmul(bank["o"][:, h, 0:64], u[:, h, :], qk[:, i, h, r], start=False, stop=True)
                    ins.then_inc(os_done, 1)
                    for h in range(HEADS):
                        ins = nc.tensor.matmul(bank["s"][:, h, :], kd[r, i, h, :], u[r, h, :], start=True, stop=True)
                    ins.then_inc(s_product, 1)

            def sample(t):
                i = t % 2
                pe.wait_ge(solved_copied, 2 * t + 2)
                pe.wait_ge(s0_landed, 16 * NB)
                pe.wait_ge(s_done, N)
                for h in range(HEADS):
                    for b in range(NB):
                        ins = nc.tensor.matmul(bank["u"][:, h, TB * b:TB * b + TB], S0[:, b, h, :],
                                               wT[:, i, h, TB * b:TB * b + TB], start=True, stop=True)
                ins.then_inc(ws_done, 1)
                pe.wait_ge(qg_done, t + 1)
                pe.wait_ge(o_copied, N)
                for h in range(HEADS):
                    for b in range(NB):
                        nc.tensor.matmul(bank["o"][:, h, TB * b:TB * b + TB], S0[:, b, h, :],
                                         qg[:, i, h, TB * b:TB * b + TB], start=(h + b == 0), stop=False,
                                         skip_group_check=True)
                pe.wait_ge(wst_copied, 1)
                for h in range(HEADS):
                    ins = nc.tensor.transpose(bank["s"][:, h, :], wsT[:, h, :], C.ident[:])
                ins.then_inc(wst_turned, 1)
                pe.wait_ge(u_done, N + 1)
                pe.wait_ge(qk_done, t + 1)
                for h in range(HEADS):
                    ins = nc.tensor.matmul(bank["o"][:, h, :], u[:, h, :], qk[:, i, h, :], start=False, stop=True,
                                           skip_group_check=True)
                ins.then_inc(os_done, 1)
                for b in range(NB):
                    pe.wait_ge(kdm_done, b + 1)
                    if b >= 2:
                        pe.wait_ge(sample_done, b - 1)
                    for h in range(HEADS):
                        ins = nc.tensor.matmul(bank["de"[b % 2]][:, h, :], kdm[:, b % 2, h, :], u[:, h, :],
                                               start=True, stop=True)
                    ins.then_inc(sample_product, 1)

            run(prep, scan, sample)

        @block.scalar
        def _(act):
            def prep(t, s):
                if s == 0:
                    act.wait_ge(sums_done, t + 1)
                    if t:
                        act.wait_ge(low_done, t)
                        act.wait_ge(qk_raw, t)
                    if t >= 2:
                        act.wait_ge(s_done, 2 * t - 2)
                    nc.scalar.activation(dec[:], bank["a"][:], ACT.Exp).then_inc(exp_done, 1)
                    nc.scalar.activation(decT[:], bank["b"][:], ACT.Exp).then_inc(exp_done, 1)
                    nc.scalar.activation(E[:, t % 2], bank["c"][:], ACT.Exp).then_inc(exp_done, 1)
                elif 3 <= s < 2 + LEVELS:
                    act.wait_ge(z_done, LEVELS * t + s - 1)
                    nc.scalar.activation(ZT[:], bank["a"][:], ACT.Copy).then_inc(z_copied, 1)
                elif s == 8:
                    for j, (to, b) in enumerate(((u0, "d"), (wT, "e"))):
                        act.wait_ge(solved, 2 * t + j + 1)
                        nc.scalar.activation(to[:, t % 2], bank[b][:], ACT.Copy).then_inc(solved_copied, 1)

            def scan(t, c, what):
                if what == "r":
                    act.wait_ge(os_done, 2 * t + c + 1)
                    nc.scalar.activation(qkv[:, 8:12, P * t + 64 * c:P * t + 64 * c + 64], bank["o"][:, :, 0:64],
                                         ACT.Copy).then_inc(o_copied, 1)

            def sample(t):
                act.wait_ge(ws_done, N + 1)
                nc.scalar.activation(wsT[:], bank["u"][:], ACT.Copy).then_inc(wst_copied, 1)
                act.wait_ge(os_done, N + 1)
                nc.scalar.activation(qkv[:, 8:12, cols(t)], bank["o"][:], ACT.Copy).then_inc(o_copied, 1)
                for b in range(NB):
                    if b >= 2:
                        act.wait_ge(sample_product, b - 1)
                    nc.scalar.activation(kdm[:, b % 2], kd[:, t % 2], ACT.Copy, scale=C.seq_mask[:, b:b + 1]
                                         ).then_inc(kdm_done, 1)

            run(prep, scan, sample)

        @block.gpsimd
        def _(pool):
            def mask(t, k):
                if k >= 2:
                    pool.wait_ge(z_done, LEVELS * t + k - 1)
                if k == 2:
                    pool.wait_ge(upd, UPD * t + 1)
                if t == PT and k >= 4:
                    ins = nc.gpsimd.memset(pair[:, k % 2], 0.0)
                else:
                    ins = nc.gpsimd.tensor_tensor(pair[:, k % 2], low[:], each(C.level[:, k, :], HEADS), ALU.mult)
                ins.then_inc(masked, 1)

            def prep(t, s):
                if s == 1:
                    pool.wait_ge(low_done, t + 1)
                    nc.gpsimd.tensor_tensor(low[:], low[:], over(beta[:, t, :], P), ALU.mult).then_inc(low_scaled, 1)
                    pool.wait_ge(low_scaled, t + 1)
                    if t:
                        pool.wait_ge(z_done, LEVELS * t)
                    mask(t, 0)
                    mask(t, 1)
                    pool.wait_ge(qk_raw, t + 1)
                    nc.gpsimd.tensor_tensor(qk[:, t % 2], qk[:, t % 2], each(C.upto[:, t // PT, :], HEADS), ALU.mult
                                            ).then_inc(qk_done, 1)
                    pool.wait_ge(exp_done, 3 * t + 3)
                    nc.gpsimd.tensor_tensor(qg[:, t % 2], qkv[:, 0:4, cols(t)], E[:, t % 2], ALU.mult
                                            ).then_inc(qg_done, 1)
                elif 3 <= s < 1 + LEVELS:
                    mask(t, s - 1)

            def scan(t, c, what):
                n = 2 * t + c
                if what == "w":
                    if n:
                        pool.wait_ge(s_done, n)
                    else:
                        pool.wait_ge(zeroed, 2)
                    last = 64 * c + 63
                    nc.gpsimd.tensor_tensor(Sg[:], S[:], E[:, t % 2, :, last:last + 1].to_broadcast([P, HEADS, P]),
                                            ALU.mult).then_inc(sg_done, 1)

            def sample(t):
                pool.wait_ge(os_done, N + 1)
                pool.wait_ge(s0_landed, 16 * NB)
                for b in range(NB):
                    last = TB * b + TB - 1
                    nc.gpsimd.tensor_tensor(S0[:, b], S0[:, b],
                                            E[:, t % 2, :, last:last + 1].to_broadcast([P, HEADS, P]), ALU.mult
                                            ).then_inc(sample_decayed, 1)

            run(prep, scan, sample)

        @block.vector
        def _(dve):
            def decay_steps(t):
                nc.vector.tensor_tensor(G[:], each(C.upto[:, t // PT, :], HEADS), over(g[:, t, :], P), ALU.mult
                                        ).then_inc(g_ready, 1)

            def prep(t, s):
                i = t % 2
                if s == 0 and t == 0:
                    nc.vector.memset(S[:], 0.0).then_inc(zeroed, 1)
                    nc.vector.memset(u[:], 0.0).then_inc(zeroed, 1)
                    decay_steps(0)
                elif s == 1:
                    dve.wait_ge(exp_done, 3 * t + 3)
                    dve.wait_ge(products, 2 * t + 1)
                    if t:
                        dve.wait_ge(masked, LEVELS * t)
                    nc.vector.tensor_tensor(low[:], bank["d"][:], dec[:], ALU.mult).then_inc(low_done, 1)
                    if t >= 2:
                        dve.wait_ge(s_done, 2 * t - 2)
                    nc.vector.tensor_tensor(qk[:, i], bank["e"][:], decT[:], ALU.mult).then_inc(qk_raw, 1)
                    dve.wait_ge(products, 2 * t + 2)
                    if t:
                        dve.wait_ge(solved, 2 * t)
                    nc.vector.tensor_tensor(rk[:], bank["a"][:], over(bu[:, t, :], P), ALU.mult)
                    nc.vector.tensor_tensor(rv[:], bank["b"][:], over(beta[:, t, :], P), ALU.mult)
                    nc.vector.tensor_tensor(kd[:, i], bank["a"][:], over(tail[:, t, :], P), ALU.mult
                                            ).then_inc(rhs_done, 1)
                elif s == 2:
                    if t:
                        dve.wait_ge(solved, 2 * t)
                    dve.wait_ge(masked, LEVELS * t + 1)
                    nc.vector.tensor_tensor(X[:], each(C.ident[:], HEADS), pair[:, 0], ALU.subtract).then_inc(upd, 1)
                    dve.wait_ge(z_done, LEVELS * t + 1)
                    nc.vector.tensor_tensor(XT[:], each(C.ident[:], HEADS), bank["c"][:], ALU.subtract).then_inc(upd, 1)
                elif 3 <= s < 2 + LEVELS:
                    k = s - 2
                    dve.wait_ge(xt_done, (LEVELS - 1) * t + k)
                    dve.wait_ge(upd, UPD * t + 2 * k)
                    nc.vector.tensor_tensor(XT[:], XT[:], bank["b"][:], ALU.subtract).then_inc(upd, 1)
                    if k < LEVELS - 1:
                        dve.wait_ge(xx_done, (LEVELS - 2) * t + k)
                        nc.vector.tensor_tensor(X[:], X[:], bank["c"][:], ALU.subtract).then_inc(upd, 1)
                elif s == 8:
                    if t + 1 < NT:
                        dve.wait_ge(sums_done, t + 1)
                        decay_steps(t + 1)

            def scan(t, c, what):
                n = 2 * t + c
                r = slice(64 * c, 64 * c + 64)
                if what == "w":
                    dve.wait_ge(ws_done, n + 1)
                    dve.wait_ge(solved_copied, 2 * t + 2)
                    if n:
                        dve.wait_ge(s_done, n)
                    else:
                        dve.wait_ge(zeroed, 2)
                    nc.vector.tensor_tensor(u[r], u0[r, t % 2], bank["u"][r], ALU.subtract).then_inc(u_done, 1)
                else:
                    dve.wait_ge(s_product, n + 1)
                    dve.wait_ge(sg_done, n + 1)
                    nc.vector.tensor_tensor(S[:], Sg[:], bank["s"][:], ALU.add).then_inc(s_done, 1)

            def sample(t):
                dve.wait_ge(wst_turned, 1)
                dve.wait_ge(solved_copied, 2 * t + 2)
                nc.vector.tensor_tensor(u[:], u0[:, t % 2], bank["s"][:], ALU.subtract).then_inc(u_done, 1)
                for b in range(NB):
                    dve.wait_ge(sample_product, b + 1)
                    dve.wait_ge(sample_decayed, b + 1)
                    nc.vector.tensor_tensor(S0[:, b], S0[:, b], bank["de"[b % 2]][:], ALU.add).then_inc(sample_done, 1)

            run(prep, scan, sample)


def gdn_output(nc, C, M):
    o = M["qkv"]
    items = [([o[:, 8 + h, :]], [o[:, 8 + h, :]], C.ones[:], 1.0 / P, [C.vec[:, V_GN:V_GN + 1]]) for h in range(HEADS)]
    column_norms(nc, C, "go", items)
    with C.phase() as ph:
        gated = ph.sem("go_gated")
        block = ph.block()

        @block.vector
        def _(dve):
            for h in range(2):
                nc.vector.tensor_tensor(C.mixT[:, h, :], C.mixT[:, h, :], o[:, 8 + h, :], ALU.mult).then_inc(gated, 1)
            dve.wait_ge(gated, 4)

        @block.gpsimd
        def _(pool):
            for h in range(2, HEADS):
                nc.gpsimd.tensor_tensor(C.mixT[:, h, :], C.mixT[:, h, :], o[:, 8 + h, :], ALU.mult).then_inc(gated, 1)



def attention(nc, C, tag, scale, hide, sinks, scores, sample_scores, values, dest, loads=None, buffers=None,
              early=None, sample_copies=None):
    slots, turned_parts, new_scores, finish_scores = sample_scores
    with C.phase() as ph:
        p = ph.sb(f"{tag}_p", [P, 2, HEADS, 256])
        pT = ph.sb(f"{tag}_pt", [P, 2, 8, P])
        mx, nm, den, rec, es = (ph.sb(f"{tag}_{n}", [P, 2, HEADS]) for n in ("mx", "nm", "den", "rec", "es"))
        B = buffers(ph) if buffers else {}
        s_bank = ph.psum(f"{tag}_scores", [P, 2, HEADS, 256])
        t_bank = ph.psum(f"{tag}_turned", [P, 8, P])
        o_bank = ph.psum(f"{tag}_out", [P, 8, P])
        names = ("scored", "hidden", "maxed", "max_step", "exp_done", "summed", "normed", "turned", "turned_copied",
                 "valued", "out_copied", "early", "sample_scored", "sample_copied")
        s = {n: ph.sem(f"{tag}_{n}") for n in names}
        block = ph.block()
        act_exps = HEADS + (1 if sinks is not None else 0)
        max_steps = 4 if sinks is not None else 2
        last = NT - 1

        @block.sync
        def _(sp):
            if loads:
                loads(sp, B, s)

        @block.tensor
        def _(pe):
            if early:
                early["pe"](pe, B, s, t_bank, o_bank)

            def score(t):
                if t >= 2:
                    pe.wait_ge(s["hidden"] if hide else s["exp_done"], t - 1 if hide else act_exps * (t - 1))
                if t < last:
                    scores(pe, t, s_bank[:, t % 2]).then_inc(s["scored"], 1)
                    return
                pe.wait_ge(s["out_copied"], last)
                pe.wait_ge(s["turned_copied"], last)
                turned_parts(pe, B, s, t_bank, o_bank)
                pe.wait_ge(s["sample_copied"], 1)
                for slot, h, half in slots:
                    ins = nc.tensor.transpose(s_bank[:, t % 2, h, P * half:P * half + P], pT[:, 1 - (last - 1) % 2, slot, :],
                                              C.ident[:])
                if new_scores:
                    ins = new_scores(pe, s_bank[:, t % 2])
                ins.then_inc(s["scored"], 1)

            def turn(t):
                pe.wait_ge(s["normed"], t + 1)
                if t:
                    pe.wait_ge(s["turned_copied"], t)
                for half in range(2):
                    for h in range(HEADS):
                        ins = nc.tensor.transpose(t_bank[:, 4 * half + h, :], p[:, t % 2, h, P * half:P * half + P],
                                                  C.ident[:])
                ins.then_inc(s["turned"], 1)

            def output(t):
                pe.wait_ge(s["turned_copied"], t + 1)
                if t:
                    pe.wait_ge(s["out_copied"], t)
                values(pe, t, pT[:, t % 2], o_bank, B, s).then_inc(s["valued"], 1)

            score(0)
            score(1)
            for t in range(last):
                turn(t)
                if t + 2 < last:
                    score(t + 2)
                output(t)
            score(last)
            turn(last)
            output(last)

        def output_copy(dve, t):
            dve.wait_ge(s["valued"], t + 1)
            to, frm = dest(t, o_bank)
            nc.vector.tensor_copy(to, frm).then_inc(s["out_copied"], 1)

        @block.vector
        def _(dve):
            if early and "dve" in early:
                early["dve"](dve, B, s, t_bank, o_bank)
            def maxima(t):
                i = t % 2
                dve.wait_ge(s["scored"], t + 1)
                if t >= 2:
                    dve.wait_ge(s["exp_done"], act_exps * (t - 1))
                src = s_bank[:, i]
                if hide:
                    kind = 1 if t == 0 else 2 if t == last else 0
                    if t >= 2:
                        dve.wait_ge(s["turned"], t - 1)
                    nc.vector.scalar_tensor_tensor(p[:, i], s_bank[:, i], scale, each(C.hide[:, kind, :], HEADS),
                                                   ALU.mult, ALU.add).then_inc(s["hidden"], 1)
                    dve.wait_ge(s["hidden"], t + 1)
                    src = p[:, i]
                nc.vector.tensor_reduce(mx[:, i], src, AX.X, ALU.max).then_inc(s["max_step"], 1)
                dve.wait_ge(s["max_step"], max_steps * t + 1)
                if sinks is not None:
                    nc.vector.tensor_tensor(mx[:, i], mx[:, i], sinks, ALU.max).then_inc(s["max_step"], 1)
                    dve.wait_ge(s["max_step"], max_steps * t + 2)
                    if t >= 2:
                        dve.wait_ge(s["summed"], t - 1)
                    nc.vector.tensor_tensor(es[:, i], sinks, mx[:, i], ALU.subtract).then_inc(s["max_step"], 1)
                nc.vector.tensor_scalar(nm[:, i], mx[:, i], -1.0 if hide else -scale, None, ALU.mult
                                        ).then_inc(s["max_step"], 1)

            def denominators(t):
                i = t % 2
                dve.wait_ge(s["exp_done"], act_exps * (t + 1))
                if sinks is not None:
                    nc.vector.tensor_tensor(den[:, i], den[:, i], es[:, i], ALU.add).then_inc(s["maxed"], 1)
                    dve.wait_ge(s["maxed"], t + 1)
                if t >= 2:
                    dve.wait_ge(s["normed"], t - 1)
                nc.vector.reciprocal(rec[:, i], den[:, i]).then_inc(s["summed"], 1)

            maxima(0)
            maxima(1)
            denominators(0)
            for t in range(last):
                if t + 1 < last:
                    denominators(t + 1)
                if t:
                    output_copy(dve, t - 1)
                if t + 2 < last:
                    maxima(t + 2)
            output_copy(dve, last - 1)
            if sample_copies:
                sample_copies(dve, B, s, o_bank)
            maxima(last)
            denominators(last)
            output_copy(dve, last)

        @block.scalar
        def _(act):
            if early and "act" in early:
                early["act"](act, B, s, t_bank, o_bank)

            def copy_turned(t):
                act.wait_ge(s["turned"], t + 1)
                if t >= 2:
                    act.wait_ge(s["valued"], t - 1)
                nc.scalar.activation(pT[:, t % 2], t_bank[:], ACT.Copy).then_inc(s["turned_copied"], 1)

            def exponentials(t):
                i = t % 2
                act.wait_ge(s["max_step"], max_steps * (t + 1))
                if t >= 2:
                    act.wait_ge(s["turned"], t - 1)
                    act.wait_ge(s["summed"], t - 1)
                src = p if hide else s_bank
                for h in range(HEADS):
                    nc.scalar.activation(p[:, i, h, :], src[:, i, h, :], ACT.Exp, bias=nm[:, i, h:h + 1],
                                         scale=1.0 if hide else scale, accum_out=den[:, i, h:h + 1]
                                         ).then_inc(s["exp_done"], 1)
                if sinks is not None:
                    nc.scalar.activation(es[:, i], es[:, i], ACT.Exp).then_inc(s["exp_done"], 1)

            exponentials(0)
            for t in range(last):
                if t + 1 < last:
                    exponentials(t + 1)
                copy_turned(t)
            act.wait_ge(s["sample_scored"], 1)
            act.wait_ge(s["valued"], last - 1)
            nc.scalar.activation(pT[:, 1 - (last - 1) % 2], t_bank[:], ACT.Copy).then_inc(s["sample_copied"], 1)
            exponentials(last)
            copy_turned(last)

        @block.gpsimd
        def _(pool):
            for t in range(NT):
                pool.wait_ge(s["summed"], t + 1)
                nc.gpsimd.tensor_tensor(p[:, t % 2], p[:, t % 2], over(rec[:, t % 2], 256), ALU.mult
                                        ).then_inc(s["normed"], 1)


def window_attention(nc, C, A, O, M):
    sq, sk, sv = M["swa_q"], M["swa_k"], M["swa_v"]

    def buffers(ph):
        return {"v": ph.sb("swa_v_rows", [P, NT, P]), "kp": ph.sb("swa_k_past", [P, NB, P]),
                "vp": ph.sb("swa_v_past", [P, NB, P]), "kpT": ph.sb("swa_k_past_t", [P, NB, P]),
                "k_rows": ph.sb("swa_k_rows", [P, 2, P]),
                "landed": ph.sem("swa_past_landed"), "stored": C.window_stored, "copied": ph.sem("swa_rows_copied")}

    def loads(sp, B, s):
        sp.dma_start(B["kp"][:], A["cache_swa_k"][0].rearrange("b k h d -> k b (h d)")).then_inc(B["landed"], 16)
        sp.dma_start(B["vp"][:], A["cache_swa_v"][0].rearrange("b k h d -> k b (h d)")).then_inc(B["landed"], 16)
        sp.wait_ge(B["copied"], 5)
        for j, (k, v) in enumerate((("p_swa_k", "p_swa_v"), ("s_swa_k", "s_swa_v"))):
            for name, rows in ((k, B["k_rows"][:, j, :]), (v, B["v"][:, PT - 1 + j, :])):
                sp.dma_start(O[name][0].rearrange("b t h d -> (b t) (h d)"), rows).then_inc(B["stored"], 16)
        sp.wait_ge(B["stored"], 64)

    groups = [[("kp", b) for b in range(8)], [("v", t) for t in range(8)], [("v", 8), ("k", 7), ("k", 8)]]

    def early_pe(pe, B, s, t_bank, o_bank):
        pe.wait_ge(B["landed"], 32)
        for n, group in enumerate(groups):
            if n == 2:
                pe.wait_ge(B["copied"], 2)
            bank = t_bank if n % 2 == 0 else o_bank
            for j, (what, t) in enumerate(group):
                src = B["kp"][:, t, :] if what == "kp" else (sk if what == "k" else sv)[:, 0, P * t:P * t + P]
                ins = nc.tensor.transpose(bank[:, j, :], src, C.ident[:])
            ins.then_inc(s["early"], 1)
        pe.wait_ge(B["copied"], 5)

    def early_dve(dve, B, s, t_bank, o_bank):
        for n, (to, frm) in enumerate(((B["kpT"][:, 0:4], t_bank[:, 0:4]), (B["kpT"][:, 4:8], t_bank[:, 4:8]),
                                       (B["v"][:, 0:8], o_bank[:]), (B["v"][:, 8], t_bank[:, 0]),
                                       (B["k_rows"][:], t_bank[:, 1:3]))):
            dve.wait_ge(s["early"], (1, 1, 2, 3, 3)[n])
            nc.vector.tensor_copy(to, frm).then_inc(B["copied"], 1)

    def half(h):
        return slice(64 * (h // 2), 64 * (h // 2) + 64)

    def scores(pe, t, out):
        for h in range(HEADS):
            q = sq[half(h), h % 2, P * t:P * t + P]
            if t:
                ins = nc.tensor.matmul(out[:, h, :], q, sk[half(h), 0, P * t - P:P * t + P], start=True, stop=True)
            else:
                for j in range(2):
                    ins = nc.tensor.matmul(out[:, h, P * j:P * j + P], q, sk[half(h), 0, 0:P], start=True, stop=True)
        return ins

    def turned_parts(pe, B, s, t_bank, o_bank):
        for h in range(HEADS):
            slot = 4 * (h // 2) + h % 2
            for b in range(NB):
                ins = nc.tensor.matmul(t_bank[:, slot, TB * b:TB * b + TB], B["kpT"][half(h), b, :],
                                       sq[half(h), h % 2, TP + TB * b:TP + TB * b + TB], start=True, stop=True)
        ins.then_inc(s["sample_scored"], 1)

    def new_scores(pe, out):
        for h in range(HEADS):
            ins = nc.tensor.matmul(out[:, h, P:2 * P], sq[half(h), h % 2, TP:T], sk[half(h), 0, TP:T],
                                   start=True, stop=True)
        return ins

    def values(pe, t, pT, out, B, s):
        for h in range(HEADS):
            kv = slice(64 * (h // 2), 64 * (h // 2) + 64)
            o = out[64 * (h % 2):64 * (h % 2) + 64, h // 2, :]
            if t < NT - 1:
                nc.tensor.matmul(o, B["v"][:, max(t - 1, 0), kv], pT[:, h, :], start=True, stop=False)
                ins = nc.tensor.matmul(o, B["v"][:, t, kv], pT[:, 4 + h, :], start=False, stop=True)
            else:
                nc.tensor.matmul(o, B["v"][:, t, kv], pT[:, 4 + h, :], start=True, stop=False, skip_group_check=True)
                for b in range(NB):
                    ins = nc.tensor.matmul(o[:, TB * b:TB * b + TB], B["vp"][:, b, kv], pT[:, h, TB * b:TB * b + TB],
                                           start=False, stop=(b == NB - 1), skip_group_check=True)
        return ins

    def dest(t, o_bank):
        return C.mixT[:, 4:6, P * t:P * t + P], o_bank[:, 0:2, :]

    slots = [(4 * (h // 2) + h % 2, h, 0) for h in range(HEADS)]
    attention(nc, C, "sw", float(SWA_HD) ** -0.5, True, C.sinks[:], scores, (slots, turned_parts, new_scores, None),
              values, dest, loads, buffers, {"pe": early_pe, "dve": early_dve})




def row_projection(nc, C, tag, actT, n_tiles, w_dram, out, residual=None, add=True):
    RING, A_RING = 3, min(4, n_tiles)
    together = min(3, n_tiles)
    with C.phase() as ph:
        raw = ph.sb(f"{tag}_w_raw", [P, RING, D])
        w_hi, w_lo = ph.sb(f"{tag}_w_hi", [P, KD, D], F32R), ph.sb(f"{tag}_w_lo", [P, KD, D], F32R)
        a_hi, a_lo = (ph.sb(f"{tag}_act_{n}", [P, A_RING, KD, P], F32R) for n in ("hi", "lo"))
        banks = ph.psum(f"{tag}_banks", [P, 8, 512])
        w_landed = [ph.sem(f"{tag}_w_landed{r}") for r in range(RING)]
        r_landed = [ph.sem(f"{tag}_r_landed{t}") for t in range(n_tiles if residual else 0)]
        act_high, act_split_first, act_split_later, w_high, w_split, projected, freed = (
            ph.sem(f"{tag}_{n}") for n in ("act_high", "act_split_first", "act_split_later", "w_high", "w_split",
                                           "projected", "freed"))
        block = ph.block()

        def act_tile(t):
            return actT[:, :, P * t:P * t + P]

        @block.sync
        def _(sp):
            for k in range(KD):
                if k >= RING:
                    sp.wait_ge(w_split, k - RING + 1)
                sp.dma_start(raw[:, k % RING, :], w_dram[P * k:P * k + P, :]).then_inc(w_landed[k % RING], 16)
            for t, rows in enumerate(residual or ()):
                sp.dma_start(out[:, t, :], rows).then_inc(r_landed[t], 16)

        @block.tensor
        def _(pe):
            def products(n, k):
                t, half = divmod(n, 2)
                col = slice(512 * half, 512 * half + 512)
                passes = ((a_hi, w_hi), (a_hi, w_lo), (a_lo, w_hi))
                for i, (a, w) in enumerate(passes):
                    ins = nc.tensor.matmul(banks[:, n % 8, :], a[:, t % A_RING, k, :], w[:, k, col],
                                           start=(k == 0 and i == 0), stop=(k == KD - 1 and i == 2))
                if k == KD - 1:
                    ins.then_inc(projected, 1)

            for k in range(KD):
                pe.wait_ge(w_split, k + 1)
                for n in range(2 * together):
                    if k == 0 and n % 2 == 0:
                        pe.wait_ge(act_split_first, n // 2 + 1)
                    products(n, k)
            for n in range(2 * together, 2 * n_tiles):
                if n % 2 == 0:
                    pe.wait_ge(act_split_later, n // 2 - together + 1)
                if n >= 8:
                    pe.wait_ge(freed, n - 7)
                for k in range(KD):
                    products(n, k)

        @block.scalar
        def _(act):
            def act_hi_part(t):
                if t >= A_RING:
                    act.wait_ge(projected, 2 * (t - A_RING + 1))
                nc.scalar.activation(a_hi[:, t % A_RING], act_tile(t), ACT.Copy).then_inc(act_high, 1)

            act_hi_part(0)
            for k in range(KD):
                act.wait_ge(w_landed[k % RING], 16 * (k // RING + 1))
                nc.scalar.activation(w_hi[:, k], raw[:, k % RING, :], ACT.Copy).then_inc(w_high, 1)
                if k + 1 < together:
                    act_hi_part(k + 1)
            for t in range(together, n_tiles):
                act_hi_part(t)

        @block.gpsimd
        def _(pool):
            for k in range(KD):
                pool.wait_ge(w_high, k + 1)
                nc.gpsimd.tensor_tensor(w_lo[:, k], raw[:, k % RING, :], w_hi[:, k].bitcast(F32), ALU.subtract
                                        ).then_inc(w_split, 1)
            for t in range(together, n_tiles):
                pool.wait_ge(act_high, t + 1)
                nc.gpsimd.tensor_tensor(a_lo[:, t % A_RING], act_tile(t), a_hi[:, t % A_RING].bitcast(F32), ALU.subtract
                                        ).then_inc(act_split_later, 1)

        @block.vector
        def _(dve):
            for t in range(together):
                dve.wait_ge(act_high, t + 1)
                nc.vector.tensor_tensor(a_lo[:, t], act_tile(t), a_hi[:, t].bitcast(F32), ALU.subtract
                                        ).then_inc(act_split_first, 1)
            for n in range(2 * n_tiles):
                t, half = divmod(n, 2)
                to = out[:, t, 512 * half:512 * half + 512]
                if residual and half == 0:
                    dve.wait_ge(r_landed[t], 16)
                dve.wait_ge(projected, n + 1)
                if add:
                    nc.vector.tensor_tensor(to, to, banks[:, n % 8, :], ALU.add).then_inc(freed, 1)
                else:
                    nc.vector.tensor_copy(to, banks[:, n % 8, :]).then_inc(freed, 1)


class FeatureWeights:
    RING = 2

    def __init__(self, C, tag, w_dram, n_tiles):
        self.raw = C.sb(f"{tag}_w_raw", [P, self.RING, KD, P], side="right")
        self.landed = [C.sem(f"{tag}_w_landed{r}") for r in range(self.RING)]
        self.dram = w_dram.rearrange("(k p) c -> p k c", p=P)

    def load(self, sp, n):
        sp.dma_start(self.raw[:, n % self.RING], self.dram[:, :, P * n:P * n + P]).then_inc(self.landed[n % self.RING], 16)

    def load_first(self, sp):
        for n in range(self.RING):
            self.load(sp, n)


def feature_projection(nc, C, tag, hi, lo, weights, n_tiles, out):
    RING = weights.RING
    with C.phase() as ph:
        w_hi, w_lo = (ph.sb(f"{tag}_w_{n}", [P, 2, KD, P], F32R) for n in ("hi", "lo"))
        banks = ph.psum(f"{tag}_banks", [P, 2 * NP, 512])
        high, split, projected, freed = (ph.sem(f"{tag}_{n}") for n in ("high", "split", "projected", "freed"))
        block = ph.block()

        @block.sync
        def _(sp):
            for n in range(RING, n_tiles):
                sp.wait_ge(split, n - RING + 1)
                weights.load(sp, n)

        @block.tensor
        def _(pe):
            for n in range(n_tiles):
                pe.wait_ge(split, n + 1)
                if n >= 2:
                    pe.wait_ge(freed, n - 1)
                for p in range(NP):
                    for k in range(KD):
                        for i, (w, x) in enumerate(((w_hi, hi), (w_hi, lo), (w_lo, hi))):
                            ins = nc.tensor.matmul(banks[:, (n % 2) * NP + p, 0:TC], w[:, n % 2, k, :],
                                                   x[:, k, TC * p:TC * p + TC], start=(k == 0 and i == 0),
                                                   stop=(k == KD - 1 and i == 2))
                    ins.then_inc(projected, 1)

        @block.scalar
        def _(act):
            def weights_high(n):
                act.wait_ge(weights.landed[n % RING], 16 * (n // RING + 1))
                if n >= 2:
                    act.wait_ge(projected, NP * (n - 1))
                nc.scalar.activation(w_hi[:, n % 2], weights.raw[:, n % RING], ACT.Copy).then_inc(high, 1)

            weights_high(0)
            weights_high(1)
            for n in range(n_tiles):
                for p in range(NP):
                    act.wait_ge(projected, NP * n + p + 1)
                    ins = nc.scalar.activation(out[:, n, TC * p:TC * p + TC], banks[:, (n % 2) * NP + p, 0:TC], ACT.Copy)
                ins.then_inc(freed, 1)
                if n + 2 < n_tiles:
                    weights_high(n + 2)

        @block.vector
        def _(dve):
            for n in range(n_tiles):
                dve.wait_ge(high, n + 1)
                nc.vector.tensor_tensor(w_lo[:, n % 2], weights.raw[:, n % RING], w_hi[:, n % 2].bitcast(F32), ALU.subtract
                                        ).then_inc(split, 1)



def memory_kv(nc, C, A, O, kT, v):
    with ExitStack() as st:
        rows = st.enter_context(nc.sbuf_tensor("mem_rows", [P, 2, D], F32))
        mT = st.enter_context(nc.sbuf_tensor("mem_t", [P, KD, MEM], F32))
        norm_turn(nc, C, "nm", rows, [A["mem_prompt"][0, P * t:P * t + P, :] for t in range(2)], 2, V_MIN, mT)
        k = rows
        row_projection(nc, C, "mk", mT, 2, A["w_mk"][0], k, add=False)
        row_projection(nc, C, "mv", mT, 2, A["w_mv"][0], v, add=False)
        with C.phase() as ph:
            squares = ph.sb("mk_squares", [P, 256])
            sums, root, inv = (ph.sb(f"mk_{n}", [P, 2 * HEADS]) for n in ("sums", "root", "inv"))
            banks = ph.psum("mk_turned", [P, 4, 512])
            summed, rooted, inverted, normed, turned, copied = (ph.sem(f"mk_{n}") for n in (
                "summed", "rooted", "inverted", "normed", "turned", "copied"))
            stored = C.memory_stored
            block = ph.block()

            @block.sync
            def _(sp):
                sp.dma_start(O["p_mem_v"][0, 0].rearrange("(t p) h d -> p t (h d)", p=P), v[:]).then_inc(stored, 16)
                sp.wait_ge(normed, 2 * HEADS)
                sp.dma_start(O["p_mem_k"][0, 0].rearrange("(t p) h d -> p t (h d)", p=P), k[:]).then_inc(stored, 16)
                sp.wait_ge(stored, 32)

            @block.scalar
            def _(act):
                for n in range(2 * HEADS):
                    t, h = divmod(n, HEADS)
                    if n:
                        act.wait_ge(summed, n)
                    nc.scalar.activation(squares[:], k[:, t, 256 * h:256 * h + 256], ACT.Square,
                                         accum_out=sums[:, n:n + 1]).then_inc(summed, 1)
                act.wait_ge(summed, 2 * HEADS)
                nc.scalar.activation(root[:], sums[:], ACT.Sqrt, scale=1.0 / 256, bias=C.eps[:, 0:1]).then_inc(rooted, 1)

            @block.vector
            def _(dve):
                dve.wait_ge(rooted, 1)
                nc.vector.reciprocal(inv[:], root[:]).then_inc(inverted, 1)
                dve.wait_ge(inverted, 1)
                for n in range(2 * HEADS):
                    t, h = divmod(n, HEADS)
                    x = k[:, t, 256 * h:256 * h + 256]
                    nc.vector.scalar_tensor_tensor(x, x, inv[:, n:n + 1], C.k_gain[:], ALU.mult, ALU.mult
                                                   ).then_inc(normed, 1)
                for n in range(4):
                    dve.wait_ge(turned, n + 1)
                    nc.vector.tensor_copy(kT[:, 2 * n:2 * n + 2, :], banks[:, n, :].rearrange("p (a b) -> p a b", a=2)
                                          ).then_inc(copied, 1)

            @block.tensor
            def _(pe):
                pe.wait_ge(normed, 2 * HEADS)
                for n in range(4):
                    for j in range(2):
                        for t in range(2):
                            f = 2 * n + j
                            ins = nc.tensor.transpose(banks[:, n, 256 * j + P * t:256 * j + P * t + P],
                                                      k[:, t, P * f:P * f + P], C.ident[:])
                    ins.then_inc(turned, 1)


def memory_attention(nc, C, A, qT, kT, v, attnT):

    def buffers(ph):
        return {"kb": ph.sb("mem_k_one", [P, 2, 2, D]), "vb": ph.sb("mem_v_one", [P, 2, 2, D]),
                "kbT": ph.sb("mem_k_one_t", [P, KD, MEM]),
                "k_landed": [ph.sem(f"mem_k_landed{i}") for i in range(2)],
                "v_landed": [ph.sem(f"mem_v_landed{i}") for i in range(2)],
                "k_turned": ph.sem("mem_k_turned"), "k_copied": ph.sem("mem_k_copied"),
                "k_used": ph.sem("mem_k_used"), "v_used": ph.sem("mem_v_used")}

    def loads(sp, B, s):
        for b in range(NB):
            if b >= 2:
                sp.wait_ge(B["k_turned"], 4 * (b - 1))
            sp.dma_start(B["kb"][:, b % 2], A["cache_mem_k"][0, b].rearrange("(t p) h d -> p t (h d)", p=P)
                         ).then_inc(B["k_landed"][b % 2], 16)
        for b in range(NB):
            if b >= 2:
                sp.wait_ge(B["v_used"], b - 1)
            sp.dma_start(B["vb"][:, b % 2], A["cache_mem_v"][0, b].rearrange("(t p) h d -> p t (h d)", p=P)
                         ).then_inc(B["v_landed"][b % 2], 16)

    def scores(pe, t, out):
        for h in range(HEADS):
            for j in range(2):
                ins = nc.tensor.matmul(out[:, h, :], qT[:, 2 * h + j, P * t:P * t + P], kT[:, 2 * h + j, :],
                                       start=(j == 0), stop=(j == 1))
        return ins

    def turned_parts(pe, B, s, t_bank, o_bank):
        for b in range(NB):
            pe.wait_ge(B["k_landed"][b % 2], 16 * (b // 2 + 1))
            for n in range(4):
                m = 4 * b + n
                if m >= 2:
                    pe.wait_ge(B["k_copied"], m - 1)
                for j in range(2):
                    for kt in range(2):
                        ins = nc.tensor.transpose(o_bank[:, 4 * (n % 2) + 2 * j + kt, :],
                                                  B["kb"][:, b % 2, kt, P * (2 * n + j):P * (2 * n + j) + P], C.ident[:])
                ins.then_inc(B["k_turned"], 1)
            pe.wait_ge(B["k_copied"], 4 * b + 4)
            for kt in range(2):
                for h in range(HEADS):
                    for j in range(2):
                        ins = nc.tensor.matmul(t_bank[:, 4 * kt + h, TB * b:TB * b + TB],
                                               B["kbT"][:, 2 * h + j, P * kt:P * kt + P],
                                               qT[:, 2 * h + j, TP + TB * b:TP + TB * b + TB],
                                               start=(j == 0), stop=(j == 1))
            ins.then_inc(B["k_used"], 1)
        pe.wait_ge(B["k_used"], NB)
        pe.sem_inc(s["sample_scored"], 1)

    def sample_copies(dve, B, s, o_bank):
        for m in range(4 * NB):
            b, n = divmod(m, 4)
            dve.wait_ge(B["k_turned"], m + 1)
            if b:
                dve.wait_ge(B["k_used"], b)
            nc.vector.tensor_copy(B["kbT"][:, 2 * n:2 * n + 2, :], o_bank[:, 4 * (n % 2):4 * (n % 2) + 4, :].rearrange(
                "p (j k) c -> p j (k c)", j=2)).then_inc(B["k_copied"], 1)

    def values(pe, t, pT, out, B, s):
        if t < NT - 1:
            for h in range(HEADS):
                for j in range(2):
                    f = 2 * h + j
                    for kt in range(2):
                        ins = nc.tensor.matmul(out[:, f, :], v[:, kt, P * f:P * f + P], pT[:, 4 * kt + h, :],
                                               start=(kt == 0), stop=(kt == 1))
            return ins
        for b in range(NB):
            pe.wait_ge(B["v_landed"][b % 2], 16 * (b // 2 + 1))
            for h in range(HEADS):
                for j in range(2):
                    f = 2 * h + j
                    for kt in range(2):
                        ins = nc.tensor.matmul(out[:, f, TB * b:TB * b + TB], B["vb"][:, b % 2, kt, P * f:P * f + P],
                                               pT[:, 4 * kt + h, TB * b:TB * b + TB], start=(kt == 0), stop=(kt == 1))
            if b < NB - 1:
                ins.then_inc(B["v_used"], 1)
        return ins

    def dest(t, o_bank):
        return attnT[:, :, P * t:P * t + P], o_bank[:]

    slots = [(4 * kt + h, h, kt) for kt in range(2) for h in range(HEADS)]
    attention(nc, C, "ma", 1.0 / 16, False, None, scores, (slots, turned_parts, None, None), values, dest,
              loads, buffers, None, sample_copies)



def ffn_states_in(nc, C, A, old):
    n_tiles = 2 * NF
    with C.phase() as ph:
        rows = ph.sb("ffn_old_rows", [16, 2 * FF])
        banks = ph.psum("ffn_old_t", [P, 2, 22, 16])
        landed, turned, copied = (ph.sem(f"fs_{n}") for n in ("landed", "turned", "copied"))
        block = ph.block()

        @block.sync
        def _(sp):
            sp.dma_start(rows[:], A["state_ffn_conv"][0].rearrange("b i c -> (b i) c")).then_inc(landed, 16)

        @block.tensor
        def _(pe):
            pe.wait_ge(landed, 16)
            for n in range(n_tiles):
                ins = nc.tensor.transpose(banks[:, n // 22, n % 22, :], rows[:, P * n:P * n + P], C.ident[0:16, 0:16])
            ins.then_inc(turned, 1)

        @block.vector
        def _(dve):
            dve.wait_ge(turned, 1)
            for i in range(2):
                nc.vector.tensor_copy(old[:, 22 * i:22 * i + 22, :], banks[:, i]).then_inc(copied, 1)
            dve.wait_ge(copied, 2)


class FfnWeights:

    def __init__(self, C, A):
        self.raw = C.sb("up_raw", [P, 2, KD, P])
        self.d_raw = C.sb("down_raw", [P, D])
        self.w_up = A["w_up"][0].rearrange("(k p) c -> p k c", p=P)
        self.w_down = A["w_down"][0].rearrange("(f p) c -> f p c", p=P)
        self.w_landed = [C.sem(f"f_w_landed_{s}") for s in "gv"]
        self.d_landed = C.sem("f_d_landed")

    def load_up(self, sp, s, f):
        sp.dma_start(self.raw[:, s], self.w_up[:, :, FF * s + P * f:FF * s + P * f + P]).then_inc(self.w_landed[s], 16)

    def load_down(self, sp, f):
        sp.dma_start(self.d_raw[:], self.w_down[f]).then_inc(self.d_landed, 16)

    def load_first(self, sp):
        self.load_up(sp, 0, 0)
        self.load_up(sp, 1, 0)
        self.load_down(sp, 0)


def ffn(nc, C, A, O, h, hi, lo, old, weights):
    W = 3
    L = xp_len(W)
    LY = L - (W - 1)
    NG = 2 * NT
    with C.phase() as ph:
        raw, d_raw, w_landed, d_landed = weights.raw, weights.d_raw, weights.w_landed, weights.d_landed
        w_hi, w_lo = ph.sb("up_hi", [P, 2, KD, P], F32R), ph.sb("up_lo", [P, 2, KD, P], F32R)
        d_hi, d_lo = ph.sb("down_hi", [P, D], F32R), ph.sb("down_lo", [P, D], F32R)
        xp = ph.sb("ffn_conv_in", [P, 2, L])
        y = ph.sb("ffn_conv_out", [P, 2, LY + 2])
        a = ph.sb("ffn_gated", [P, T])
        a_hi, a_lo = ph.sb("gated_hi", [P, T], F32R), ph.sb("gated_lo", [P, T], F32R)
        tails = ph.sb("ffn_tails", [P, 2, NF, 18])
        banks = ph.psum("ffn_banks", [P, 8, 512])
        d_bank = (2, 6, 7, 0, 1)
        split, w_high, up, evacuated, padded, tailed, tap0, conv = (
            [ph.sem(f"f_{n}_{s}") for s in "gv"] for n in (
                "split", "w_high", "up", "evacuated", "padded", "tailed", "tap0", "conv"))
        d_split, d_high, silued, gated, a_high, a_ready, down, added, conv_step, zeroed = (
            ph.sem(f"f_{n}") for n in ("d_split", "d_high", "silued", "gated", "a_high", "a_ready", "down",
                                       "added", "conv_step", "zeroed"))
        turned, copied = ph.sem("f_turned"), ph.sem("f_copied")
        G, V = 0, 1
        LAST = NG * (NF - 1)
        row_slots = [(raw[0:18].rearrange("p s k c -> p (s k c)"), 4)] + [(y[0:18, s], 2) for s in (G, V)] + [
            (xp[0:18, s], 2) for s in (G, V)]
        slot_of = [(b, j) for b, (_, n) in enumerate(row_slots) for j in range(n)][:2 * NF // 4]
        block = ph.block()

        def cycles(body):
            for f in range(NF + 1):
                body(f, f < NF, f >= 1)

        @block.sync
        def _(sp):
            def body(f, now, before):
                if now and before:
                    for s in (G, V):
                        sp.wait_ge(split[s], f)
                        weights.load_up(sp, s, f)
                    sp.wait_ge(d_split, f)
                    weights.load_down(sp, f)
            cycles(body)

            def store_y(t):
                sp.wait_ge(added, LAST + 2 * t + 2)
                to = O["y_prompt"][0, P * t:P * t + P, :] if t < PT else O["y_sample"].rearrange("b t d -> (b t) d")
                sp.dma_start(to, h[:, t, :]).then_inc(C.y_stored, 16)

            def store_rows(b):
                buf = row_slots[b][0]
                ms = [m for m, (at, _) in enumerate(slot_of) if at == b]
                c0, cn = 512 * ms[0], 512 * len(ms)
                sp.wait_ge(copied, ms[-1] + 1)
                sp.dma_start(O["p_ffn_conv"][0, 0][:, c0:c0 + cn], buf[0:2, 0:cn]).then_inc(C.ffn_rows_stored[0], 16)
                sp.dma_start(O["s_ffn_conv"][0].rearrange("b i c -> (b i) c")[:, c0:c0 + cn], buf[2:18, 0:cn]
                             ).then_inc(C.ffn_rows_stored[1], 16)

            for t in range(NT):
                store_y(t)
                if t >= 4:
                    store_rows(t - 4)
            sp.wait_ge(C.y_stored, 16 * NT)
            for kind in range(2):
                sp.wait_ge(C.ffn_rows_stored[kind], 16 * len(row_slots))

        @block.tensor
        def _(pe):
            def project(s, f, before):
                pe.wait_ge(split[s], f + 1)
                if before and s == V:
                    pe.wait_ge(evacuated[V], f)
                if before and s == G and f >= 2:
                    pe.wait_ge(added, NG * (f - 1) - 2)
                for p in range(NP):
                    n = 0
                    for k in range(KD):
                        for wt, x in ((w_hi, hi), (w_hi, lo), (w_lo, hi)):
                            ins = nc.tensor.matmul(banks[:, NP * s + p, 0:TC], wt[:, s, k, :], x[:, k, TC * p:TC * p + TC],
                                                   start=(n == 0), stop=(n == 3 * KD - 1))
                            n += 1
                    ins.then_inc(up[s], 1)

            def turn_rows(m):
                if m >= 3:
                    pe.wait_ge(copied, m - 2)
                for j in range(4):
                    s, i = divmod(4 * m + j, NF)
                    ins = nc.tensor.transpose(banks[0:18, NP + m % 3, P * j:P * j + P], tails[:, s, i, :], C.ident[:])
                ins.then_inc(turned, 1)

            def body(f, now, before):
                if now:
                    project(G, f, before)
                    project(V, f, before)
                else:
                    for s in (G, V):
                        pe.wait_ge(tailed[s], NF)
                    for m in range(3):
                        turn_rows(m)
                if before:
                    pe.wait_ge(evacuated[G], min(f + 1, NF))
                    pe.wait_ge(a_ready, f)
                    pe.wait_ge(d_split, f)
                    for n in range(NG):
                        t, half = divmod(n, 2)
                        bank = banks[:, d_bank[n % 5], :]
                        if n >= 5 or f >= 2:
                            pe.wait_ge(added, NG * (f - 1) + n - 4)
                        tok, col = slice(P * t, P * t + P), slice(512 * half, 512 * half + 512)
                        nc.tensor.matmul(bank, a_hi[:, tok], d_hi[:, col], start=True, stop=False)
                        nc.tensor.matmul(bank, a_hi[:, tok], d_lo[:, col], start=False, stop=False)
                        nc.tensor.matmul(bank, a_lo[:, tok], d_hi[:, col], start=False, stop=True
                                         ).then_inc(down, 1)
                        if not now and n % 2 and n < NG - 1:
                            turn_rows(3 + n // 2)
            cycles(body)

        @block.scalar
        def _(act):
            def weights_high(s, f, before):
                act.wait_ge(w_landed[s], 16 * (f + 1))
                if before:
                    act.wait_ge(up[s], NP * f)
                nc.scalar.activation(w_hi[:, s], raw[:, s], ACT.Copy).then_inc(w_high[s], 1)

            def evacuate(s, f, before):
                if before:
                    act.wait_ge(conv[s], f)
                    act.wait_ge(tailed[s], f)
                for p in range(NP):
                    act.wait_ge(up[s], NP * f + p + 1)
                    cn = TC if p < 2 else PP
                    nc.scalar.activation(xp[:, s, W - 1 + TC * p:W - 1 + TC * p + cn], banks[:, NP * s + p, 0:cn], ACT.Copy)
                nc.scalar.activation(xp_sample(xp[:, s, :], W, W - 1, TB), seqs(banks[:, NP * s + 2, PP:TC]), ACT.Copy
                                     ).then_inc(evacuated[s], 1)

            def first_tap(s, f, before):
                act.wait_ge(evacuated[s], f + 1)
                act.wait_ge(padded[s], f + 1)
                if before:
                    act.wait_ge(gated, f)
                col = V_FC + NF * s + f
                nc.scalar.activation(y[:, s, 0:LY], xp[:, s, 0:LY], ACT.Copy, scale=C.vec[:, col:col + 1]
                                     ).then_inc(tap0[s], 1)

            def body(f, now, before):
                if before:
                    first_tap(V, f - 1, f >= 2)
                if now:
                    if not before:
                        weights_high(G, 0, False)
                    weights_high(V, f, before)
                if before:
                    act.wait_ge(conv[G], f)
                    nc.scalar.activation(y[:, G, 0:LY], y[:, G, 0:LY], ACT.Silu).then_inc(silued, 1)
                    act.wait_ge(d_landed, 16 * f)
                    if f >= 2:
                        act.wait_ge(down, NG * (f - 1))
                    nc.scalar.activation(d_hi[:], d_raw[:], ACT.Copy).then_inc(d_high, 1)
                    act.wait_ge(gated, f)
                    nc.scalar.activation(a_hi[:], a[:], ACT.Copy).then_inc(a_high, 1)
                if now:
                    evacuate(G, f, before)
                    first_tap(G, f, before)
                    if f + 1 < NF:
                        weights_high(G, f + 1, True)
                    evacuate(V, f, before)
            cycles(body)

            for s in (G, V):
                act.wait_ge(split[s], NF)
                act.wait_ge(conv[s], NF)
            for m, (b, j) in enumerate(slot_of):
                act.wait_ge(turned, m + 1)
                nc.scalar.activation(row_slots[b][0][:, 512 * j:512 * j + 512], banks[0:18, NP + m % 3, :], ACT.Copy
                                     ).then_inc(copied, 1)

        @block.gpsimd
        def _(pool):
            nc.gpsimd.memset(xp[:, :, 0:W - 1], 0.0).then_inc(zeroed, 1)
            pool.wait_ge(zeroed, 1)

            def weights_low(s, f, before):
                pool.wait_ge(w_high[s], f + 1)
                nc.gpsimd.tensor_tensor(w_lo[:, s], raw[:, s], w_hi[:, s].bitcast(F32), ALU.subtract).then_inc(split[s], 1)

            def pads(s, f, before):
                if before:
                    pool.wait_ge(conv[s], f)
                nc.gpsimd.tensor_copy(xp_sample(xp[:, s, :], W, 0, W - 1),
                                      old[:, NF * s + f, :].rearrange("p (b i) -> p b i", b=NB)).then_inc(padded[s], 1)

            def tail(s, f):
                pool.wait_ge(evacuated[s], f + 1)
                nc.gpsimd.tensor_copy(tails[:, s, f, 0:2], xp[:, s, TP:TP + 2])
                nc.gpsimd.tensor_copy(tails[:, s, f, 2:18].rearrange("p (b i) -> p b i", b=NB),
                                      xp_sample(xp[:, s, :], W, TB, 2)).then_inc(tailed[s], 1)

            def body(f, now, before):
                if now:
                    if not before:
                        weights_low(G, 0, False)
                    weights_low(V, f, before)
                if before:
                    pool.wait_ge(d_high, f)
                    nc.gpsimd.tensor_tensor(d_lo[:], d_raw[:], d_hi[:].bitcast(F32), ALU.subtract).then_inc(d_split, 1)
                if now:
                    pads(G, f, before)
                    tail(G, f)
                    if f + 1 < NF:
                        weights_low(G, f + 1, True)
                    pads(V, f, before)
                    tail(V, f)
            cycles(body)

        @block.vector
        def _(dve):
            def taps(s, f):
                dve.wait_ge(tap0[s], f + 1)
                for j in (1, 2):
                    col = V_FC + 2 * NF * j + NF * s + f
                    ins = nc.vector.scalar_tensor_tensor(y[:, s, 0:LY], xp[:, s, j:j + LY], C.vec[:, col:col + 1],
                                                         y[:, s, 0:LY], ALU.mult, ALU.add)
                    if j == 1:
                        ins.then_inc(conv_step, 1)
                        dve.wait_ge(conv_step, 2 * f + s + 1)
                ins.then_inc(conv[s], 1)

            def body(f, now, before):
                if before:
                    taps(V, f - 1)
                    dve.wait_ge(conv[V], f)
                    dve.wait_ge(silued, f)
                    if f >= 2:
                        dve.wait_ge(a_ready, f - 1)
                        dve.wait_ge(a_high, f - 1)
                    nc.vector.tensor_tensor(a[:, 0:TP], y[:, G, 0:TP], y[:, V, 0:TP], ALU.mult)
                    nc.vector.tensor_tensor(seqs(a[:, TP:T]), xp_sample(y[:, G, :], W, 0, TB), xp_sample(y[:, V, :], W, 0, TB),
                                            ALU.mult).then_inc(gated, 1)
                    dve.wait_ge(a_high, f)
                    nc.vector.tensor_tensor(a_lo[:], a[:], a_hi[:].bitcast(F32), ALU.subtract).then_inc(a_ready, 1)
                if now:
                    taps(G, f)
                if before:
                    for n in range(NG):
                        t, half = divmod(n, 2)
                        to = h[:, t, 512 * half:512 * half + 512]
                        dve.wait_ge(down, NG * (f - 1) + n + 1)
                        if f >= 2:
                            dve.wait_ge(added, NG * (f - 2) + n + 1)
                        nc.vector.tensor_tensor(to, to, banks[:, d_bank[n % 5], :], ALU.add).then_inc(added, 1)
            cycles(body)



def program(nc, A, O):
    with ExitStack() as stack:
        C = Ctx(nc, stack)
        C.ident, C.ones, C.pair_ones = (C.sb(n, [P, P]) for n in ("ident", "ones", "pair_ones"))
        C.upto, C.after = C.sb("upto", [P, 2, P]), C.sb("after", [P, 2, P])
        C.level, C.hide = C.sb("level", [P, 6, P]), C.sb("hide", [P, 3, 256])
        C.vec, C.k_gain = C.sb("vec", [P, V_ALL]), C.sb("k_gain", [P, 256])
        C.seq_mask = C.sb("seq_mask", [P, NB])
        C.a_log, C.dt_bias, C.sinks, C.eps = (C.sb(n, [P, 4]) for n in ("a_log", "dt_bias", "sinks", "eps"))
        C.state_stored, C.window_stored, C.memory_stored, C.y_stored = (
            C.sem(f"{n}_stored") for n in ("state", "window", "memory", "y"))
        C.conv_stored, C.ffn_rows_stored = ([C.sem(f"{n}_stored{i}") for i in range(2)] for n in ("conv", "ffn_rows"))
        setup(nc, C, A)
        x_tiles = [A["x_prompt"][0, P * t:P * t + P, :] for t in range(PT)] + [
            A["x_sample"].rearrange("b t d -> (b t) d")]
        ffn_old = C.sb("ffn_old", [P, 2 * NF, 16])
        ffn_states_in(nc, C, A, ffn_old)
        mix = ExitStack()
        C.mixT = mix.enter_context(nc.sbuf_tensor("mixT", [P, KD, T], F32))
        with ExitStack() as first:
            M = {}
            for name, shape in (("qkv", [P, 12, T]), ("swa_q", [P, 2, T]), ("swa_k", [P, 1, T]),
                                ("swa_v", [P, 1, T]), ("gate", [8, T])):
                M[name] = first.enter_context(nc.sbuf_tensor(name, shape, F32))
            with nc.sbuf_tensor("xT", [P, KD, T], F32) as xT:
                M["xT"] = xT
                x_rows = M["qkv"][:].rearrange("p a b -> p (a b)")[:, 0:NT * D].rearrange("p (t d) -> p t d", d=D)
                norm_turn(nc, C, "nx", x_rows, x_tiles, NT, V_MIX, xT)
                in_projection(nc, C, A, O, M)
            for name in ("g", "beta", "up", "tail", "beta_up"):
                M[name] = first.enter_context(nc.sbuf_tensor(f"gate_{name}", [P, NT, HEADS], F32))
            group_norms(nc, C, M)
            gates(nc, C, M)
            delta_net(nc, C, A, O, M)
            gdn_output(nc, C, M)
            window_attention(nc, C, A, O, M)
        h = stack.enter_context(nc.sbuf_tensor("h", [P, NT, D], F32, side="right"))
        row_projection(nc, C, "wo", C.mixT, NT, A["w_o"][0], h, residual=x_tiles)
        mix.close()
        attn = ExitStack()
        with ExitStack() as second:
            kT = second.enter_context(nc.sbuf_tensor("mem_k_t", [P, KD, MEM], F32))
            v = second.enter_context(nc.sbuf_tensor("mem_v", [P, 2, D], F32))
            memory_kv(nc, C, A, O, kT, v)
            with C.phase() as ph:
                hn_hi, hn_lo = (ph.sb(f"hn_{n}", [P, KD, T], F32R, side="right") for n in ("hi", "lo"))
                weights = FeatureWeights(ph, "mq", A["w_mq"][0], KD)
                norm_turn(nc, C, "nh", h, [], NT, V_MEM, hn_hi, hn_lo, ahead=weights.load_first)
                qT = second.enter_context(nc.sbuf_tensor("mem_q_t", [P, KD, T], F32))
                feature_projection(nc, C, "mq", hn_hi, hn_lo, weights, KD, qT)
            column_norms(nc, C, "qn", [([qT[:, 2 * i, :], qT[:, 2 * i + 1, :]], [qT[:, 2 * i, :], qT[:, 2 * i + 1, :]],
                                        C.ones[:], 1.0 / 256, [C.vec[:, V_MQ + j:V_MQ + j + 1] for j in range(2)])
                                       for i in range(HEADS)])
            attnT = attn.enter_context(nc.sbuf_tensor("mem_attn_t", [P, KD, T], F32, side="right"))
            memory_attention(nc, C, A, qT, kT, v, attnT)
        row_projection(nc, C, "mo", attnT, NT, A["w_mo"][0], h)
        attn.close()
        hi, lo = (C.sb(f"h_{n}", [P, KD, T], F32R) for n in ("hi", "lo"))
        weights = FfnWeights(C, A)
        norm_turn(nc, C, "nf", h, [], NT, V_FFN, hi, lo, ahead=weights.load_first)
        ffn(nc, C, A, O, h, hi, lo, ffn_old, weights)


_INS = ["x_prompt", "x_sample", "mem_prompt", "state_gdn", "state_gdn_conv", "cache_swa_k", "cache_swa_v",
        "state_sc_conv", "cache_mem_k", "cache_mem_v", "state_ffn_conv", "norm_mix_g", "w_in", "w_gdn_conv",
        "gdn_a_log", "gdn_dt_bias", "gdn_norm_g", "swa_q_norm_g", "swa_k_norm_g", "swa_sinks", "w_sc_conv", "w_o",
        "norm_mem_g", "mem_in_norm_g", "w_mq", "w_mk", "w_mv", "mem_q_norm_g", "mem_k_norm_g", "w_mo",
        "norm_ffn_g", "w_up", "w_ffn_conv", "w_down"]
_OUTS = [("y_prompt", (1, 1024, 1024)), ("y_sample", (8, 16, 1024)), ("p_gdn", (1, 1, 4, 128, 128)),
         ("p_gdn_conv", (1, 1, 3, 1536)), ("p_swa_k", (1, 1, 128, 2, 64)), ("p_swa_v", (1, 1, 128, 2, 64)),
         ("p_sc_conv", (1, 1, 2, 256)), ("p_mem_k", (1, 1, 256, 4, 256)), ("p_mem_v", (1, 1, 256, 4, 256)),
         ("p_ffn_conv", (1, 1, 2, 5632)), ("s_gdn", (1, 8, 4, 128, 128)), ("s_gdn_conv", (1, 8, 3, 1536)),
         ("s_swa_k", (1, 8, 16, 2, 64)), ("s_swa_v", (1, 8, 16, 2, 64)), ("s_sc_conv", (1, 8, 2, 256)),
         ("s_ffn_conv", (1, 8, 2, 5632))]


def kernel(**inputs):
    import numpy as _np
    import concourse.bacc as _bacc
    from concourse import mybir as _mybir
    from concourse.bass_utils import run_bass_kernel_spmd as _run

    nc = _bacc.Bacc("TRN2", target_bir_lowering=False, num_devices=1)
    arrays, A, O = {}, {}, {}
    for name in _INS:
        a = _np.ascontiguousarray(inputs[name])
        arrays[f"in_{name}"] = a
        A[name] = nc.dram_tensor(f"in_{name}", a.shape, _mybir.dt.from_np(a.dtype), kind="ExternalInput").ap()
    for name, shape in _OUTS:
        O[name] = nc.dram_tensor(f"out_{name}", shape, _mybir.dt.float32, kind="ExternalOutput").ap()
    program(nc, A, O)
    r = _run(nc, [arrays], core_ids=[0])
    return tuple(r.results[0][f"out_{name}"] for name, _ in _OUTS)
```

```python
from contextlib import ExitStack

import concourse.bass as bass
from concourse import mybir

F32 = mybir.dt.float32
F32R = mybir.dt.float32r
ALU = mybir.AluOpType
ACT = mybir.ActivationFunctionType
AX = mybir.AxisListType

P = 128
D = 1024
KD = D // P
TP = 1024
NB, TB = 8, 16
TS = NB * TB
T = TP + TS
NT = T // P
PT = TP // P
NP = 3
TC = T // NP
PP = TP - 2 * TC
HEADS = 4
HW = HEADS * P
CONV_CH = 1536
WIDTH = 3336
EPS = 1e-6
NEG = -1e30
FF = 2816
NF = FF // P
MEM = 256
SWA_HD = 64

V_MIX, V_MEM, V_MIN, V_FFN, V_MQ, V_GN, V_SQ, V_SK, V_GC, V_SC, V_FC = 0, 8, 16, 24, 32, 34, 35, 36, 37, 85, 91
V_ALL = V_FC + 3 * 2 * NF


def xp_len(w):
    return TP + w - 1 + NB * (TB + w - 1)


def xp_sample(buf, w, lo, n):
    s = TB + w - 1
    a = TP + w - 1
    return buf[:, a:a + NB * s].rearrange("p (b s) -> p b s", s=s)[:, :, lo:lo + n]


def seqs(ap):
    return ap.rearrange("p (b s) -> p b s", s=TB)


def heads(ap):
    return ap.rearrange("p (h c) -> p h c", h=HEADS)


def over(ap, n):
    return ap.unsqueeze(2).to_broadcast([ap.shape[0], ap.shape[1], n])


def each(ap, n):
    return ap.unsqueeze(1).to_broadcast([ap.shape[0], n, ap.shape[1]])


class Ctx:

    def __init__(self, nc, stack):
        self.nc, self.stack = nc, stack

    def sb(self, name, shape, dt=F32, side="left"):
        return self.stack.enter_context(self.nc.sbuf_tensor(name, shape, dt, side=side))

    def psum(self, name, shape, dt=F32):
        return self.stack.enter_context(self.nc.psum_tensor(name, shape, dt))

    def sem(self, name):
        return self.stack.enter_context(self.nc.semaphore(name))

    def phase(self):
        return Phase(self.nc)


class Phase(Ctx):

    def __init__(self, nc):
        super().__init__(nc, ExitStack())
        self.open = None
        self.sems = []

    def sem(self, name):
        s = super().sem(name)
        self.sems.append(s)
        return s

    def __enter__(self):
        self.stack.__enter__()
        return self

    def end_block(self):
        if self.open is not None:
            self.open.__exit__(None, None, None)
            self.open = None

    def block(self):
        self.end_block()
        self.open = self.nc.Block()
        return self.open.__enter__()

    def __exit__(self, *a):
        if a[0] is None:
            self.end_block()
            for s in self.sems:
                self.nc.sync.sem_clear(s)
        return self.stack.__exit__(*a)



def setup(nc, C, A, ffn_old, ahead):
    with C.phase() as ph:
        rows_a = ph.sb("vec_rows_a", [91, P])
        rows_b = ph.sb("vec_rows_b", [88, P])
        rows_c = ph.sb("vec_rows_c", [44, P])
        ffn_rows = ph.sb("ffn_old_rows", [16, 2 * FF])
        tp = ph.psum("vec_cols", [P, 512])
        ffn_banks = ph.psum("ffn_old_t", [P, 2, 22, 16])
        loaded, ffn_landed, ready, turned, ffn_turned, copied = (ph.sem(f"s0_{n}") for n in (
            "loaded", "ffn_landed", "ready", "turned", "ffn_turned", "copied"))
        pool_step = ph.sem("s0_pool_step")
        ident, ones = C.ident, C.ones
        block = ph.block()

        def rows_of(a):
            return a.rearrange("(k p) -> k p", p=P)

        def taps_of(a):
            return a.rearrange("i (k p) -> (i k) p", p=P)

        table = [(rows_a[V_MIX:V_MIX + 8, :], rows_of(A["norm_mix_g"][0])),
                 (rows_a[V_MEM:V_MEM + 8, :], rows_of(A["norm_mem_g"][0])),
                 (rows_a[V_MIN:V_MIN + 8, :], rows_of(A["mem_in_norm_g"][0])),
                 (rows_a[V_FFN:V_FFN + 8, :], rows_of(A["norm_ffn_g"][0])),
                 (rows_a[V_MQ:V_MQ + 2, :], rows_of(A["mem_q_norm_g"][0])),
                 (rows_a[V_GN:V_GN + 1, :], rows_of(A["gdn_norm_g"][0])),
                 (rows_a[V_GC:V_GC + 48, :], taps_of(A["w_gdn_conv"][0])),
                 (rows_a[V_SC:V_SC + 6, :], taps_of(A["w_sc_conv"][0])),
                 (rows_b[:], taps_of(A["w_ffn_conv"][0][0:2])), (rows_c[:], taps_of(A["w_ffn_conv"][0][2:3]))]
        table += [(rows_a[col:col + 1, half * 64:half * 64 + 64], A[name])
                  for col, name in ((V_SQ, "swa_q_norm_g"), (V_SK, "swa_k_norm_g")) for half in range(2)]
        vectors = [(to[:], A[name].to_broadcast([P, to.shape[1]])) for to, name in (
            (C.k_gain, "mem_k_norm_g"), (C.a_log, "gdn_a_log"), (C.dt_bias, "gdn_dt_bias"), (C.sinks, "swa_sinks"))]

        @block.sync
        def _(sp):
            ahead(sp, "first")
            for to, frm in table[:8]:
                sp.dma_start(to, frm).then_inc(loaded, 16)
            sp.wait_ge(loaded, 16 * (len(table) + len(vectors)))
            sp.sem_inc(ready, 1)

        @block.scalar
        def _(act):
            for to, frm in table[8:] + vectors:
                act.dma_start(to, frm).then_inc(loaded, 16)
            act.dma_start(ffn_rows[:], A["state_ffn_conv"][0].rearrange("b i c -> (b i) c")).then_inc(ffn_landed, 16)
            ahead(act, "rest")

        @block.gpsimd
        def _(pool):
            step = stepper(pool, pool_step)
            step(nc.gpsimd.memset(ones[:], 1.0))
            step(nc.gpsimd.memset(C.eps[:], EPS))
            same_block(nc, step, ident[:], ones, 0)
            pool.sem_inc(ready, 1)

        @block.tensor
        def _(pe):
            pe.wait_ge(ready, 2)
            nc.tensor.transpose(tp[:, 0:91], rows_a[:], ident[0:91, 0:91])
            nc.tensor.transpose(tp[:, 91:179], rows_b[:], ident[0:88, 0:88])
            nc.tensor.transpose(tp[:, 179:223], rows_c[:], ident[0:44, 0:44]).then_inc(turned, 1)
            pe.wait_ge(ffn_landed, 16)
            for n in range(2 * NF):
                ins = nc.tensor.transpose(ffn_banks[:, n // 22, n % 22, :], ffn_rows[:, P * n:P * n + P], ident[0:16, 0:16])
            ins.then_inc(ffn_turned, 1)

        @block.vector
        def _(dve):
            dve.wait_ge(turned, 1)
            nc.vector.tensor_copy(C.vec[:], tp[:, 0:V_ALL]).then_inc(copied, 1)
            dve.wait_ge(ffn_turned, 1)
            for i in range(2):
                nc.vector.tensor_copy(ffn_old[:, 22 * i:22 * i + 22, :], ffn_banks[:, i]).then_inc(copied, 1)
            dve.wait_ge(copied, 3)


def stepper(pool, sem):
    steps = 0

    def step(ins):
        nonlocal steps
        ins.then_inc(sem, 1)
        steps += 1
        pool.wait_ge(sem, steps)
    return step


def same_block(nc, step, out, ones, k):
    s = 1 << k
    v = out.rearrange("p (b c) -> p b c", c=s)
    one = ones[:].rearrange("p (b c) -> p b c", c=s)
    step(nc.gpsimd.affine_select(out=v, in_=one, compare_op=ALU.is_ge, fill=0.0, base=0,
                                 pattern=[[-s, P // s], [0, s]], channel_multiplier=1))
    step(nc.gpsimd.affine_select(out=v, in_=v, compare_op=ALU.is_ge, fill=0.0, base=s - 1,
                                 pattern=[[s, P // s], [0, s]], channel_multiplier=-1))


def masks(nc, C, blocks, pool, sem):
    step = stepper(pool, sem)
    for k in range(1, 7):
        same_block(nc, step, blocks[:, k, :], C.ones, k)
    step(nc.gpsimd.tensor_copy(blocks[:, 0, :], C.ident[:]))
    step(nc.gpsimd.tensor_copy(C.pair_ones[:], blocks[:, 6, :]))
    for kind, k in ((0, 6), (1, 4)):
        step(nc.gpsimd.affine_select(out=C.upto[:, kind, :], in_=blocks[:, k, :], compare_op=ALU.is_ge,
                                     fill=0.0, base=0, pattern=[[1, P]], channel_multiplier=-1))
        step(nc.gpsimd.affine_select(out=C.after[:, kind, :], in_=blocks[:, k, :], compare_op=ALU.is_gt,
                                     fill=0.0, base=0, pattern=[[-1, P]], channel_multiplier=1))
    for k in range(6):
        step(nc.gpsimd.tensor_tensor(C.level[:, k, :], blocks[:, k + 1, :], blocks[:, k, :], ALU.subtract))
        step(nc.gpsimd.affine_select(out=C.level[:, k, :], in_=C.level[:, k, :], compare_op=ALU.is_gt,
                                     fill=0.0, base=0, pattern=[[-1, P]], channel_multiplier=1))
    step(nc.gpsimd.memset(C.hide[:], 0.0))
    for kind in range(2):
        step(nc.gpsimd.memset(C.hide[0:64, kind, 192:256], NEG))
        step(nc.gpsimd.memset(C.hide[64:128, kind, 0:64], NEG))
    step(nc.gpsimd.memset(C.hide[:, 1, 0:128], NEG))
    step(nc.gpsimd.tensor_scalar(C.hide[:, 2, 128:256], blocks[:, 4, :], 1.0, -NEG, ALU.subtract, ALU.mult))
    step(nc.gpsimd.tensor_copy(C.seq_mask[:], blocks[:, 4, :].rearrange("p (b s) -> p b s", s=TB)[:, :, 0]))



def norm_turn(nc, C, tag, src, n_tiles, gain_col, out, out_lo=None, landed=(), ahead=None, with_masks=False):
    with C.phase() as ph:
        group = 3 if n_tiles % 3 == 0 else n_tiles
        ng = n_tiles // group
        W = group * P
        squares = ph.sb(f"{tag}_squares", [P, D])
        sums = ph.sb(f"{tag}_sums", [P, n_tiles])
        root = ph.sb(f"{tag}_root", [P, n_tiles])
        inv = ph.sb(f"{tag}_inv", [P, n_tiles])
        xn = ph.sb(f"{tag}_xn", [P, 2, group, D])
        banks = ph.psum(f"{tag}_banks", [P, 4, 512])
        blocks = ph.sb("same_block", [P, 7, P]) if with_masks else None
        summed, rooted, inverted, scaled, turned, high, low = (
            ph.sem(f"{tag}_{n}") for n in ("summed", "rooted", "inverted", "scaled", "turned", "high", "low"))
        block = ph.block()

        @block.sync
        def _(sp):
            if ahead:
                ahead(sp)

        @block.gpsimd
        def _(pool):
            if with_masks:
                masks(nc, C, blocks, pool, ph.sem("mask_steps"))

        @block.scalar
        def _(act):
            def factors(g):
                for t in range(g * group, (g + 1) * group):
                    if landed:
                        act.wait_ge(landed[t], 16)
                    if t:
                        act.wait_ge(summed, t)
                    nc.scalar.activation(squares[:], src[:, t, :], ACT.Square, accum_out=sums[:, t:t + 1]
                                         ).then_inc(summed, 1)
                act.wait_ge(summed, (g + 1) * group)
                ts = slice(g * group, (g + 1) * group)
                nc.scalar.activation(root[:, ts], sums[:, ts], ACT.Sqrt, scale=1.0 / D, bias=C.eps[:, 0:1]
                                     ).then_inc(rooted, 1)

            def turned_out(g):
                for k in range(KD):
                    i = g * KD + k
                    act.wait_ge(turned, i + 1)
                    nc.scalar.activation(out[:, k, g * W:g * W + W], banks[:, i % 4, 0:W], ACT.Copy,
                                         scale=C.vec[:, gain_col + k:gain_col + k + 1]).then_inc(high, 1)

            factors(0)
            for g in range(ng):
                if g + 1 < ng:
                    factors(g + 1)
                turned_out(g)

        @block.vector
        def _(dve):
            def scale(g):
                ts = slice(g * group, (g + 1) * group)
                dve.wait_ge(rooted, g + 1)
                nc.vector.reciprocal(inv[:, ts], root[:, ts]).then_inc(inverted, 1)
                dve.wait_ge(inverted, g + 1)
                if g >= 2:
                    dve.wait_ge(turned, KD * (g - 1))
                for t in range(g * group, (g + 1) * group):
                    nc.vector.tensor_scalar(xn[:, g % 2, t % group, :], src[:, t, :], inv[:, t:t + 1], None,
                                            ALU.mult).then_inc(scaled, 1)
            scale(0)
            for g in range(ng):
                if g + 1 < ng:
                    scale(g + 1)
                if out_lo is not None:
                    for k in range(KD):
                        i = g * KD + k
                        dve.wait_ge(high, i + 1)
                        nc.vector.scalar_tensor_tensor(
                            out_lo[:, k, g * W:g * W + W], banks[:, i % 4, 0:W], C.vec[:, gain_col + k:gain_col + k + 1],
                            out[:, k, g * W:g * W + W].bitcast(F32), ALU.mult, ALU.subtract).then_inc(low, 1)

        @block.tensor
        def _(pe):
            for i in range(ng * KD):
                g, k = divmod(i, KD)
                pe.wait_ge(scaled, group * (g + 1))
                if i >= 4:
                    pe.wait_ge(high if out_lo is None else low, i - 3)
                for j in range(group):
                    ins = nc.tensor.transpose(banks[:, i % 4, j * P:j * P + P], xn[:, g % 2, j, k * P:k * P + P],
                                              C.ident[:])
                ins.then_inc(turned, 1)



class FeatureWeights:
    RING = 2

    def __init__(self, C, tag, w_dram, columns):
        self.raw = C.sb(f"{tag}_w_raw", [P, self.RING, KD, P], side="right")
        self.landed = [C.sem(f"{tag}_w_landed{r}") for r in range(self.RING)]
        self.dram = w_dram.rearrange("(k p) c -> p k c", p=P)
        self.columns = columns

    def load(self, sp, n):
        at = 0
        for c0, width in self.columns[n]:
            sp.dma_start(self.raw[:, n % self.RING, :, at:at + width], self.dram[:, :, c0:c0 + width]
                         ).then_inc(self.landed[n % self.RING], 16)
            at += width

    def load_first(self, sp):
        for n in range(self.RING):
            self.load(sp, n)

    def wait(self, engine, n):
        parts = sum(len(self.columns[m]) for m in range(n % self.RING, n + 1, self.RING))
        engine.wait_ge(self.landed[n % self.RING], 16 * parts)


def column_tiles():
    z0 = CONV_CH
    ab0 = z0 + 512
    sq0 = ab0 + 8
    sk0, sv0 = sq0 + 256, sq0 + 384
    b0 = sv0 + 128
    c0, h0 = b0 + 256, b0 + 512
    tiles = []
    for i in range(2):
        tiles += [("sc_c", i, [(c0 + P * i, P)]), ("sc_h", i, [(h0 + P * i, P)]), ("sc_b", i, [(b0 + P * i, P)])]
    tiles += [("swa_q", i, [(sq0 + 64 * i, 64), (sq0 + 128 + 64 * i, 64)]) for i in range(2)]
    tiles += [("swa_k", 0, [(sk0, P)]), ("swa_v", 0, [(sv0, P)])]
    for h in range(HEADS):
        tiles += [("z", h, [(z0 + P * h, P)])] + [("conv", HEADS * j + h, [(512 * j + P * h, P)]) for j in range(3)]
    return tiles + [("gate", 0, [(ab0, 8)])]


SPILL = {**{("z", h): h for h in range(HEADS)}, ("swa_q", 0): 4, ("swa_q", 1): 5, ("swa_k", 0): 6, ("swa_v", 0): 7,
         ("sc_b", 0): 8, ("sc_b", 1): 9}


def in_projection(nc, C, A, O, M, hi, lo, weights, spill):
    tiles = column_tiles()
    n_tiles = len(tiles)
    RING = weights.RING
    at = {(kind, i): n for n, (kind, i, _) in enumerate(tiles)}
    by_act = [kind not in ("sc_h", "sc_b") for kind, _, _ in tiles]
    act_count = [sum(by_act[:n + 1]) for n in range(n_tiles)]
    dve_count = [n + 1 - act_count[n] for n in range(n_tiles)]
    spilled = [n for n, (kind, i, _) in enumerate(tiles) if (kind, i) in SPILL]
    convs = [(n, i) for n, (kind, i, _) in enumerate(tiles) if kind == "conv"]
    L4, L3 = xp_len(4), xp_len(3)
    with C.phase() as ph:
        w_hi, w_lo = (ph.sb(f"w_in_{n}", [P, 2, KD, P], F32R) for n in ("hi", "lo"))
        xp = ph.sb("conv_in", [P, 2, L4])
        y = ph.sb("conv_out", [P, L4])
        sc_c = ph.sb("sc_c", [P, T])
        stage = ph.sb("spill_stage", [P, 2, T])
        flat = xp[:].rearrange("p a b -> p (a b)")
        old_rows, old_sc_rows = flat[0:24, 0:CONV_CH], flat[0:16, CONV_CH:CONV_CH + 256]
        old = ph.sb("gdn_old", [P, 12 * 24 + 2 * 16])
        tail = ph.sb("tail", [P, 2, 27])
        new_s = ph.sb("new_sample_rows", [24, 2, P])
        new_p = ph.sb("new_prompt_rows", [3, 2, P])
        banks = ph.psum("proj_banks", [P, 2 * NP, 512])
        state_in = ph.psum("state_in", [P, 512])
        state_out = ph.psum("state_out", [P, 512])
        high, split, staged = (ph.sem(f"c_{n}") for n in ("high", "split", "staged"))
        stored = C.conv_stored
        (rows_landed, projected, act_freed, dve_freed, old_turned, old_copied, padded, conv_step, conv_done,
         silu_done, state_turned, state_saved, sc_done, gathered) = (
            ph.sem(f"c_{n}") for n in (
                "rows_landed", "projected", "act_freed", "dve_freed", "old_turned", "old_copied", "padded",
                "conv_step", "conv_done", "silu_done", "state_turned", "state_saved", "sc_done", "gathered"))
        q = M["qkv"]
        padded_of = {("sc", 0): 0, ("sc", 1): 1, **{("conv", i): 2 + m for m, (_, i) in enumerate(convs)}}
        block = ph.block()

        @block.sync
        def _(sp):
            sp.dma_start(old_rows, A["state_gdn_conv"][0].rearrange("b i c -> (b i) c")).then_inc(rows_landed, 16)
            sp.dma_start(old_sc_rows, A["state_sc_conv"][0].rearrange("b i c -> (b i) c")).then_inc(rows_landed, 16)

            def store_spilled(n):
                if n in spilled:
                    m = spilled.index(n)
                    sp.wait_ge(staged, m + 1)
                    sp.dma_start(spill[SPILL[tiles[n][0:2]]], stage[:, m % 2, :]).then_inc(C.spilled[m % 2], 16)

            for n in range(RING, n_tiles):
                sp.wait_ge(split, n - RING + 1)
                weights.load(sp, n)
                if n >= 4:
                    store_spilled(n - 4)
            for n in range(n_tiles - 4, n_tiles):
                store_spilled(n)
            for r in range(2):
                sp.wait_ge(C.spilled[r], 16 * (len(spilled) // 2))

        def stage_slot(engine, n):
            m = spilled.index(n)
            if m >= 2:
                engine.wait_ge(C.spilled[m % 2], 16 * (m // 2))
            if m:
                engine.wait_ge(staged, m)
            return stage[:, m % 2, :]

        def weights_low(dve, n):
            rows = sum(c for _, c in tiles[n][2])
            dve.wait_ge(high, n + 1)
            nc.vector.tensor_tensor(w_lo[:, n % 2, :, 0:rows], weights.raw[:, n % RING, :, 0:rows],
                                    w_hi[:, n % 2, :, 0:rows].bitcast(F32), ALU.subtract).then_inc(split, 1)

        @block.tensor
        def _(pe):
            pe.wait_ge(rows_landed, 32)
            for i in range(12):
                nc.tensor.transpose(state_in[:, 24 * i:24 * i + 24], old_rows[:, P * i:P * i + P], C.ident[0:24, 0:24])
            for i in range(2):
                ins = nc.tensor.transpose(state_in[:, 288 + 16 * i:304 + 16 * i], old_sc_rows[:, P * i:P * i + P],
                                          C.ident[0:16, 0:16])
            ins.then_inc(old_turned, 1)

            def turn_state(m):
                W = 3 if m < 2 else 4
                pe.wait_ge(gathered, m + 1)
                if m:
                    pe.wait_ge(state_saved, m)
                nc.tensor.transpose(state_out[0:W - 1, 0:P], tail[:, m % 2, 24:24 + W - 1], C.ident[:])
                nc.tensor.transpose(state_out[0:NB * (W - 1), P:2 * P], tail[:, m % 2, 0:NB * (W - 1)],
                                    C.ident[:]).then_inc(state_turned, 1)

            for n, (kind, i, cols) in enumerate(tiles):
                rows = sum(c for _, c in cols)
                pe.wait_ge(split, n + 1)
                if n >= 2:
                    if by_act[n - 2]:
                        pe.wait_ge(act_freed, act_count[n - 2])
                    else:
                        pe.wait_ge(dve_freed, dve_count[n - 2])
                for piece in range(NP):
                    for k in range(KD):
                        for m, (w, x) in enumerate(((w_hi, hi), (w_hi, lo), (w_lo, hi))):
                            ins = nc.tensor.matmul(banks[0:rows, (n % 2) * NP + piece, 0:TC], w[:, n % 2, k, 0:rows],
                                                   x[:, k, piece * TC:piece * TC + TC], start=(k == 0 and m == 0),
                                                   stop=(k == KD - 1 and m == 2))
                    ins.then_inc(projected, 1)
                if n >= 1 and tiles[n - 1][0] == "sc_h":
                    turn_state(tiles[n - 1][1])
                if n >= 1 and tiles[n - 1][0] == "conv":
                    turn_state(padded_of["conv", tiles[n - 1][1]])

        def pieces(n):
            return [((n % 2) * NP + p, p * TC, TC if p < 2 else PP) for p in range(NP)]

        @block.scalar
        def _(act):
            def weights_high(n):
                rows = sum(c for _, c in tiles[n][2])
                weights.wait(act, n)
                if n >= 2:
                    act.wait_ge(projected, NP * (n - 1))
                nc.scalar.activation(w_hi[:, n % 2, :, 0:rows], weights.raw[:, n % RING, :, 0:rows], ACT.Copy
                                     ).then_inc(high, 1)

            def silu(m):
                n, i = convs[m]
                act.wait_ge(conv_done, m + 1)
                nc.scalar.activation(q[:, i, 0:TP], y[:, 0:TP], ACT.Silu)
                nc.scalar.activation(seqs(q[:, i, TP:T]), xp_sample(y, 4, 0, TB), ACT.Silu).then_inc(silu_done, 1)

            weights_high(0)
            weights_high(1)
            m = 0
            for n, (kind, i, cols) in enumerate(tiles):
                rows = sum(c for _, c in cols)
                if by_act[n]:
                    for p, (bank, c0, cn) in enumerate(pieces(n)):
                        act.wait_ge(projected, NP * n + p + 1)
                        if kind == "conv":
                            pad = padded_of[kind, i]
                            if p == 0:
                                act.wait_ge(padded, pad + 1)
                            ins = nc.scalar.activation(xp[:, pad % 2, 3 + c0:3 + c0 + cn], banks[:, bank, 0:cn], ACT.Copy)
                            if p == 2:
                                ins = nc.scalar.activation(xp_sample(xp[:, pad % 2, :], 4, 3, TB),
                                                           seqs(banks[:, bank, PP:TC]), ACT.Copy)
                        elif kind == "z":
                            if p == 0:
                                to = stage_slot(act, n)
                            ins = nc.scalar.activation(to[:, p * TC:p * TC + TC], banks[:, bank, 0:TC], ACT.Silu)
                        else:
                            if p == 0:
                                to = {"sc_c": sc_c[:], "gate": M["gate"][:]}.get(kind)
                                to = stage_slot(act, n) if to is None else to
                            if kind == "sc_c" and i:
                                act.wait_ge(dve_freed, dve_count[at["sc_h", 0]])
                            ins = nc.scalar.activation(to[0:rows, p * TC:p * TC + TC], banks[0:rows, bank, 0:TC], ACT.Copy)
                    ins.then_inc(act_freed, 1)
                    if n in spilled:
                        act.wait_ge(act_freed, act_count[n])
                        act.sem_inc(staged, 1)
                if n + 2 < n_tiles:
                    weights_high(n + 2)
                if n >= 1 and tiles[n - 1][0] == "conv":
                    silu(m)
                    m += 1

        @block.gpsimd
        def _(pool):
            def store_state(m):
                W = 3 if m < 2 else 4
                i = m if m < 2 else convs[m - 2][1]
                to_p, to_s = (O["p_sc_conv"], O["s_sc_conv"]) if m < 2 else (O["p_gdn_conv"], O["s_gdn_conv"])
                pool.wait_ge(state_saved, m + 1)
                pool.dma_start(to_p[0, 0][:, P * i:P * i + P], new_p[0:W - 1, m % 2, :]).then_inc(stored[m % 2], 16)
                pool.dma_start(to_s[0].rearrange("b i c -> (b i) c")[:, P * i:P * i + P],
                               new_s[0:NB * (W - 1), m % 2, :]).then_inc(stored[m % 2], 16)

            for pad in range(14):
                W = 3 if pad < 2 else 4
                buf = xp[:, pad % 2, :]
                if pad == 0:
                    pool.wait_ge(old_copied, 1)
                if pad >= 2:
                    if pad < 4:
                        pool.wait_ge(sc_done, pad - 1)
                    else:
                        pool.wait_ge(conv_done, pad - 3)
                if pad < 2:
                    was = old[:, 288 + 16 * pad:304 + 16 * pad]
                else:
                    i = convs[pad - 2][1]
                    was = old[:, 24 * i:24 * i + 24]
                nc.gpsimd.memset(buf[:, 0:W - 1], 0.0)
                nc.gpsimd.tensor_copy(xp_sample(buf, W, 0, W - 1), was.rearrange("p (b i) -> p b i", b=NB)
                                      ).then_inc(padded, 1)
                if pad >= 2:
                    store_state(pad - 2)
            store_state(12)
            store_state(13)
            for r in range(2):
                pool.wait_ge(stored[r], 32 * 7)

        @block.vector
        def _(dve):
            steps = 0

            def taps(W, pad, vec0, stride):
                nonlocal steps
                L = xp_len(W) - (W - 1)
                buf = xp[:, pad % 2, :]
                for j in range(W):
                    wt = C.vec[:, vec0 + stride * j:vec0 + stride * j + 1]
                    if j == 0:
                        ins = nc.vector.tensor_scalar(y[:, 0:L], buf[:, 0:L], wt, None, ALU.mult)
                    else:
                        dve.wait_ge(conv_step, steps)
                        ins = nc.vector.scalar_tensor_tensor(y[:, 0:L], buf[:, j:j + L], wt, y[:, 0:L],
                                                             ALU.mult, ALU.add)
                    if j < W - 1:
                        ins.then_inc(conv_step, 1)
                        steps += 1
                return ins

            def gather_tail(m):
                W = 3 if m < 2 else 4
                if m >= 2:
                    dve.wait_ge(state_turned, m - 1)
                nc.vector.tensor_copy(tail[:, m % 2, 0:NB * (W - 1)].rearrange("p (b i) -> p b i", b=NB),
                                      xp_sample(xp[:, m % 2, :], W, TB, W - 1))
                nc.vector.tensor_copy(tail[:, m % 2, 24:24 + W - 1], xp[:, m % 2, TP:TP + W - 1]).then_inc(gathered, 1)

            def save_state(m):
                W = 3 if m < 2 else 4
                dve.wait_ge(state_turned, m + 1)
                if m >= 2:
                    dve.wait_ge(stored[m % 2], 32 * (m // 2))
                nc.vector.tensor_copy(new_p[0:W - 1, m % 2, :], state_out[0:W - 1, 0:P])
                nc.vector.tensor_copy(new_s[0:NB * (W - 1), m % 2, :], state_out[0:NB * (W - 1), P:2 * P]
                                      ).then_inc(state_saved, 1)

            dve.wait_ge(old_turned, 1)
            nc.vector.tensor_copy(old[:], state_in[:, 0:320]).then_inc(old_copied, 1)
            weights_low(dve, 0)
            weights_low(dve, 1)
            for n, (kind, i, cols) in enumerate(tiles):
                if n + 2 < n_tiles and kind != "sc_b":
                    weights_low(dve, n + 2)
                if kind == "sc_h":
                    dve.wait_ge(act_freed, act_count[at["sc_c", i]])
                    dve.wait_ge(padded, i + 1)
                    for p, (bank, c0, cn) in enumerate(pieces(n)):
                        dve.wait_ge(projected, NP * n + p + 1)
                        nc.vector.tensor_tensor(xp[:, i, 2 + c0:2 + c0 + cn], banks[:, bank, 0:cn], sc_c[:, c0:c0 + cn],
                                                ALU.mult)
                    nc.vector.tensor_tensor(xp_sample(xp[:, i, :], 3, 2, TB), seqs(banks[:, bank, PP:TC]),
                                            seqs(sc_c[:, TP:T]), ALU.mult).then_inc(dve_freed, 1)
                    dve.wait_ge(dve_freed, dve_count[n])
                    gather_tail(i)
                    taps(3, i, V_SC + i, 2).then_inc(sc_done, 1)
                    dve.wait_ge(sc_done, i + 1)
                elif kind == "sc_b":
                    save_state(i)
                    to = stage_slot(dve, n)
                    for p, (bank, c0, cn) in enumerate(pieces(n)):
                        dve.wait_ge(projected, NP * n + p + 1)
                        nc.vector.tensor_tensor(to[:, c0:c0 + cn], banks[:, bank, 0:cn], y[:, c0:c0 + cn], ALU.mult)
                    nc.vector.tensor_tensor(seqs(to[:, TP:T]), seqs(banks[:, bank, PP:TC]),
                                            xp_sample(y, 3, 0, TB), ALU.mult).then_inc(dve_freed, 1)
                    dve.wait_ge(dve_freed, dve_count[n])
                    dve.sem_inc(staged, 1)
                    weights_low(dve, n + 2)
                elif kind == "conv":
                    pad = padded_of[kind, i]
                    dve.wait_ge(act_freed, act_count[n])
                    if pad >= 3:
                        dve.wait_ge(silu_done, pad - 2)
                    gather_tail(pad)
                    taps(4, pad, V_GC + i, 12).then_inc(conv_done, 1)
                    save_state(pad)



def column_norms(nc, C, tag, items, batch_size, ahead=None):
    RING, BATCH = 4, batch_size
    n_items = len(items)
    with C.phase() as ph:
        squares = ph.sb(f"{tag}_squares", [P, RING, T])
        logs = ph.sb(f"{tag}_logs", [P, n_items, T])
        banks = ph.psum(f"{tag}_sums", [P, 2 * NP, 512])
        squared_pool, squared_dve, summed, logged, rooted, normed = (ph.sem(f"{tag}_{n}") for n in (
            "squared_pool", "squared_dve", "summed", "logged", "rooted", "normed"))
        squares_of = [(m, j) for m, it in enumerate(items) for j in range(len(it[0]))]
        through = [sum(len(it[0]) for it in items[:m + 1]) for m in range(n_items)]
        by_pool = [n % 3 == 0 for n in range(len(squares_of))]

        def square(engine, wait, n, done):
            m, j = squares_of[n]
            if n >= RING:
                wait.wait_ge(summed, n - RING + 1)
            x = items[m][0][j]
            engine.tensor_tensor(squares[:, n % RING, :], x, x, ALU.mult).then_inc(done, 1)

        block = ph.block()

        @block.sync
        def _(sp):
            if ahead:
                ahead(sp)

        @block.gpsimd
        def _(pool):
            for n, mine in enumerate(by_pool):
                if mine:
                    square(nc.gpsimd, pool, n, squared_pool)

        @block.tensor
        def _(pe):
            for n, (m, j) in enumerate(squares_of):
                if by_pool[n]:
                    pe.wait_ge(squared_pool, sum(by_pool[:n + 1]))
                else:
                    pe.wait_ge(squared_dve, n + 1 - sum(by_pool[:n + 1]))
                if j == 0 and m >= 2:
                    pe.wait_ge(logged, m - 1)
                for p in range(NP):
                    ins = nc.tensor.matmul(banks[:, (m % 2) * NP + p, 0:TC], items[m][2],
                                           squares[:, n % RING, p * TC:p * TC + TC], start=(j == 0),
                                           stop=(j == len(items[m][0]) - 1), skip_group_check=True)
                ins.then_inc(summed, 1)

        @block.scalar
        def _(act):
            for m0 in range(0, n_items, BATCH):
                batch = range(m0, min(m0 + BATCH, n_items))
                for m in batch:
                    act.wait_ge(summed, through[m])
                    for p in range(NP):
                        ins = nc.scalar.activation(logs[:, m, p * TC:p * TC + TC],
                                                   banks[:, (m % 2) * NP + p, 0:TC], ACT.Ln, scale=items[m][3],
                                                   bias=C.eps[:, 0:1])
                    ins.then_inc(logged, 1)
                for m in batch:
                    act.wait_ge(logged, m + 1)
                    at = logs[:, m, :]
                    nc.scalar.activation(at, at, ACT.Exp, scale=-0.5).then_inc(rooted, 1)

        @block.vector
        def _(dve):
            def squares_through(m):
                nonlocal done
                for n in range(done, through[min(m, n_items - 1)]):
                    if not by_pool[n]:
                        square(nc.vector, dve, n, squared_dve)
                done = max(done, through[min(m, n_items - 1)])

            done = 0
            for m0 in range(0, n_items, BATCH):
                squares_through(m0 + BATCH - 1)
                for m in range(m0, min(m0 + BATCH, n_items)):
                    squares_through(m + 4)
                    dve.wait_ge(rooted, m + 1)
                    for x, out, gain in zip(items[m][0], items[m][1], items[m][4]):
                        nc.vector.scalar_tensor_tensor(out, x, gain, logs[:, m, :], ALU.mult, ALU.mult
                                                       ).then_inc(normed, 1)


def delta_norms(nc, C, M):
    qkv = M["qkv"]
    items = [([qkv[:, h, :]], [qkv[:, h, :]], C.ones[:], 1.0, [float(P) ** -0.5]) for h in range(HEADS)]
    items += [([qkv[:, 4 + h, :]], [qkv[:, 4 + h, :]], C.ones[:], 1.0, [1.0]) for h in range(HEADS)]
    column_norms(nc, C, "gn", items, 6)



def gates(nc, C, M):
    with C.phase() as ph:
        raw, pos, neg, e, l = (ph.sb(f"gate_{n}", [P, NT, HEADS]) for n in ("raw", "pos", "neg", "e", "l"))
        eb = ph.sb("gate_eb", [P, NT, HEADS])
        rate = ph.sb("gate_rate", [P, HEADS])
        ps = ph.psum("gate_rows", [P, NT, 8])
        sums = ph.psum("gate_sums", [P, 2, NT, HEADS])
        turned, act_step, dve_step, summed = (ph.sem(f"g_{n}") for n in ("turned", "act_step", "dve_step", "summed"))
        g, beta, up, tail, bu = (M[n] for n in ("g", "beta", "up", "tail", "beta_up"))
        block = ph.block()

        @block.tensor
        def _(pe):
            for t in range(NT):
                ins = nc.tensor.transpose(ps[:, t, :], M["gate"][:, P * t:P * t + P], C.ident[0:8, 0:8])
            ins.then_inc(turned, 1)
            pe.wait_ge(dve_step, 6)
            for kind, a, b in ((0, 0, PT), (1, PT, NT)):
                nc.tensor.matmul(sums[:, 0, a:b, :], C.upto[:, kind, :], g[:, a:b, :], start=True, stop=True)
                ins = nc.tensor.matmul(sums[:, 1, a:b, :], C.after[:, kind, :], g[:, a:b, :], start=True, stop=True)
            ins.then_inc(summed, 1)

        @block.scalar
        def _(act):
            act.wait_ge(dve_step, 1)
            nc.scalar.activation(neg[:], raw[:], ACT.Abs).then_inc(act_step, 1)
            act.wait_ge(act_step, 1)
            nc.scalar.activation(e[:], neg[:], ACT.Exp, scale=-1.0).then_inc(act_step, 1)
            nc.scalar.activation(eb[:], ps[:, :, 4:8], ACT.Exp, scale=-1.0).then_inc(act_step, 1)
            nc.scalar.activation(rate[:], C.a_log[:], ACT.Exp).then_inc(act_step, 1)
            act.wait_ge(act_step, 2)
            nc.scalar.activation(l[:], e[:], ACT.Ln, bias=C.ones[:, 0:1]).then_inc(act_step, 1)
            act.wait_ge(summed, 1)
            nc.scalar.activation(up[:], sums[:, 0], ACT.Exp).then_inc(act_step, 1)
            nc.scalar.activation(tail[:], sums[:, 1], ACT.Exp).then_inc(act_step, 1)
            act.wait_ge(act_step, 7)

        @block.vector
        def _(dve):
            dve.wait_ge(turned, 1)
            nc.vector.tensor_tensor(raw[:], ps[:, :, 0:4], each(C.dt_bias[:], NT), ALU.add).then_inc(dve_step, 1)
            dve.wait_ge(dve_step, 1)
            nc.vector.tensor_scalar(pos[:], raw[:], 0.0, None, ALU.max).then_inc(dve_step, 1)
            dve.wait_ge(act_step, 3)
            nc.vector.tensor_scalar(eb[:], eb[:], 1.0, None, ALU.add).then_inc(dve_step, 1)
            dve.wait_ge(dve_step, 3)
            nc.vector.reciprocal(beta[:], eb[:]).then_inc(dve_step, 1)
            dve.wait_ge(act_step, 5)
            nc.vector.tensor_tensor(pos[:], pos[:], l[:], ALU.add).then_inc(dve_step, 1)
            dve.wait_ge(dve_step, 5)
            nc.vector.scalar_tensor_tensor(g[:], pos[:], -1.0, each(rate[:], NT), ALU.mult, ALU.mult
                                           ).then_inc(dve_step, 1)
            dve.wait_ge(act_step, 6)
            nc.vector.tensor_tensor(bu[:], beta[:], up[:], ALU.mult).then_inc(dve_step, 1)
            dve.wait_ge(dve_step, 7)



def delta_net(nc, C, A, O, M, load_spilled):
    qkv, g, beta, tail, bu = M["qkv"], M["g"], M["beta"], M["tail"], M["beta_up"]
    LEVELS = 6
    UPD = 2 + 2 * (LEVELS - 1)
    ZBANK, UBANK = "ac", "bd"

    def upd_after(t, k, j):
        return UPD * t + (2 if k == 0 else 2 + 2 * (k - 1) + j + 1)

    def z_after(t, k, j):
        return (2 * LEVELS - 1) * t + (1 if k == 0 else 2 * k + j)

    def level_after(t, k, j):
        return 2 * ((LEVELS - 1) * t + k - 1) + j + 1

    STEPS = (("p", 0), ("w", 0), ("p", 1), ("r", 0), ("p", 2), ("w", 1), ("p", 3), ("r", 1),
             ("p", 4), ("p", 5), ("p", 6), ("p", 7), ("p", 8))
    N = 2 * PT

    with C.phase() as ph:
        G = ph.sb("decay_steps", [P, HEADS, P])
        dec, decT = ph.sb("decay", [P, HEADS, P]), ph.sb("decay_t", [P, HEADS, P])
        E = ph.sb("decay_up", [P, 2, HEADS, P])
        low = ph.sb("low", [P, HEADS, P])
        pair = ph.sb("low_pairs", [P, 2, HEADS, P])
        inv = ph.sb("inv", [P, 2, 2, 2, P])
        ZT = ph.sb("inv_low_t", [P, 2, 2, P])

        def XT(h):
            return inv[:, h // 2, 0, h % 2, :]

        def X(h):
            return inv[:, h // 2, 1, h % 2, :]

        rk, rv = ph.sb("rhs_k", [P, HEADS, P]), ph.sb("rhs_v", [P, HEADS, P])
        kd, qk, qg, u0, wT = (ph.sb(n, [P, 2, HEADS, P]) for n in ("k_tail", "qk_t", "q_up", "u0", "w_t"))
        S, Sg, u = (ph.sb(n, [P, HEADS, P]) for n in ("state", "state_decayed", "u"))
        S0 = ph.sb("sample_state", [P, NB, HEADS, P])
        one = ph.sb("one_sample", [P, 2, HEADS, P])
        bank = {n: ph.psum(f"gdn_bank_{n}", [P, HEADS, P]) for n in ("a", "b", "c", "d", "e", "u", "o", "s")}
        (g_ready, sums_done, exp_done, products, low_done, low_scaled, qk_raw, qk_done, qg_done, rhs_done, masked, upd,
         z_done, z_copied, x_done, solved, solved_copied, zeroed, sg_done, ws_done, u_done, os_done,
         s_product, o_copied, s_done, cleared, one_ready, one_used, kdm_done, sample_product, sample_decayed,
         sample_done, s0_landed) = (ph.sem(f"d_{n}") for n in (
             "g_ready", "sums_done", "exp_done", "products", "low_done", "low_scaled", "qk_raw", "qk_done", "qg_done",
             "rhs_done", "masked", "upd", "z_done", "z_copied", "x_done", "solved", "solved_copied",
             "zeroed", "sg_done", "ws_done", "u_done", "os_done", "s_product", "o_copied", "s_done", "cleared",
             "one_ready", "one_used", "kdm_done", "sample_product", "sample_decayed", "sample_done", "s0_landed"))
        stored = C.state_stored

        def cols(t):
            return slice(P * t, P * t + P)

        def run(prep, scan, sample):
            for t in range(NT):
                for what, s in STEPS:
                    if what == "p":
                        prep(t, s)
                    elif t >= 1:
                        scan(t - 1, s, what)
            sample(NT - 1)

        block = ph.block()

        @block.sync
        def _(sp):
            for b in range(NB):
                sp.dma_start(S0[:, b], A["state_gdn"][0, b].rearrange("h k v -> k h v")).then_inc(s0_landed, 16)
            load_spilled(sp)
            sp.wait_ge(s_done, N)
            sp.dma_start(O["p_gdn"][0, 0].rearrange("h k v -> k h v"), S[:]).then_inc(stored, 16)
            for b in range(NB):
                sp.wait_ge(sample_done, b + 1)
                sp.dma_start(O["s_gdn"][0, b].rearrange("h k v -> k h v"), S0[:, b]).then_inc(stored, 16)
            sp.wait_ge(stored, 16 * (NB + 1))
            sp.wait_ge(C.spill_landed, 16 * 5)

        @block.tensor
        def _(pe):
            def prep(t, s):
                kind = t // PT
                if s == 0:
                    pe.wait_ge(g_ready, t + 1)
                    if t:
                        pe.wait_ge(upd, UPD * t)
                    for h in range(HEADS):
                        nc.tensor.matmul(bank["a"][:, h, :], G[:, h, :], C.after[:, kind, :], start=True, stop=True)
                    nc.tensor.matmul(bank["b"][:], C.after[:, kind, :], G[:], start=True, stop=True)
                    nc.tensor.matmul(bank["c"][:], C.ones[:], G[:], start=True, stop=True).then_inc(sums_done, 1)
                elif s == 1:
                    if t:
                        pe.wait_ge(solved_copied, 2 * t)
                    for h in range(HEADS):
                        k = qkv[:, 4 + h, cols(t)]
                        nc.tensor.matmul(bank["d"][:, h, :], k, k, start=True, stop=True)
                    for h in range(HEADS):
                        ins = nc.tensor.matmul(bank["e"][:, h, :], qkv[:, 4 + h, cols(t)], qkv[:, h, cols(t)],
                                               start=True, stop=True)
                    ins.then_inc(products, 1)
                    pe.wait_ge(exp_done, 3 * t + 3)
                    for h in range(HEADS):
                        nc.tensor.transpose(bank["a"][:, h, :], qkv[:, 4 + h, cols(t)], C.ident[:])
                    for h in range(HEADS):
                        ins = nc.tensor.transpose(bank["b"][:, h, :], qkv[:, 8 + h, cols(t)], C.ident[:])
                    ins.then_inc(products, 1)
                elif s == 2:
                    pe.wait_ge(masked, LEVELS * t + 1)
                    for h in range(HEADS):
                        ins = nc.tensor.transpose(bank["c"][:, h, :], pair[:, 0, h, :], C.ident[:])
                    ins.then_inc(z_done, 1)
                elif s < 2 + LEVELS:
                    k = s - 2
                    pe.wait_ge(masked, LEVELS * t + k + 1)
                    if k == 1:
                        pe.wait_ge(rhs_done, t + 1)
                        pe.wait_ge(low_done, t + 1)
                    for j in range(2):
                        pe.wait_ge(upd, upd_after(t, k - 1, j))
                        for i in range(2):
                            h = 2 * j + i
                            ins = nc.tensor.matmul(bank[ZBANK[j]][:, i, :], pair[:, k % 2, h, :], XT(h),
                                                   start=True, stop=True)
                        ins.then_inc(z_done, 1)
                    for j in range(2):
                        pe.wait_ge(z_copied, level_after(t, k, j))
                        for i in range(2):
                            ins = nc.tensor.matmul(bank[UBANK[j]][:, i, :], X(2 * j + i), ZT[:, j, i, :],
                                                   start=True, stop=True)
                        if k < LEVELS - 1:
                            for i in range(2):
                                ins = nc.tensor.matmul(bank[UBANK[j]][:, 2 + i, :], ZT[:, j, i, :], X(2 * j + i),
                                                       start=True, stop=True)
                        ins.then_inc(x_done, 1)
                else:
                    pe.wait_ge(upd, UPD * (t + 1))
                    pe.wait_ge(qk_raw, t + 1)
                    for h in range(HEADS):
                        ins = nc.tensor.matmul(bank["d"][:, h, :], XT(h), rv[:, h, :], start=True, stop=True)
                    ins.then_inc(solved, 1)
                    for h in range(HEADS):
                        ins = nc.tensor.matmul(bank["e"][:, h, :], rk[:, h, :], XT(h), start=True, stop=True)
                    ins.then_inc(solved, 1)

            def scan(t, c, what):
                n = 2 * t + c
                r, i = slice(64 * c, 64 * c + 64), t % 2
                if what == "w":
                    pe.wait_ge(solved_copied, 2 * t + 2)
                    if n:
                        pe.wait_ge(s_done, n)
                    else:
                        pe.wait_ge(zeroed, 2)
                    for h in range(HEADS):
                        ins = nc.tensor.matmul(bank["u"][r, h, :], wT[:, i, h, r], S[:, h, :], start=True, stop=True)
                    ins.then_inc(ws_done, 1)
                else:
                    pe.wait_ge(u_done, n + 1)
                    pe.wait_ge(qk_done, t + 1)
                    pe.wait_ge(qg_done, t + 1)
                    if n:
                        pe.wait_ge(o_copied, n)
                    for h in range(HEADS):
                        nc.tensor.matmul(bank["o"][:, h, 0:64], S[:, h, :], qg[:, i, h, r], start=True, stop=False)
                        ins = nc.tensor.matmul(bank["o"][:, h, 0:64], u[:, h, :], qk[:, i, h, r], start=False, stop=True)
                    ins.then_inc(os_done, 1)
                    for h in range(HEADS):
                        ins = nc.tensor.matmul(bank["s"][:, h, :], kd[r, i, h, :], u[r, h, :], start=True, stop=True)
                    ins.then_inc(s_product, 1)

            def sample(t):
                i = t % 2
                pe.wait_ge(s0_landed, 16 * NB)
                pe.wait_ge(s_done, N)
                pe.wait_ge(o_copied, N)
                for n in range(2 * NB):
                    b = n % NB
                    pe.wait_ge(one_ready, n + 1)
                    for h in range(HEADS):
                        if n < NB:
                            ins = nc.tensor.matmul(bank["u"][:, h, :], one[:, n % 2, h, :], S0[:, b, h, :],
                                                   start=(b + h == 0), stop=(b == NB - 1), skip_group_check=True)
                        else:
                            ins = nc.tensor.matmul(bank["o"][:, h, :], S0[:, b, h, :], one[:, n % 2, h, :],
                                                   start=(b + h == 0), stop=False, skip_group_check=True)
                    ins.then_inc(one_used, 1)
                pe.wait_ge(u_done, N + 1)
                pe.wait_ge(qk_done, t + 1)
                for h in range(HEADS):
                    ins = nc.tensor.matmul(bank["o"][:, h, :], u[:, h, :], qk[:, i, h, :], start=False, stop=True,
                                           skip_group_check=True)
                ins.then_inc(os_done, 1)
                for b in range(NB):
                    pe.wait_ge(kdm_done, b + 1)
                    if b >= 2:
                        pe.wait_ge(sample_done, b - 1)
                    for h in range(HEADS):
                        ins = nc.tensor.matmul(bank["de"[b % 2]][:, h, :], one[:, b % 2, h, :], u[:, h, :],
                                               start=True, stop=True)
                    ins.then_inc(sample_product, 1)

            run(prep, scan, sample)

        @block.scalar
        def _(act):
            def prep(t, s):
                if s == 0:
                    act.wait_ge(sums_done, t + 1)
                    if t:
                        act.wait_ge(low_done, t)
                        act.wait_ge(qk_raw, t)
                    if t >= 2:
                        act.wait_ge(s_done, 2 * t - 2)
                    nc.scalar.activation(dec[:], bank["a"][:], ACT.Exp).then_inc(exp_done, 1)
                    nc.scalar.activation(decT[:], bank["b"][:], ACT.Exp).then_inc(exp_done, 1)
                    nc.scalar.activation(E[:, t % 2], bank["c"][:], ACT.Exp).then_inc(exp_done, 1)
                elif 3 <= s < 2 + LEVELS:
                    for j in range(2):
                        act.wait_ge(z_done, z_after(t, s - 2, j))
                        nc.scalar.activation(ZT[:, j], bank[ZBANK[j]][:, 0:2, :], ACT.Copy).then_inc(z_copied, 1)
                elif s == 8:
                    for j, (to, b) in enumerate(((u0, "d"), (wT, "e"))):
                        act.wait_ge(solved, 2 * t + j + 1)
                        nc.scalar.activation(to[:, t % 2], bank[b][:], ACT.Copy).then_inc(solved_copied, 1)

            def scan(t, c, what):
                if what == "r":
                    act.wait_ge(os_done, 2 * t + c + 1)
                    nc.scalar.activation(qkv[:, 8:12, P * t + 64 * c:P * t + 64 * c + 64], bank["o"][:, :, 0:64],
                                         ACT.Copy).then_inc(o_copied, 1)

            def sample(t):
                act.wait_ge(one_used, 2 * NB)
                for b in range(NB):
                    if b == 2:
                        act.wait_ge(os_done, N + 1)
                        nc.scalar.activation(qkv[:, 8:12, cols(t)], bank["o"][:], ACT.Copy).then_inc(o_copied, 1)
                    if b >= 2:
                        act.wait_ge(sample_product, b - 1)
                    nc.scalar.activation(one[:, b % 2], kd[:, t % 2], ACT.Copy, scale=C.seq_mask[:, b:b + 1]
                                         ).then_inc(kdm_done, 1)

            run(prep, scan, sample)

        @block.gpsimd
        def _(pool):
            def mask(t, k):
                if k >= 2:
                    pool.wait_ge(z_done, z_after(t, k - 2, 1))
                if k == 2:
                    pool.wait_ge(upd, UPD * t + 1)
                if t == PT and k >= 4:
                    ins = nc.gpsimd.memset(pair[:, k % 2], 0.0)
                else:
                    ins = nc.gpsimd.tensor_tensor(pair[:, k % 2], low[:], each(C.level[:, k, :], HEADS), ALU.mult)
                ins.then_inc(masked, 1)

            def prep(t, s):
                if s == 1:
                    pool.wait_ge(low_done, t + 1)
                    nc.gpsimd.tensor_tensor(low[:], low[:], over(beta[:, t, :], P), ALU.mult).then_inc(low_scaled, 1)
                    pool.wait_ge(low_scaled, t + 1)
                    if t:
                        pool.wait_ge(z_done, z_after(t - 1, LEVELS - 1, 1))
                    mask(t, 0)
                    mask(t, 1)
                    pool.wait_ge(qk_raw, t + 1)
                    nc.gpsimd.tensor_tensor(qk[:, t % 2], qk[:, t % 2], each(C.upto[:, t // PT, :], HEADS), ALU.mult
                                            ).then_inc(qk_done, 1)
                    pool.wait_ge(exp_done, 3 * t + 3)
                    nc.gpsimd.tensor_tensor(qg[:, t % 2], qkv[:, 0:4, cols(t)], E[:, t % 2], ALU.mult
                                            ).then_inc(qg_done, 1)
                elif 3 <= s < 1 + LEVELS:
                    mask(t, s - 1)

            def scan(t, c, what):
                n = 2 * t + c
                if what == "w":
                    if n:
                        pool.wait_ge(s_done, n)
                    else:
                        pool.wait_ge(zeroed, 2)
                    last = 64 * c + 63
                    nc.gpsimd.tensor_tensor(Sg[:], S[:], E[:, t % 2, :, last:last + 1].to_broadcast([P, HEADS, P]),
                                            ALU.mult).then_inc(sg_done, 1)

            def sample(t):
                nc.gpsimd.memset(one[:], 0.0).then_inc(cleared, 1)
                pool.wait_ge(cleared, 1)
                pool.wait_ge(solved_copied, 2 * t + 2)
                for n in range(2 * NB):
                    now = slice(TB * (n % NB), TB * (n % NB) + TB)
                    if n >= 2:
                        pool.wait_ge(one_used, n - 1)
                        pool.wait_ge(one_ready, n - 1)
                        was = slice(TB * ((n - 2) % NB), TB * ((n - 2) % NB) + TB)
                        nc.gpsimd.memset(one[:, n % 2, :, was], 0.0)
                    if n == NB:
                        pool.wait_ge(qg_done, t + 1)
                    frm = wT if n < NB else qg
                    nc.gpsimd.tensor_copy(one[:, n % 2, :, now], frm[:, t % 2, :, now]).then_inc(one_ready, 1)
                pool.wait_ge(s0_landed, 16 * NB)
                pool.wait_ge(one_used, 2 * NB)
                for b in range(NB):
                    last = TB * b + TB - 1
                    nc.gpsimd.tensor_tensor(S0[:, b], S0[:, b],
                                            E[:, t % 2, :, last:last + 1].to_broadcast([P, HEADS, P]), ALU.mult
                                            ).then_inc(sample_decayed, 1)

            run(prep, scan, sample)

        @block.vector
        def _(dve):
            def decay_steps(t):
                nc.vector.tensor_tensor(G[:], each(C.upto[:, t // PT, :], HEADS), over(g[:, t, :], P), ALU.mult
                                        ).then_inc(g_ready, 1)

            def prep(t, s):
                i = t % 2
                if s == 0 and t == 0:
                    nc.vector.memset(S[:], 0.0).then_inc(zeroed, 1)
                    nc.vector.memset(u[:], 0.0).then_inc(zeroed, 1)
                    decay_steps(0)
                elif s == 1:
                    dve.wait_ge(exp_done, 3 * t + 3)
                    dve.wait_ge(products, 2 * t + 1)
                    if t:
                        dve.wait_ge(masked, LEVELS * t)
                    nc.vector.tensor_tensor(low[:], bank["d"][:], dec[:], ALU.mult).then_inc(low_done, 1)
                    if t >= 2:
                        dve.wait_ge(s_done, 2 * t - 2)
                    nc.vector.tensor_tensor(qk[:, i], bank["e"][:], decT[:], ALU.mult).then_inc(qk_raw, 1)
                    dve.wait_ge(products, 2 * t + 2)
                    if t:
                        dve.wait_ge(solved, 2 * t)
                    nc.vector.tensor_tensor(rk[:], bank["a"][:], over(bu[:, t, :], P), ALU.mult)
                    nc.vector.tensor_tensor(rv[:], bank["b"][:], over(beta[:, t, :], P), ALU.mult)
                    nc.vector.tensor_tensor(kd[:, i], bank["a"][:], over(tail[:, t, :], P), ALU.mult
                                            ).then_inc(rhs_done, 1)
                elif s == 2:
                    if t:
                        dve.wait_ge(solved, 2 * t)
                    dve.wait_ge(masked, LEVELS * t + 1)
                    ident = C.ident[:].unsqueeze(1).unsqueeze(1).to_broadcast([P, 2, 2, P])
                    nc.vector.tensor_tensor(inv[:, :, 1], ident,
                                            pair[:, 0].rearrange("p (j i) c -> p j i c", j=2), ALU.subtract
                                            ).then_inc(upd, 1)
                    dve.wait_ge(z_done, z_after(t, 0, 1))
                    nc.vector.tensor_tensor(inv[:, :, 0], ident, bank["c"][:].rearrange("p (j i) c -> p j i c", j=2),
                                            ALU.subtract).then_inc(upd, 1)
                elif 3 <= s < 2 + LEVELS:
                    k = s - 2
                    kinds = 2 if k < LEVELS - 1 else 1
                    for j in range(2):
                        dve.wait_ge(x_done, level_after(t, k, j))
                        dve.wait_ge(upd, upd_after(t, k - 1, j))
                        was = inv[:, j, 0:kinds]
                        nc.vector.tensor_tensor(was, was, bank[UBANK[j]][:, 0:2 * kinds, :].rearrange(
                            "p (n i) c -> p n i c", n=kinds), ALU.subtract).then_inc(upd, 1)
                elif s == 8:
                    if t + 1 < NT:
                        dve.wait_ge(sums_done, t + 1)
                        decay_steps(t + 1)

            def scan(t, c, what):
                n = 2 * t + c
                r = slice(64 * c, 64 * c + 64)
                if what == "w":
                    dve.wait_ge(ws_done, n + 1)
                    dve.wait_ge(solved_copied, 2 * t + 2)
                    if n:
                        dve.wait_ge(s_done, n)
                    else:
                        dve.wait_ge(zeroed, 2)
                    nc.vector.tensor_tensor(u[r], u0[r, t % 2], bank["u"][r], ALU.subtract).then_inc(u_done, 1)
                else:
                    dve.wait_ge(s_product, n + 1)
                    dve.wait_ge(sg_done, n + 1)
                    nc.vector.tensor_tensor(S[:], Sg[:], bank["s"][:], ALU.add).then_inc(s_done, 1)

            def sample(t):
                dve.wait_ge(one_used, NB)
                dve.wait_ge(solved_copied, 2 * t + 2)
                nc.vector.tensor_tensor(u[:], u0[:, t % 2], bank["u"][:], ALU.subtract).then_inc(u_done, 1)
                for b in range(NB):
                    dve.wait_ge(sample_product, b + 1)
                    dve.wait_ge(sample_decayed, b + 1)
                    nc.vector.tensor_tensor(S0[:, b], S0[:, b], bank["de"[b % 2]][:], ALU.add).then_inc(sample_done, 1)

            run(prep, scan, sample)


def late_norms(nc, C, M, ahead):
    sq, sk = M["swa_q"], M["swa_k"]
    o = M["qkv"]
    items = [([o[:, 8 + h, :]], [o[:, 8 + h, :]], C.ones[:], 1.0 / P, [C.vec[:, V_GN:V_GN + 1]]) for h in range(HEADS)]
    items += [([x], [x], C.pair_ones[:], 1.0 / SWA_HD, [C.vec[:, v:v + 1]])
              for x, v in ((sq[:, 0, :], V_SQ), (sq[:, 1, :], V_SQ), (sk[:, 0, :], V_SK))]
    column_norms(nc, C, "go", items, 4, ahead)



def attention(nc, C, tag, scale, hide, sinks, scores, sample_scores, values, dest, loads=None, buffers=None,
              early=None, sample_copies=None, direct=None, before=None):
    slots, turned_parts, new_scores = sample_scores or (None, None, None)
    with C.phase() as ph:
        p = ph.sb(f"{tag}_p", [P, 2, HEADS, 256])
        pT = ph.sb(f"{tag}_pt", [P, 2, 8, P])
        mx, nm, den, rec, es = (ph.sb(f"{tag}_{n}", [P, 2, HEADS]) for n in ("mx", "nm", "den", "rec", "es"))
        B = buffers(ph) if buffers else {}
        s_bank = ph.psum(f"{tag}_scores", [P, 2, HEADS, 256])
        t_bank = ph.psum(f"{tag}_turned", [P, 8, P])
        o_bank = ph.psum(f"{tag}_out", [P, 8, P])
        names = ("scored", "hidden", "maxed", "max_step", "exp_done", "summed", "normed", "turned", "turned_copied",
                 "valued", "out_copied", "early", "sample_scored", "sample_copied", "rows_copied", "rows_turned")
        s = {n: ph.sem(f"{tag}_{n}") for n in names}
        block = ph.block()
        act_exps = HEADS + (1 if sinks is not None else 0)
        max_steps = 4 if sinks is not None else 2
        last = NT - 1

        @block.sync
        def _(sp):
            if loads:
                loads(sp, B, s)

        @block.tensor
        def _(pe):
            if early:
                early["pe"](pe, B, s, t_bank, o_bank)

            def score(t):
                if t >= 2:
                    pe.wait_ge(s["hidden"] if hide else s["exp_done"], t - 1 if hide else act_exps * (t - 1))
                if t < last:
                    scores(pe, t, s_bank[:, t % 2]).then_inc(s["scored"], 1)
                    return
                pe.wait_ge(s["out_copied"], last)
                if direct:
                    direct["scores"](pe, B, s, s_bank[:, t % 2], o_bank)
                    return
                pe.wait_ge(s["turned_copied"], last)
                turned_parts(pe, B, s, t_bank, o_bank)
                pe.wait_ge(s["sample_copied"], 1)
                for slot, h, half in slots:
                    ins = nc.tensor.transpose(s_bank[:, t % 2, h, P * half:P * half + P], pT[:, 1 - (last - 1) % 2, slot, :],
                                              C.ident[:])
                if new_scores:
                    ins = new_scores(pe, s_bank[:, t % 2])
                ins.then_inc(s["scored"], 1)

            def turn(t):
                pe.wait_ge(s["normed"], t + 1)
                if t:
                    pe.wait_ge(s["turned_copied"], t)
                for half in range(2):
                    for h in range(HEADS):
                        ins = nc.tensor.transpose(t_bank[:, 4 * half + h, :], p[:, t % 2, h, P * half:P * half + P],
                                                  C.ident[:])
                ins.then_inc(s["turned"], 1)

            def output(t):
                pe.wait_ge(s["turned_copied"], t + 1)
                if t:
                    pe.wait_ge(s["out_copied"], t)
                values(pe, t, pT[:, t % 2], o_bank, B, s).then_inc(s["valued"], 1)

            score(0)
            score(1)
            for t in range(last):
                turn(t)
                if t + 2 < last:
                    score(t + 2)
                output(t)
            score(last)
            turn(last)
            output(last)
            if direct:
                pe.wait_ge(s["rows_copied"], 1)
                rows = p[:, last % 2].rearrange("p h c -> p (h c)")
                for f in range(8):
                    ins = nc.tensor.transpose(t_bank[:, f, :], rows[:, P * f:P * f + P], C.ident[:])
                ins.then_inc(s["rows_turned"], 1)

        def output_copy(dve, t):
            dve.wait_ge(s["valued"], t + 1)
            to, frm = dest(t, o_bank)
            nc.vector.tensor_copy(to, frm).then_inc(s["out_copied"], 1)

        @block.vector
        def _(dve):
            if early and "dve" in early:
                early["dve"](dve, B, s, t_bank, o_bank)
            def maxima(t):
                i = t % 2
                dve.wait_ge(s["scored"], t + 1)
                if t >= 2:
                    dve.wait_ge(s["exp_done"], act_exps * (t - 1))
                src = s_bank[:, i]
                if hide:
                    kind = 1 if t == 0 else 2 if t == last else 0
                    if t >= 2:
                        dve.wait_ge(s["turned"], t - 1)
                    nc.vector.scalar_tensor_tensor(p[:, i], s_bank[:, i], scale, each(C.hide[:, kind, :], HEADS),
                                                   ALU.mult, ALU.add).then_inc(s["hidden"], 1)
                    dve.wait_ge(s["hidden"], t + 1)
                    src = p[:, i]
                nc.vector.tensor_reduce(mx[:, i], src, AX.X, ALU.max).then_inc(s["max_step"], 1)
                dve.wait_ge(s["max_step"], max_steps * t + 1)
                if sinks is not None:
                    nc.vector.tensor_tensor(mx[:, i], mx[:, i], sinks, ALU.max).then_inc(s["max_step"], 1)
                    dve.wait_ge(s["max_step"], max_steps * t + 2)
                    if t >= 2:
                        dve.wait_ge(s["summed"], t - 1)
                    nc.vector.tensor_tensor(es[:, i], sinks, mx[:, i], ALU.subtract).then_inc(s["max_step"], 1)
                nc.vector.tensor_scalar(nm[:, i], mx[:, i], -1.0 if hide else -scale, None, ALU.mult
                                        ).then_inc(s["max_step"], 1)

            def denominators(t):
                i = t % 2
                dve.wait_ge(s["exp_done"], act_exps * (t + 1))
                if sinks is not None:
                    nc.vector.tensor_tensor(den[:, i], den[:, i], es[:, i], ALU.add).then_inc(s["maxed"], 1)
                    dve.wait_ge(s["maxed"], t + 1)
                if t >= 2:
                    dve.wait_ge(s["normed"], t - 1)
                nc.vector.reciprocal(rec[:, i], den[:, i]).then_inc(s["summed"], 1)

            maxima(0)
            maxima(1)
            denominators(0)
            for t in range(last):
                if t + 1 < last:
                    denominators(t + 1)
                if t:
                    output_copy(dve, t - 1)
                if t + 2 < last:
                    maxima(t + 2)
            output_copy(dve, last - 1)
            if sample_copies:
                sample_copies(dve, B, s, o_bank)
            maxima(last)
            denominators(last)
            if direct:
                dve.wait_ge(s["valued"], NT)
                nc.vector.tensor_copy(p[:, last % 2].rearrange("p h c -> p (h c)"), o_bank[:].rearrange("p f c -> p (f c)")
                                      ).then_inc(s["rows_copied"], 1)
                dve.wait_ge(s["rows_turned"], 1)
                to, frm = dest(last, t_bank)
                nc.vector.tensor_copy(to, frm).then_inc(s["out_copied"], 1)
            else:
                output_copy(dve, last)

        @block.scalar
        def _(act):
            if early and "act" in early:
                early["act"](act, B, s, t_bank, o_bank)

            def copy_turned(t):
                act.wait_ge(s["turned"], t + 1)
                if t >= 2:
                    act.wait_ge(s["valued"], t - 1)
                nc.scalar.activation(pT[:, t % 2], t_bank[:], ACT.Copy).then_inc(s["turned_copied"], 1)

            def exponentials(t):
                i = t % 2
                act.wait_ge(s["max_step"], max_steps * (t + 1))
                if t >= 2:
                    act.wait_ge(s["turned"], t - 1)
                    act.wait_ge(s["summed"], t - 1)
                src = p if hide else s_bank
                for h in range(HEADS):
                    nc.scalar.activation(p[:, i, h, :], src[:, i, h, :], ACT.Exp, bias=nm[:, i, h:h + 1],
                                         scale=1.0 if hide else scale, accum_out=den[:, i, h:h + 1]
                                         ).then_inc(s["exp_done"], 1)
                if sinks is not None:
                    nc.scalar.activation(es[:, i], es[:, i], ACT.Exp).then_inc(s["exp_done"], 1)

            exponentials(0)
            for t in range(last):
                if t + 1 < last:
                    exponentials(t + 1)
                copy_turned(t)
            if not direct:
                act.wait_ge(s["sample_scored"], 1)
                act.wait_ge(s["valued"], last - 1)
                nc.scalar.activation(pT[:, 1 - (last - 1) % 2], t_bank[:], ACT.Copy).then_inc(s["sample_copied"], 1)
            exponentials(last)
            copy_turned(last)

        @block.gpsimd
        def _(pool):
            if before:
                before(pool)
            if direct:
                direct["clear"](pool, B)
            for t in range(NT):
                if direct and t == last:
                    direct["masks"](pool, B, s, 0, None)
                pool.wait_ge(s["summed"], t + 1)
                nc.gpsimd.tensor_tensor(p[:, t % 2], p[:, t % 2], over(rec[:, t % 2], 256), ALU.mult
                                        ).then_inc(s["normed"], 1)
            if direct:
                pool.wait_ge(s["turned_copied"], NT)
                direct["masks"](pool, B, s, NB, pT[:, last % 2])


class WindowPast:

    def __init__(self, C, A):
        self.k, self.v = C.sb("swa_k_past", [P, NB, P]), C.sb("swa_v_past", [P, NB, P])
        self.landed = C.sem("swa_past_landed")
        self.A = A

    def load(self, sp):
        for to, name in ((self.k, "cache_swa_k"), (self.v, "cache_swa_v")):
            sp.dma_start(to[:], self.A[name][0].rearrange("b k h d -> k b (h d)")).then_inc(self.landed, 16)


def window_attention(nc, C, A, O, M, past, ahead):
    sq, sk, sv = M["swa_q"], M["swa_k"], M["swa_v"]

    def buffers(ph):
        return {"v": ph.sb("swa_v_rows", [P, NT, P]), "kp": past.k, "vp": past.v,
                "kpT": ph.sb("swa_k_past_t", [P, NB, P]),
                "k_rows": ph.sb("swa_k_rows", [P, 2, P]),
                "landed": past.landed, "stored": C.window_stored, "copied": ph.sem("swa_rows_copied")}

    def loads(sp, B, s):
        ahead(sp)
        sp.wait_ge(B["copied"], 5)
        for j, (k, v) in enumerate((("p_swa_k", "p_swa_v"), ("s_swa_k", "s_swa_v"))):
            for name, rows in ((k, B["k_rows"][:, j, :]), (v, B["v"][:, PT - 1 + j, :])):
                sp.dma_start(O[name][0].rearrange("b t h d -> (b t) (h d)"), rows).then_inc(B["stored"], 16)
        sp.wait_ge(B["stored"], 64)

    groups = [[("kp", b) for b in range(8)], [("v", t) for t in range(8)], [("v", 8), ("k", 7), ("k", 8)]]

    def early_pe(pe, B, s, t_bank, o_bank):
        pe.wait_ge(B["landed"], 32)
        for n, group in enumerate(groups):
            if n == 2:
                pe.wait_ge(B["copied"], 2)
            bank = t_bank if n % 2 == 0 else o_bank
            for j, (what, t) in enumerate(group):
                src = B["kp"][:, t, :] if what == "kp" else (sk if what == "k" else sv)[:, 0, P * t:P * t + P]
                ins = nc.tensor.transpose(bank[:, j, :], src, C.ident[:])
            ins.then_inc(s["early"], 1)
        pe.wait_ge(B["copied"], 5)

    def early_dve(dve, B, s, t_bank, o_bank):
        for n, (to, frm) in enumerate(((B["kpT"][:, 0:4], t_bank[:, 0:4]), (B["kpT"][:, 4:8], t_bank[:, 4:8]),
                                       (B["v"][:, 0:8], o_bank[:]), (B["v"][:, 8], t_bank[:, 0]),
                                       (B["k_rows"][:], t_bank[:, 1:3]))):
            dve.wait_ge(s["early"], (1, 1, 2, 3, 3)[n])
            nc.vector.tensor_copy(to, frm).then_inc(B["copied"], 1)

    def gate(pool):
        for h in range(HEADS):
            nc.gpsimd.tensor_tensor(C.mixT[:, h, :], C.mixT[:, h, :], M["qkv"][:, 8 + h, :], ALU.mult)

    def half(h):
        return slice(64 * (h // 2), 64 * (h // 2) + 64)

    def scores(pe, t, out):
        for h in range(HEADS):
            q = sq[half(h), h % 2, P * t:P * t + P]
            if t:
                ins = nc.tensor.matmul(out[:, h, :], q, sk[half(h), 0, P * t - P:P * t + P], start=True, stop=True)
            else:
                for j in range(2):
                    ins = nc.tensor.matmul(out[:, h, P * j:P * j + P], q, sk[half(h), 0, 0:P], start=True, stop=True)
        return ins

    def turned_parts(pe, B, s, t_bank, o_bank):
        for h in range(HEADS):
            slot = 4 * (h // 2) + h % 2
            for b in range(NB):
                ins = nc.tensor.matmul(t_bank[:, slot, TB * b:TB * b + TB], B["kpT"][half(h), b, :],
                                       sq[half(h), h % 2, TP + TB * b:TP + TB * b + TB], start=True, stop=True)
        ins.then_inc(s["sample_scored"], 1)

    def new_scores(pe, out):
        for h in range(HEADS):
            ins = nc.tensor.matmul(out[:, h, P:2 * P], sq[half(h), h % 2, TP:T], sk[half(h), 0, TP:T],
                                   start=True, stop=True)
        return ins

    def values(pe, t, pT, out, B, s):
        for h in range(HEADS):
            kv = slice(64 * (h // 2), 64 * (h // 2) + 64)
            o = out[64 * (h % 2):64 * (h % 2) + 64, h // 2, :]
            if t < NT - 1:
                nc.tensor.matmul(o, B["v"][:, max(t - 1, 0), kv], pT[:, h, :], start=True, stop=False)
                ins = nc.tensor.matmul(o, B["v"][:, t, kv], pT[:, 4 + h, :], start=False, stop=True)
            else:
                nc.tensor.matmul(o, B["v"][:, t, kv], pT[:, 4 + h, :], start=True, stop=False, skip_group_check=True)
                for b in range(NB):
                    ins = nc.tensor.matmul(o[:, TB * b:TB * b + TB], B["vp"][:, b, kv], pT[:, h, TB * b:TB * b + TB],
                                           start=False, stop=(b == NB - 1), skip_group_check=True)
        return ins

    def dest(t, o_bank):
        return C.mixT[:, 4:6, P * t:P * t + P], o_bank[:, 0:2, :]

    slots = [(4 * (h // 2) + h % 2, h, 0) for h in range(HEADS)]
    attention(nc, C, "sw", float(SWA_HD) ** -0.5, True, C.sinks[:], scores, (slots, turned_parts, new_scores),
              values, dest, loads, buffers, {"pe": early_pe, "dve": early_dve}, before=gate)




class RowWeights:
    RING = 3

    def __init__(self, C, tag, matrices, side="left"):
        self.raw = C.sb(f"{tag}_w_raw", [P, self.RING, D], side=side)
        self.landed = [C.sem(f"{tag}_w_landed{r}") for r in range(self.RING)]
        self.slices = [w[P * k:P * k + P, :] for w in matrices for k in range(KD)]

    def at(self, i):
        return self.raw[:, i % self.RING, :]

    def load(self, sp, i):
        sp.dma_start(self.at(i), self.slices[i]).then_inc(self.landed[i % self.RING], 16)

    def load_first(self, sp):
        for i in range(self.RING):
            self.load(sp, i)

    def load_rest(self, sp, w_split):
        for i in range(self.RING, len(self.slices)):
            sp.wait_ge(w_split, i - self.RING + 1)
            self.load(sp, i)

    def wait(self, engine, i):
        engine.wait_ge(self.landed[i % self.RING], 16 * (i // self.RING + 1))


def memory_projections(nc, C, actT, weights, outs):
    SPLIT_RING = 3
    n_slices = len(weights.slices)
    with C.phase() as ph:
        w_hi, w_lo = (ph.sb(f"mkv_w_{n}", [P, SPLIT_RING, D], F32R) for n in ("hi", "lo"))
        a_hi, a_lo = (ph.sb(f"mkv_act_{n}", [P, KD, 2 * P], F32R) for n in ("hi", "lo"))
        banks = ph.psum("mkv_banks", [P, 8, 512])
        act_high, act_split, w_high, w_split, multiplied, copied = (ph.sem(f"mkv_{n}") for n in (
            "act_high", "act_split", "w_high", "w_split", "multiplied", "copied"))
        block = ph.block()

        @block.sync
        def _(sp):
            weights.load_rest(sp, w_split)

        @block.tensor
        def _(pe):
            pe.wait_ge(act_split, 1)
            for i in range(n_slices):
                m, k = divmod(i, KD)
                pe.wait_ge(w_split, i + 1)
                for g in range(4):
                    tok, col = slice(P * (g // 2), P * (g // 2) + P), slice(512 * (g % 2), 512 * (g % 2) + 512)
                    for n, (a, w) in enumerate(((a_hi, w_hi), (a_hi, w_lo), (a_lo, w_hi))):
                        ins = nc.tensor.matmul(banks[:, 4 * m + g, :], a[:, k, tok], w[:, i % SPLIT_RING, col],
                                               start=(k == 0 and n == 0), stop=(k == KD - 1 and n == 2))
                ins.then_inc(multiplied, 1)

        @block.scalar
        def _(act):
            nc.scalar.activation(a_hi[:], actT[:], ACT.Copy).then_inc(act_high, 1)
            for i in range(n_slices):
                weights.wait(act, i)
                if i >= SPLIT_RING:
                    act.wait_ge(multiplied, i - SPLIT_RING + 1)
                nc.scalar.activation(w_hi[:, i % SPLIT_RING, :], weights.at(i), ACT.Copy).then_inc(w_high, 1)

        @block.gpsimd
        def _(pool):
            for i in range(n_slices):
                pool.wait_ge(w_high, i + 1)
                nc.gpsimd.tensor_tensor(w_lo[:, i % SPLIT_RING, :], weights.at(i), w_hi[:, i % SPLIT_RING, :].bitcast(F32),
                                        ALU.subtract).then_inc(w_split, 1)

        @block.vector
        def _(dve):
            dve.wait_ge(act_high, 1)
            nc.vector.tensor_tensor(a_lo[:], actT[:], a_hi[:].bitcast(F32), ALU.subtract).then_inc(act_split, 1)
            for m, out in enumerate(outs):
                dve.wait_ge(multiplied, KD * (m + 1))
                for g in range(4):
                    nc.vector.tensor_copy(out[:, g // 2, 512 * (g % 2):512 * (g % 2) + 512], banks[:, 4 * m + g, :]
                                          ).then_inc(copied, 1)


def row_projection(nc, C, tag, actT, n_tiles, weights, out, residual=None, loaded=False):
    A_RING, together = 4, 3
    with C.phase() as ph:
        w_hi, w_lo = ph.sb(f"{tag}_w_hi", [P, KD, D], F32R), ph.sb(f"{tag}_w_lo", [P, KD, D], F32R)
        a_hi, a_lo = (ph.sb(f"{tag}_act_{n}", [P, A_RING, KD, P], F32R) for n in ("hi", "lo"))
        banks = ph.psum(f"{tag}_banks", [P, 8, 512])
        r_landed = [ph.sem(f"{tag}_r_landed{t}") for t in range(n_tiles if residual else 0)]
        act_high, act_split_first, act_split_later, w_high, w_split, projected, freed = (
            ph.sem(f"{tag}_{n}") for n in ("act_high", "act_split_first", "act_split_later", "w_high", "w_split",
                                           "projected", "freed"))
        block = ph.block()

        def act_tile(t):
            return actT[:, :, P * t:P * t + P]

        @block.sync
        def _(sp):
            if not loaded:
                weights.load_first(sp)
            weights.load_rest(sp, w_split)
            for t, rows in enumerate(residual or ()):
                sp.dma_start(out[:, t, :], rows).then_inc(r_landed[t], 16)

        @block.tensor
        def _(pe):
            def products(n, k):
                t, half = divmod(n, 2)
                col = slice(512 * half, 512 * half + 512)
                passes = ((a_hi, w_hi), (a_hi, w_lo), (a_lo, w_hi))
                for i, (a, w) in enumerate(passes):
                    ins = nc.tensor.matmul(banks[:, n % 8, :], a[:, t % A_RING, k, :], w[:, k, col],
                                           start=(k == 0 and i == 0), stop=(k == KD - 1 and i == 2))
                if k == KD - 1:
                    ins.then_inc(projected, 1)

            for k in range(KD):
                pe.wait_ge(w_split, k + 1)
                for n in range(2 * together):
                    if k == 0 and n % 2 == 0:
                        pe.wait_ge(act_split_first, n // 2 + 1)
                    products(n, k)
            for n in range(2 * together, 2 * n_tiles):
                if n % 2 == 0:
                    pe.wait_ge(act_split_later, n // 2 - together + 1)
                if n >= 8:
                    pe.wait_ge(freed, n - 7)
                for k in range(KD):
                    products(n, k)

        @block.scalar
        def _(act):
            def act_hi_part(t):
                if t >= A_RING:
                    act.wait_ge(projected, 2 * (t - A_RING + 1))
                nc.scalar.activation(a_hi[:, t % A_RING], act_tile(t), ACT.Copy).then_inc(act_high, 1)

            act_hi_part(0)
            for k in range(KD):
                weights.wait(act, k)
                nc.scalar.activation(w_hi[:, k], weights.at(k), ACT.Copy).then_inc(w_high, 1)
                if k + 1 < together:
                    act_hi_part(k + 1)
            for t in range(together, n_tiles):
                act_hi_part(t)

        @block.gpsimd
        def _(pool):
            for k in range(KD):
                pool.wait_ge(w_high, k + 1)
                nc.gpsimd.tensor_tensor(w_lo[:, k], weights.at(k), w_hi[:, k].bitcast(F32), ALU.subtract
                                        ).then_inc(w_split, 1)
            for t in range(together, n_tiles):
                pool.wait_ge(act_high, t + 1)
                nc.gpsimd.tensor_tensor(a_lo[:, t % A_RING], act_tile(t), a_hi[:, t % A_RING].bitcast(F32), ALU.subtract
                                        ).then_inc(act_split_later, 1)

        @block.vector
        def _(dve):
            for t in range(together):
                dve.wait_ge(act_high, t + 1)
                nc.vector.tensor_tensor(a_lo[:, t], act_tile(t), a_hi[:, t].bitcast(F32), ALU.subtract
                                        ).then_inc(act_split_first, 1)
            for n in range(2 * n_tiles):
                t, half = divmod(n, 2)
                to = out[:, t, 512 * half:512 * half + 512]
                if residual and half == 0:
                    dve.wait_ge(r_landed[t], 16)
                dve.wait_ge(projected, n + 1)
                nc.vector.tensor_tensor(to, to, banks[:, n % 8, :], ALU.add).then_inc(freed, 1)


def feature_projection(nc, C, tag, hi, lo, weights, n_tiles, out):
    RING = weights.RING
    with C.phase() as ph:
        w_hi, w_lo = (ph.sb(f"{tag}_w_{n}", [P, 2, KD, P], F32R) for n in ("hi", "lo"))
        banks = ph.psum(f"{tag}_banks", [P, 2 * NP, 512])
        high, split, projected, freed = (ph.sem(f"{tag}_{n}") for n in ("high", "split", "projected", "freed"))
        block = ph.block()

        @block.sync
        def _(sp):
            for n in range(RING, n_tiles):
                sp.wait_ge(split, n - RING + 1)
                weights.load(sp, n)

        @block.tensor
        def _(pe):
            for n in range(n_tiles):
                pe.wait_ge(split, n + 1)
                if n >= 2:
                    pe.wait_ge(freed, n - 1)
                for p in range(NP):
                    for k in range(KD):
                        for i, (w, x) in enumerate(((w_hi, hi), (w_hi, lo), (w_lo, hi))):
                            ins = nc.tensor.matmul(banks[:, (n % 2) * NP + p, 0:TC], w[:, n % 2, k, :],
                                                   x[:, k, TC * p:TC * p + TC], start=(k == 0 and i == 0),
                                                   stop=(k == KD - 1 and i == 2))
                    ins.then_inc(projected, 1)

        @block.scalar
        def _(act):
            def weights_high(n):
                weights.wait(act, n)
                if n >= 2:
                    act.wait_ge(projected, NP * (n - 1))
                nc.scalar.activation(w_hi[:, n % 2], weights.raw[:, n % RING], ACT.Copy).then_inc(high, 1)

            weights_high(0)
            weights_high(1)
            for n in range(n_tiles):
                for p in range(NP):
                    act.wait_ge(projected, NP * n + p + 1)
                    ins = nc.scalar.activation(out[:, n, TC * p:TC * p + TC], banks[:, (n % 2) * NP + p, 0:TC], ACT.Copy)
                ins.then_inc(freed, 1)
                if n + 2 < n_tiles:
                    weights_high(n + 2)

        @block.vector
        def _(dve):
            for n in range(n_tiles):
                dve.wait_ge(high, n + 1)
                nc.vector.tensor_tensor(w_lo[:, n % 2], weights.raw[:, n % RING], w_hi[:, n % 2].bitcast(F32), ALU.subtract
                                        ).then_inc(split, 1)



def memory_kv(nc, C, A, O, kT, v):
    with C.phase() as st:
        rows = st.sb("mem_rows", [P, 2, D])
        landed = [st.sem(f"mem_landed{t}") for t in range(2)]

        weights = RowWeights(st, "mkv", (A["w_mk"][0], A["w_mv"][0]))

        def load_rows(sp):
            for t in range(2):
                sp.dma_start(rows[:, t, :], A["mem_prompt"][0, P * t:P * t + P, :]).then_inc(landed[t], 16)
            weights.load_first(sp)

        mT = st.sb("mem_t", [P, KD, MEM])
        norm_turn(nc, C, "nm", rows, 2, V_MIN, mT, landed=landed, ahead=load_rows)
        k = rows
        memory_projections(nc, C, mT, weights, (k, v))
        with C.phase() as ph:
            squares = ph.sb("mk_squares", [P, 256])
            sums, root, inv = (ph.sb(f"mk_{n}", [P, 2 * HEADS]) for n in ("sums", "root", "inv"))
            banks = ph.psum("mk_turned", [P, 4, 512])
            summed, rooted, inverted, normed, turned, copied = (ph.sem(f"mk_{n}") for n in (
                "summed", "rooted", "inverted", "normed", "turned", "copied"))
            stored = C.memory_stored
            block = ph.block()

            @block.sync
            def _(sp):
                sp.dma_start(O["p_mem_v"][0, 0].rearrange("(t p) h d -> p t (h d)", p=P), v[:]).then_inc(stored, 16)
                sp.wait_ge(normed, 2 * HEADS)
                sp.dma_start(O["p_mem_k"][0, 0].rearrange("(t p) h d -> p t (h d)", p=P), k[:]).then_inc(stored, 16)
                sp.wait_ge(stored, 32)

            @block.scalar
            def _(act):
                for n in range(2 * HEADS):
                    t, h = divmod(n, HEADS)
                    if n:
                        act.wait_ge(summed, n)
                    nc.scalar.activation(squares[:], k[:, t, 256 * h:256 * h + 256], ACT.Square,
                                         accum_out=sums[:, n:n + 1]).then_inc(summed, 1)
                act.wait_ge(summed, 2 * HEADS)
                nc.scalar.activation(root[:], sums[:], ACT.Sqrt, scale=1.0 / 256, bias=C.eps[:, 0:1]).then_inc(rooted, 1)

            @block.vector
            def _(dve):
                dve.wait_ge(rooted, 1)
                nc.vector.reciprocal(inv[:], root[:]).then_inc(inverted, 1)
                dve.wait_ge(inverted, 1)
                for n in range(2 * HEADS):
                    t, h = divmod(n, HEADS)
                    x = k[:, t, 256 * h:256 * h + 256]
                    nc.vector.scalar_tensor_tensor(x, x, inv[:, n:n + 1], C.k_gain[:], ALU.mult, ALU.mult
                                                   ).then_inc(normed, 1)
                for n in range(4):
                    dve.wait_ge(turned, n + 1)
                    nc.vector.tensor_copy(kT[:, 2 * n:2 * n + 2, :], banks[:, n, :].rearrange("p (a b) -> p a b", a=2)
                                          ).then_inc(copied, 1)

            @block.tensor
            def _(pe):
                pe.wait_ge(normed, 2 * HEADS)
                for n in range(4):
                    for j in range(2):
                        for t in range(2):
                            f = 2 * n + j
                            ins = nc.tensor.transpose(banks[:, n, 256 * j + P * t:256 * j + P * t + P],
                                                      k[:, t, P * f:P * f + P], C.ident[:])
                    ins.then_inc(turned, 1)


def memory_attention(nc, C, A, qT, kT, v, attnT):

    def buffers(ph):
        return {"kb": ph.sb("mem_k_one", [P, 2, 2, D]), "vb": ph.sb("mem_v_one", [P, 2, 2, D]),
                "kbT": ph.sb("mem_k_one_t", [P, 2, 2, MEM]), "masked": ph.sb("mem_masked", [P, 2, 8, P]),
                "masked_ready": ph.sem("mem_masked_ready"), "cleared": ph.sem("mem_cleared"),
                "k_landed": [ph.sem(f"mem_k_landed{i}") for i in range(2)],
                "v_landed": [ph.sem(f"mem_v_landed{i}") for i in range(4)],
                "k_turned": ph.sem("mem_k_turned"), "k_copied": ph.sem("mem_k_copied"),
                "k_used": ph.sem("mem_k_used"), "v_used": ph.sem("mem_v_used")}

    def v_one(B, b):
        return (B["vb"] if b % 4 < 2 else B["kb"])[:, b % 2]

    def loads(sp, B, s):
        def load_k(b):
            if b >= 2:
                sp.wait_ge(B["k_turned"], HEADS * (b - 1))
            sp.dma_start(B["kb"][:, b % 2], A["cache_mem_k"][0, b].rearrange("(t p) h d -> p t (h d)", p=P)
                         ).then_inc(B["k_landed"][b % 2], 16)

        def load_v(b):
            if 2 <= b < 4:
                sp.wait_ge(B["k_turned"], HEADS * (NB - 3 + b))
            if b >= 4:
                sp.wait_ge(B["v_used"], b - 3)
            sp.dma_start(v_one(B, b), A["cache_mem_v"][0, b].rearrange("(t p) h d -> p t (h d)", p=P)
                         ).then_inc(B["v_landed"][b % 4], 16)

        for b in range(2):
            load_k(b)
        for b in range(2):
            load_v(b)
        for b in range(2, NB):
            load_k(b)
        for b in range(2, NB):
            load_v(b)

    def scores(pe, t, out):
        for h in range(HEADS):
            for j in range(2):
                ins = nc.tensor.matmul(out[:, h, :], qT[:, 2 * h + j, P * t:P * t + P], kT[:, 2 * h + j, :],
                                       start=(j == 0), stop=(j == 1))
        return ins


    def clear(pool, B):
        nc.gpsimd.memset(B["masked"][:], 0.0).then_inc(B["cleared"], 1)
        pool.wait_ge(B["cleared"], 1)

    def masks(pool, B, s, first, pT):
        for n in range(first, first + NB):
            slot, b = B["masked"][:, n % 2], n % NB
            if n >= 2:
                was = (n - 2) % NB
                pool.wait_ge(B["masked_ready"], n - 1)
                if n - 2 < NB:
                    pool.wait_ge(B["k_used"], HEADS * (n - 1))
                else:
                    pool.wait_ge(B["v_used"], n - 1 - NB)
                nc.gpsimd.memset(slot[:, :, TB * was:TB * was + TB], 0.0)
            frm = qT[:, :, TP + TB * b:TP + TB * b + TB] if pT is None else pT[:, :, TB * b:TB * b + TB]
            nc.gpsimd.tensor_copy(slot[:, :, TB * b:TB * b + TB], frm).then_inc(B["masked_ready"], 1)

    def sample_scores(pe, B, s, out, o_bank):
        for m in range(HEADS * NB + 2):
            if m >= 2:
                b, h = divmod(m - 2, HEADS)
                pe.wait_ge(B["masked_ready"], b + 1)
                pe.wait_ge(B["k_copied"], m - 1)
                for j in range(2):
                    ins = nc.tensor.matmul(out[:, h, :], B["masked"][:, b % 2, 2 * h + j, :], B["kbT"][:, m % 2, j, :],
                                           start=(b == 0 and h % 2 == 0 and j == 0), stop=(b == NB - 1 and j == 1),
                                           skip_group_check=True)
                ins.then_inc(B["k_used"], 1)
            if m < HEADS * NB:
                b, h = divmod(m, HEADS)
                if h == 0:
                    pe.wait_ge(B["k_landed"][b % 2], 16 * (b // 2 + 1))
                for j in range(2):
                    for kt in range(2):
                        ins = nc.tensor.transpose(o_bank[:, 4 * (m % 2) + 2 * j + kt, :],
                                                  B["kb"][:, b % 2, kt, P * (2 * h + j):P * (2 * h + j) + P], C.ident[:])
                ins.then_inc(B["k_turned"], 1)
        pe.wait_ge(B["k_used"], HEADS * NB)
        pe.sem_inc(s["scored"], 1)

    def sample_copies(dve, B, s, o_bank):
        for m in range(HEADS * NB):
            dve.wait_ge(B["k_turned"], m + 1)
            if m >= 2:
                dve.wait_ge(B["k_used"], m - 1)
            nc.vector.tensor_copy(B["kbT"][:, m % 2], o_bank[:, 4 * (m % 2):4 * (m % 2) + 4, :].rearrange(
                "p (j k) c -> p j (k c)", j=2)).then_inc(B["k_copied"], 1)

    def values(pe, t, pT, out, B, s):
        if t < NT - 1:
            for h in range(HEADS):
                for j in range(2):
                    f = 2 * h + j
                    for kt in range(2):
                        ins = nc.tensor.matmul(out[:, f, :], v[:, kt, P * f:P * f + P], pT[:, 4 * kt + h, :],
                                               start=(kt == 0), stop=(kt == 1))
            return ins
        rows = out.rearrange("p f c -> p (f c)")
        for b in range(NB):
            pe.wait_ge(B["v_landed"][b % 4], 16 * (b // 4 + 1))
            pe.wait_ge(B["masked_ready"], NB + b + 1)
            for h in range(HEADS):
                for kt in range(2):
                    ins = nc.tensor.matmul(rows[:, MEM * h:MEM * h + MEM], B["masked"][:, b % 2, 4 * kt + h, :],
                                           v_one(B, b)[:, kt, MEM * h:MEM * h + MEM],
                                           start=(b == 0 and h % 2 == 0 and kt == 0), stop=(b == NB - 1 and kt == 1),
                                           skip_group_check=True)
            if b < NB - 1:
                ins.then_inc(B["v_used"], 1)
        return ins

    def dest(t, o_bank):
        return attnT[:, :, P * t:P * t + P], o_bank[:]

    attention(nc, C, "ma", 1.0 / 16, False, None, scores, None, values, dest, loads, buffers, None, sample_copies,
              {"scores": sample_scores, "clear": clear, "masks": masks})



class FfnWeights:

    def __init__(self, C, A):
        self.raw = C.sb("up_raw", [P, 2, KD, P])
        self.d_raw = C.sb("down_raw", [P, D])
        self.w_up = A["w_up"][0].rearrange("(k p) c -> p k c", p=P)
        self.w_down = A["w_down"][0].rearrange("(f p) c -> f p c", p=P)
        self.w_landed = [C.sem(f"f_w_landed_{s}") for s in "gv"]
        self.d_landed = C.sem("f_d_landed")

    def load_up(self, sp, s, f):
        sp.dma_start(self.raw[:, s], self.w_up[:, :, FF * s + P * f:FF * s + P * f + P]).then_inc(self.w_landed[s], 16)

    def load_down(self, sp, f):
        sp.dma_start(self.d_raw[:], self.w_down[f]).then_inc(self.d_landed, 16)

    def load_first(self, sp):
        self.load_up(sp, 0, 0)
        self.load_up(sp, 1, 0)
        self.load_down(sp, 0)


def ffn(nc, C, A, O, h, hi, lo, old, weights):
    W = 3
    L = xp_len(W)
    LY = L - (W - 1)
    NG = 2 * NT
    with C.phase() as ph:
        raw, d_raw, w_landed, d_landed = weights.raw, weights.d_raw, weights.w_landed, weights.d_landed
        w_hi, w_lo = ph.sb("up_hi", [P, 2, KD, P], F32R), ph.sb("up_lo", [P, 2, KD, P], F32R)
        d_hi, d_lo = ph.sb("down_hi", [P, D], F32R), ph.sb("down_lo", [P, D], F32R)
        xp = ph.sb("ffn_conv_in", [P, 2, L])
        y = ph.sb("ffn_conv_out", [P, 2, LY + 2])
        a = ph.sb("ffn_gated", [P, T])
        a_hi, a_lo = ph.sb("gated_hi", [P, T], F32R), ph.sb("gated_lo", [P, T], F32R)
        tails = ph.sb("ffn_tails", [P, 2, NF, 18])
        banks = ph.psum("ffn_banks", [P, 8, 512])
        d_bank = (2, 6, 7, 0, 1)
        split, w_high, up, evacuated, padded, tailed, tap0, conv = (
            [ph.sem(f"f_{n}_{s}") for s in "gv"] for n in (
                "split", "w_high", "up", "evacuated", "padded", "tailed", "tap0", "conv"))
        d_split, d_high, silued, gated, a_high, a_ready, down, added, conv_step, zeroed = (
            ph.sem(f"f_{n}") for n in ("d_split", "d_high", "silued", "gated", "a_high", "a_ready", "down",
                                       "added", "conv_step", "zeroed"))
        turned, copied = ph.sem("f_turned"), ph.sem("f_copied")
        G, V = 0, 1
        LAST = NG * (NF - 1)
        row_slots = [(raw[0:18].rearrange("p s k c -> p (s k c)"), 4)] + [(y[0:18, s], 2) for s in (G, V)] + [
            (xp[0:18, s], 2) for s in (G, V)]
        slot_of = [(b, j) for b, (_, n) in enumerate(row_slots) for j in range(n)][:2 * NF // 4]
        block = ph.block()

        def cycles(body):
            for f in range(NF + 1):
                body(f, f < NF, f >= 1)

        @block.sync
        def _(sp):
            def body(f, now, before):
                if now and before:
                    for s in (G, V):
                        sp.wait_ge(split[s], f)
                        weights.load_up(sp, s, f)
                    sp.wait_ge(d_split, f)
                    weights.load_down(sp, f)
            cycles(body)

            def store_y(t):
                sp.wait_ge(added, LAST + 2 * t + 2)
                to = O["y_prompt"][0, P * t:P * t + P, :] if t < PT else O["y_sample"].rearrange("b t d -> (b t) d")
                sp.dma_start(to, h[:, t, :]).then_inc(C.y_stored, 16)

            def store_rows(b):
                buf = row_slots[b][0]
                ms = [m for m, (at, _) in enumerate(slot_of) if at == b]
                c0, cn = 512 * ms[0], 512 * len(ms)
                sp.wait_ge(copied, ms[-1] + 1)
                sp.dma_start(O["p_ffn_conv"][0, 0][:, c0:c0 + cn], buf[0:2, 0:cn]).then_inc(C.ffn_rows_stored[0], 16)
                sp.dma_start(O["s_ffn_conv"][0].rearrange("b i c -> (b i) c")[:, c0:c0 + cn], buf[2:18, 0:cn]
                             ).then_inc(C.ffn_rows_stored[1], 16)

            for t in range(NT):
                store_y(t)
                if t >= 4:
                    store_rows(t - 4)
            sp.wait_ge(C.y_stored, 16 * NT)
            for kind in range(2):
                sp.wait_ge(C.ffn_rows_stored[kind], 16 * len(row_slots))

        @block.tensor
        def _(pe):
            def project(s, f, before):
                pe.wait_ge(split[s], f + 1)
                if before and s == V:
                    pe.wait_ge(evacuated[V], f)
                if before and s == G and f >= 2:
                    pe.wait_ge(added, NG * (f - 1) - 2)
                for p in range(NP):
                    n = 0
                    for k in range(KD):
                        for wt, x in ((w_hi, hi), (w_hi, lo), (w_lo, hi)):
                            ins = nc.tensor.matmul(banks[:, NP * s + p, 0:TC], wt[:, s, k, :], x[:, k, TC * p:TC * p + TC],
                                                   start=(n == 0), stop=(n == 3 * KD - 1))
                            n += 1
                    ins.then_inc(up[s], 1)

            def turn_rows(m):
                if m >= 3:
                    pe.wait_ge(copied, m - 2)
                for j in range(4):
                    s, i = divmod(4 * m + j, NF)
                    ins = nc.tensor.transpose(banks[0:18, NP + m % 3, P * j:P * j + P], tails[:, s, i, :], C.ident[:])
                ins.then_inc(turned, 1)

            def body(f, now, before):
                if now:
                    project(G, f, before)
                    project(V, f, before)
                else:
                    for s in (G, V):
                        pe.wait_ge(tailed[s], NF)
                    for m in range(3):
                        turn_rows(m)
                if before:
                    pe.wait_ge(evacuated[G], min(f + 1, NF))
                    pe.wait_ge(a_ready, f)
                    pe.wait_ge(d_split, f)
                    for n in range(NG):
                        t, half = divmod(n, 2)
                        bank = banks[:, d_bank[n % 5], :]
                        if n >= 5 or f >= 2:
                            pe.wait_ge(added, NG * (f - 1) + n - 4)
                        tok, col = slice(P * t, P * t + P), slice(512 * half, 512 * half + 512)
                        nc.tensor.matmul(bank, a_hi[:, tok], d_hi[:, col], start=True, stop=False)
                        nc.tensor.matmul(bank, a_hi[:, tok], d_lo[:, col], start=False, stop=False)
                        nc.tensor.matmul(bank, a_lo[:, tok], d_hi[:, col], start=False, stop=True
                                         ).then_inc(down, 1)
                        if not now and n % 2 and n < NG - 1:
                            turn_rows(3 + n // 2)
            cycles(body)

        @block.scalar
        def _(act):
            def weights_high(s, f, before):
                act.wait_ge(w_landed[s], 16 * (f + 1))
                if before:
                    act.wait_ge(up[s], NP * f)
                nc.scalar.activation(w_hi[:, s], raw[:, s], ACT.Copy).then_inc(w_high[s], 1)

            def evacuate(s, f, before):
                if before:
                    act.wait_ge(conv[s], f)
                    act.wait_ge(tailed[s], f)
                for p in range(NP):
                    act.wait_ge(up[s], NP * f + p + 1)
                    cn = TC if p < 2 else PP
                    nc.scalar.activation(xp[:, s, W - 1 + TC * p:W - 1 + TC * p + cn], banks[:, NP * s + p, 0:cn], ACT.Copy)
                nc.scalar.activation(xp_sample(xp[:, s, :], W, W - 1, TB), seqs(banks[:, NP * s + 2, PP:TC]), ACT.Copy
                                     ).then_inc(evacuated[s], 1)

            def first_tap(s, f, before):
                act.wait_ge(evacuated[s], f + 1)
                act.wait_ge(padded[s], f + 1)
                if before:
                    act.wait_ge(gated, f)
                col = V_FC + NF * s + f
                nc.scalar.activation(y[:, s, 0:LY], xp[:, s, 0:LY], ACT.Copy, scale=C.vec[:, col:col + 1]
                                     ).then_inc(tap0[s], 1)

            def body(f, now, before):
                if before:
                    first_tap(V, f - 1, f >= 2)
                if now:
                    if not before:
                        weights_high(G, 0, False)
                    weights_high(V, f, before)
                if before:
                    act.wait_ge(conv[G], f)
                    nc.scalar.activation(y[:, G, 0:LY], y[:, G, 0:LY], ACT.Silu).then_inc(silued, 1)
                    act.wait_ge(d_landed, 16 * f)
                    if f >= 2:
                        act.wait_ge(down, NG * (f - 1))
                    nc.scalar.activation(d_hi[:], d_raw[:], ACT.Copy).then_inc(d_high, 1)
                    act.wait_ge(gated, f)
                    nc.scalar.activation(a_hi[:], a[:], ACT.Copy).then_inc(a_high, 1)
                if now:
                    evacuate(G, f, before)
                    first_tap(G, f, before)
                    if f + 1 < NF:
                        weights_high(G, f + 1, True)
                    evacuate(V, f, before)
            cycles(body)

            for s in (G, V):
                act.wait_ge(split[s], NF)
                act.wait_ge(conv[s], NF)
            for m, (b, j) in enumerate(slot_of):
                act.wait_ge(turned, m + 1)
                nc.scalar.activation(row_slots[b][0][:, 512 * j:512 * j + 512], banks[0:18, NP + m % 3, :], ACT.Copy
                                     ).then_inc(copied, 1)

        @block.gpsimd
        def _(pool):
            nc.gpsimd.memset(xp[:, :, 0:W - 1], 0.0).then_inc(zeroed, 1)
            pool.wait_ge(zeroed, 1)

            def weights_low(s, f, before):
                pool.wait_ge(w_high[s], f + 1)
                nc.gpsimd.tensor_tensor(w_lo[:, s], raw[:, s], w_hi[:, s].bitcast(F32), ALU.subtract).then_inc(split[s], 1)

            def pads(s, f, before):
                if before:
                    pool.wait_ge(conv[s], f)
                nc.gpsimd.tensor_copy(xp_sample(xp[:, s, :], W, 0, W - 1),
                                      old[:, NF * s + f, :].rearrange("p (b i) -> p b i", b=NB)).then_inc(padded[s], 1)

            def tail(s, f):
                pool.wait_ge(evacuated[s], f + 1)
                nc.gpsimd.tensor_copy(tails[:, s, f, 0:2], xp[:, s, TP:TP + 2])
                nc.gpsimd.tensor_copy(tails[:, s, f, 2:18].rearrange("p (b i) -> p b i", b=NB),
                                      xp_sample(xp[:, s, :], W, TB, 2)).then_inc(tailed[s], 1)

            def body(f, now, before):
                if now:
                    if not before:
                        weights_low(G, 0, False)
                    weights_low(V, f, before)
                if before:
                    pool.wait_ge(d_high, f)
                    nc.gpsimd.tensor_tensor(d_lo[:], d_raw[:], d_hi[:].bitcast(F32), ALU.subtract).then_inc(d_split, 1)
                if now:
                    pads(G, f, before)
                    tail(G, f)
                    if f + 1 < NF:
                        weights_low(G, f + 1, True)
                    pads(V, f, before)
                    tail(V, f)
            cycles(body)

        @block.vector
        def _(dve):
            def taps(s, f):
                dve.wait_ge(tap0[s], f + 1)
                for j in (1, 2):
                    col = V_FC + 2 * NF * j + NF * s + f
                    ins = nc.vector.scalar_tensor_tensor(y[:, s, 0:LY], xp[:, s, j:j + LY], C.vec[:, col:col + 1],
                                                         y[:, s, 0:LY], ALU.mult, ALU.add)
                    if j == 1:
                        ins.then_inc(conv_step, 1)
                        dve.wait_ge(conv_step, 2 * f + s + 1)
                ins.then_inc(conv[s], 1)

            def body(f, now, before):
                if before:
                    taps(V, f - 1)
                    dve.wait_ge(conv[V], f)
                    dve.wait_ge(silued, f)
                    if f >= 2:
                        dve.wait_ge(a_ready, f - 1)
                        dve.wait_ge(a_high, f - 1)
                    nc.vector.tensor_tensor(a[:, 0:TP], y[:, G, 0:TP], y[:, V, 0:TP], ALU.mult)
                    nc.vector.tensor_tensor(seqs(a[:, TP:T]), xp_sample(y[:, G, :], W, 0, TB), xp_sample(y[:, V, :], W, 0, TB),
                                            ALU.mult).then_inc(gated, 1)
                    dve.wait_ge(a_high, f)
                    nc.vector.tensor_tensor(a_lo[:], a[:], a_hi[:].bitcast(F32), ALU.subtract).then_inc(a_ready, 1)
                if now:
                    taps(G, f)
                if before:
                    for n in range(NG):
                        t, half = divmod(n, 2)
                        to = h[:, t, 512 * half:512 * half + 512]
                        dve.wait_ge(down, NG * (f - 1) + n + 1)
                        if f >= 2:
                            dve.wait_ge(added, NG * (f - 2) + n + 1)
                        nc.vector.tensor_tensor(to, to, banks[:, d_bank[n % 5], :], ALU.add).then_inc(added, 1)
            cycles(body)



def program(nc, A, O):
    with ExitStack() as stack:
        C = Ctx(nc, stack)
        C.ident, C.ones, C.pair_ones = (C.sb(n, [P, P]) for n in ("ident", "ones", "pair_ones"))
        C.upto, C.after = C.sb("upto", [P, 2, P]), C.sb("after", [P, 2, P])
        C.level, C.hide = C.sb("level", [P, 6, P]), C.sb("hide", [P, 3, 256])
        C.vec, C.k_gain = C.sb("vec", [P, V_ALL]), C.sb("k_gain", [P, 256])
        C.seq_mask = C.sb("seq_mask", [P, NB])
        C.a_log, C.dt_bias, C.sinks, C.eps = (C.sb(n, [P, 4]) for n in ("a_log", "dt_bias", "sinks", "eps"))
        C.state_stored, C.window_stored, C.memory_stored, C.y_stored = (
            C.sem(f"{n}_stored") for n in ("state", "window", "memory", "y"))
        C.conv_stored, C.ffn_rows_stored = ([C.sem(f"{n}_stored{i}") for i in range(2)] for n in ("conv", "ffn_rows"))
        C.spilled, C.spill_landed = [C.sem(f"spilled{i}") for i in range(2)], C.sem("spill_landed")
        x_tiles = [A["x_prompt"][0, P * t:P * t + P, :] for t in range(PT)] + [
            A["x_sample"].rearrange("b t d -> (b t) d")]
        ffn_old = C.sb("ffn_old", [P, 2 * NF, 16])
        columns = [cols for _, _, cols in column_tiles()]
        spill = nc.dram_tensor("spill", (len(SPILL), P, T), F32, kind="Internal").ap()
        mix = ExitStack()
        with ExitStack() as first:
            M = {}
            M["qkv"] = first.enter_context(nc.sbuf_tensor("qkv", [P, 12, T], F32))
            M["gate"] = first.enter_context(nc.sbuf_tensor("gate", [8, T], F32))
            x_rows = M["qkv"][:].rearrange("p a b -> p (a b)")[:, 0:NT * D].rearrange("p (t d) -> p t d", d=D)
            with C.phase() as ph:
                weights = FeatureWeights(ph, "in", A["w_in"][0], columns)
                x_landed = [ph.sem(f"x_landed{t}") for t in range(NT)]

                def load_x(queue, part):
                    for t in range(3) if part == "first" else range(3, NT):
                        queue.dma_start(x_rows[:, t, :], x_tiles[t]).then_inc(x_landed[t], 16)
                    if part == "rest":
                        weights.load_first(queue)

                setup(nc, C, A, ffn_old, load_x)
                xn_hi, xn_lo = (ph.sb(f"x_{n}", [P, KD, T], F32R) for n in ("hi", "lo"))
                norm_turn(nc, C, "nx", x_rows, NT, V_MIX, xn_hi, xn_lo, landed=x_landed, with_masks=True)
                in_projection(nc, C, A, O, M, xn_hi, xn_lo, weights, spill)
            for name, shape in (("swa_q", [P, 2, T]), ("swa_k", [P, 1, T]), ("swa_v", [P, 1, T])):
                M[name] = first.enter_context(nc.sbuf_tensor(name, shape, F32))
            for name in ("g", "beta", "up", "tail", "beta_up"):
                M[name] = first.enter_context(nc.sbuf_tensor(f"gate_{name}", [P, NT, HEADS], F32))
            mix_phase = mix.enter_context(C.phase())
            C.mixT = mix_phase.sb("mixT", [P, KD, T], side="right")

            def load_spilled(sp):
                for to, a, b in ((M["swa_q"][:], 4, 6), (M["swa_k"][:], 6, 7), (M["swa_v"][:], 7, 8),
                                 (C.mixT[:, 0:4, :], 0, 4), (C.mixT[:, 6:8, :], 8, 10)):
                    sp.dma_start(to, spill[a:b].rearrange("s p t -> p s t")).then_inc(C.spill_landed, 16)

            delta_norms(nc, C, M)
            gates(nc, C, M)
            delta_net(nc, C, A, O, M, load_spilled)
            w_o = RowWeights(mix_phase, "wo", (A["w_o"][0],), side="right")
            with C.phase() as ph:
                past = WindowPast(ph, A)
                late_norms(nc, C, M, past.load)
                window_attention(nc, C, A, O, M, past, w_o.load_first)
        h = stack.enter_context(nc.sbuf_tensor("h", [P, NT, D], F32))
        row_projection(nc, C, "wo", C.mixT, NT, w_o, h, residual=x_tiles, loaded=True)
        mix.close()
        attn = ExitStack()
        with ExitStack() as second:
            kT = second.enter_context(nc.sbuf_tensor("mem_k_t", [P, KD, MEM], F32))
            v = second.enter_context(nc.sbuf_tensor("mem_v", [P, 2, D], F32))
            memory_kv(nc, C, A, O, kT, v)
            with C.phase() as ph:
                hn_hi, hn_lo = (ph.sb(f"hn_{n}", [P, KD, T], F32R, side="right") for n in ("hi", "lo"))
                weights = FeatureWeights(ph, "mq", A["w_mq"][0], [[(P * n, P)] for n in range(KD)])
                norm_turn(nc, C, "nh", h, NT, V_MEM, hn_hi, hn_lo, ahead=weights.load_first)
                qT = second.enter_context(nc.sbuf_tensor("mem_q_t", [P, KD, T], F32))
                feature_projection(nc, C, "mq", hn_hi, hn_lo, weights, KD, qT)
            column_norms(nc, C, "qn", [([qT[:, 2 * i, :], qT[:, 2 * i + 1, :]], [qT[:, 2 * i, :], qT[:, 2 * i + 1, :]],
                                        C.ones[:], 1.0 / 256, [C.vec[:, V_MQ + j:V_MQ + j + 1] for j in range(2)])
                                       for i in range(HEADS)], 2)
            attnT = attn.enter_context(nc.sbuf_tensor("mem_attn_t", [P, KD, T], F32, side="right"))
            memory_attention(nc, C, A, qT, kT, v, attnT)
        with C.phase() as ph:
            row_projection(nc, C, "mo", attnT, NT, RowWeights(ph, "mo", (A["w_mo"][0],)), h)
        attn.close()
        hi, lo = (C.sb(f"h_{n}", [P, KD, T], F32R) for n in ("hi", "lo"))
        weights = FfnWeights(C, A)
        norm_turn(nc, C, "nf", h, NT, V_FFN, hi, lo, ahead=weights.load_first)
        ffn(nc, C, A, O, h, hi, lo, ffn_old, weights)


_INS = ["x_prompt", "x_sample", "mem_prompt", "state_gdn", "state_gdn_conv", "cache_swa_k", "cache_swa_v",
        "state_sc_conv", "cache_mem_k", "cache_mem_v", "state_ffn_conv", "norm_mix_g", "w_in", "w_gdn_conv",
        "gdn_a_log", "gdn_dt_bias", "gdn_norm_g", "swa_q_norm_g", "swa_k_norm_g", "swa_sinks", "w_sc_conv", "w_o",
        "norm_mem_g", "mem_in_norm_g", "w_mq", "w_mk", "w_mv", "mem_q_norm_g", "mem_k_norm_g", "w_mo",
        "norm_ffn_g", "w_up", "w_ffn_conv", "w_down"]
_OUTS = [("y_prompt", (1, 1024, 1024)), ("y_sample", (8, 16, 1024)), ("p_gdn", (1, 1, 4, 128, 128)),
         ("p_gdn_conv", (1, 1, 3, 1536)), ("p_swa_k", (1, 1, 128, 2, 64)), ("p_swa_v", (1, 1, 128, 2, 64)),
         ("p_sc_conv", (1, 1, 2, 256)), ("p_mem_k", (1, 1, 256, 4, 256)), ("p_mem_v", (1, 1, 256, 4, 256)),
         ("p_ffn_conv", (1, 1, 2, 5632)), ("s_gdn", (1, 8, 4, 128, 128)), ("s_gdn_conv", (1, 8, 3, 1536)),
         ("s_swa_k", (1, 8, 16, 2, 64)), ("s_swa_v", (1, 8, 16, 2, 64)), ("s_sc_conv", (1, 8, 2, 256)),
         ("s_ffn_conv", (1, 8, 2, 5632))]


def kernel(**inputs):
    import numpy as _np
    import concourse.bacc as _bacc
    from concourse import mybir as _mybir
    from concourse.bass_utils import run_bass_kernel_spmd as _run

    nc = _bacc.Bacc("TRN2", target_bir_lowering=False, num_devices=1)
    arrays, A, O = {}, {}, {}
    for name in _INS:
        a = _np.ascontiguousarray(inputs[name])
        arrays[f"in_{name}"] = a
        A[name] = nc.dram_tensor(f"in_{name}", a.shape, _mybir.dt.from_np(a.dtype), kind="ExternalInput").ap()
    for name, shape in _OUTS:
        O[name] = nc.dram_tensor(f"out_{name}", shape, _mybir.dt.float32, kind="ExternalOutput").ap()
    program(nc, A, O)
    r = _run(nc, [arrays], core_ids=[0])
    return tuple(r.results[0][f"out_{name}"] for name, _ in _OUTS)
```
